# Optimizing a Trainium2 kernel written in Bass

```python
import jax, jax.numpy as jnp
from jax import lax
import numpy as np

D_MODEL = 1024
BATCH = 1
SEQ = 2048
DEPTH = 1

N_META = 16
HEAD_DIM = 64
N_Q_HEADS = 8
N_KV_HEADS = 2
GROUP = N_Q_HEADS // N_KV_HEADS
ATTN_W = N_Q_HEADS * HEAD_DIM
KV_W = N_KV_HEADS * HEAD_DIM
CONV_W = D_MODEL - ATTN_W
IN_W = ATTN_W + 2 * KV_W + 2 * CONV_W
WINDOW = 128
BLOCK = 128
CONV_K = 31
CONV_PAD = CONV_K // 2
N_EXPERTS = 32
TOP_K = 4
D_FF = D_MODEL
SWIGLU_LIMIT = 7.0
SWIGLU_ALPHA = 1.702
RMS_EPS = 1e-6
LN_EPS = 1e-5
NEG_INF = -1e30

kernel_name = 'hymba_conformer_swa_moe_encoder_layer'

def rms_norm(x, g):
    xf = x.astype(jnp.float32)
    y = xf * lax.rsqrt(jnp.mean(xf * xf, axis=-1, keepdims=True) + RMS_EPS)
    return (y * g.astype(jnp.float32)).astype(x.dtype)

def layer_norm(x, g, b):
    xf = x.astype(jnp.float32)
    mu = jnp.mean(xf, axis=-1, keepdims=True)
    var = jnp.mean(jnp.square(xf - mu), axis=-1, keepdims=True)
    y = (xf - mu) * lax.rsqrt(var + LN_EPS)
    return (y * g.astype(jnp.float32) + b.astype(jnp.float32)).astype(x.dtype)

def alibi_slopes():
    return jnp.exp2(-8.0 * (jnp.arange(N_Q_HEADS, dtype=jnp.float32) + 1.0) / N_Q_HEADS)

def windowed_attention(q, k, v, sink):
    B, L = q.shape[0], q.shape[1]
    S = L - N_META
    nb = S // BLOCK
    scale = HEAD_DIM ** -0.5
    q5 = q.reshape(B, L, N_KV_HEADS, GROUP, HEAD_DIM)
    qm, qr = q5[:, :N_META], q5[:, N_META:]
    km, kr = k[:, :N_META], k[:, N_META:]
    vm, vr = v[:, :N_META], v[:, N_META:]
    sink_f = sink.astype(jnp.float32).reshape(N_KV_HEADS, GROUP)

    qb = qr.reshape(B, nb, BLOCK, N_KV_HEADS, GROUP, HEAD_DIM)
    pad = ((0, 0), (BLOCK, BLOCK), (0, 0), (0, 0))
    kb = jnp.pad(kr, pad).reshape(B, nb + 2, BLOCK, N_KV_HEADS, HEAD_DIM)
    vb = jnp.pad(vr, pad).reshape(B, nb + 2, BLOCK, N_KV_HEADS, HEAD_DIM)
    kwin = jnp.concatenate([kb[:, :-2], kb[:, 1:-1], kb[:, 2:]], axis=2)
    vwin = jnp.concatenate([vb[:, :-2], vb[:, 1:-1], vb[:, 2:]], axis=2)
    s_win = jnp.einsum('bnqhgd,bnkhd->bhgnqk', qb, kwin).astype(jnp.float32) * scale
    s_meta = jnp.einsum('bnqhgd,bmhd->bhgnqm', qb, km).astype(jnp.float32) * scale

    qpos = jnp.arange(nb)[:, None] * BLOCK + jnp.arange(BLOCK)[None, :]
    kpos = (jnp.arange(nb)[:, None] - 1) * BLOCK + jnp.arange(3 * BLOCK)[None, :]
    dist = jnp.abs(qpos[:, :, None] - kpos[:, None, :])
    valid = (kpos >= 0)[:, None, :] & (kpos < S)[:, None, :] & (dist <= WINDOW)
    slopes = alibi_slopes().reshape(N_KV_HEADS, GROUP)
    alibi = slopes[:, :, None, None, None] * dist.astype(jnp.float32)[None, None]
    s_win = jnp.where(valid, s_win - alibi, NEG_INF)
    sink_col = jnp.broadcast_to(sink_f[None, :, :, None, None, None], s_win.shape[:-1] + (1,))
    p = jax.nn.softmax(jnp.concatenate([s_meta, s_win, sink_col], axis=-1), axis=-1)
    p_meta = p[..., :N_META].astype(v.dtype)
    p_win = p[..., N_META:N_META + 3 * BLOCK].astype(v.dtype)
    o_real = (jnp.einsum('bhgnqm,bmhd->bnqhgd', p_meta, vm)
              + jnp.einsum('bhgnqk,bnkhd->bnqhgd', p_win, vwin))
    o_real = o_real.reshape(B, S, ATTN_W)

    s_g = jnp.einsum('bmhgd,blhd->bhgml', qm, k).astype(jnp.float32) * scale
    sink_g = jnp.broadcast_to(sink_f[None, :, :, None, None], s_g.shape[:-1] + (1,))
    p_g = jax.nn.softmax(jnp.concatenate([s_g, sink_g], axis=-1), axis=-1)[..., :L].astype(v.dtype)
    o_meta = jnp.einsum('bhgml,blhd->bmhgd', p_g, v).reshape(B, N_META, ATTN_W)
    return jnp.concatenate([o_meta, o_real], axis=1)

def conv_group(u, dw_w, dw_b, ln_g, ln_b):
    a, g = u[..., :CONV_W], u[..., CONV_W:]
    hc = a * jax.nn.sigmoid(g)
    hc = lax.conv_general_dilated(hc, dw_w, window_strides=(1,), padding=[(CONV_PAD, CONV_PAD)],
                                  dimension_numbers=('NWC', 'WIO', 'NWC'),
                                  feature_group_count=CONV_W) + dw_b
    hc = layer_norm(hc, ln_g, ln_b)
    return jax.nn.silu(hc)

def moe(hn, router_w, router_b, w_gate_up, b_gate_up, w_down, b_down):
    B, L, D = hn.shape
    t = hn.reshape(B * L, D)
    n_tok = t.shape[0]
    logits = t.astype(jnp.float32) @ router_w.astype(jnp.float32) + router_b.astype(jnp.float32)
    top_val, top_idx = lax.top_k(logits, TOP_K)
    gates = jax.nn.softmax(top_val, axis=-1)
    flat_e = top_idx.reshape(-1)
    order = jnp.argsort(flat_e)
    tok = order // TOP_K
    e_sorted = flat_e[order]
    group_sizes = jnp.bincount(flat_e, length=N_EXPERTS).astype(jnp.int32)
    xs = t[tok]
    gu = lax.ragged_dot(xs, w_gate_up, group_sizes) + b_gate_up[e_sorted]
    gate = jnp.minimum(gu[:, :D_FF], SWIGLU_LIMIT)
    up = jnp.clip(gu[:, D_FF:], -SWIGLU_LIMIT, SWIGLU_LIMIT)
    act = gate * jax.nn.sigmoid(SWIGLU_ALPHA * gate) * (up + 1.0)
    y = lax.ragged_dot(act, w_down, group_sizes) + b_down[e_sorted]
    y = y * gates.reshape(-1)[order][:, None].astype(y.dtype)
    out = jax.ops.segment_sum(y, tok, num_segments=n_tok)
    return out.reshape(B, L, D)

def setup_inputs(seed: int = 0) -> dict:
    key = jax.random.key(seed)
    ks = jax.random.split(key, 20)
    f = jnp.float32
    nrm = lambda k, s, sc: jax.random.normal(k, s, f) * sc
    return {
        'x': nrm(ks[0], (BATCH, SEQ, D_MODEL), 1.0),
        'meta_tokens': nrm(ks[1], (N_META, D_MODEL), 1.0),
        'norm1_g': 1.0 + nrm(ks[2], (DEPTH, D_MODEL), 0.02),
        'w_in': nrm(ks[3], (DEPTH, D_MODEL, IN_W), D_MODEL ** -0.5),
        'q_norm_g': 1.0 + nrm(ks[4], (DEPTH, HEAD_DIM), 0.02),
        'k_norm_g': 1.0 + nrm(ks[5], (DEPTH, HEAD_DIM), 0.02),
        'attn_sink': nrm(ks[6], (DEPTH, N_Q_HEADS), 0.5),
        'dw_w': nrm(ks[7], (DEPTH, CONV_K, 1, CONV_W), CONV_K ** -0.5),
        'dw_b': nrm(ks[8], (DEPTH, CONV_W), 0.02),
        'conv_ln_g': 1.0 + nrm(ks[9], (DEPTH, CONV_W), 0.02),
        'conv_ln_b': nrm(ks[10], (DEPTH, CONV_W), 0.02),
        'w_out': nrm(ks[11], (DEPTH, D_MODEL, D_MODEL), D_MODEL ** -0.5),
        'norm2_g': 1.0 + nrm(ks[12], (DEPTH, D_MODEL), 0.02),
        'router_w': nrm(ks[13], (DEPTH, D_MODEL, N_EXPERTS), D_MODEL ** -0.5),
        'router_b': nrm(ks[14], (DEPTH, N_EXPERTS), 0.01),
        'w_gate_up': nrm(ks[15], (DEPTH, N_EXPERTS, D_MODEL, 2 * D_FF), D_MODEL ** -0.5),
        'b_gate_up': nrm(ks[16], (DEPTH, N_EXPERTS, 2 * D_FF), 0.02),
        'w_down': nrm(ks[17], (DEPTH, N_EXPERTS, D_FF, D_MODEL), D_FF ** -0.5),
        'b_down': nrm(ks[18], (DEPTH, N_EXPERTS, D_MODEL), 0.02),
    }

def reference(x, meta_tokens, norm1_g, w_in, q_norm_g, k_norm_g, attn_sink, dw_w, dw_b,
              conv_ln_g, conv_ln_b, w_out, norm2_g, router_w, router_b, w_gate_up, b_gate_up,
              w_down, b_down):
    B = x.shape[0]
    meta = jnp.broadcast_to(meta_tokens[None].astype(x.dtype), (B, N_META, D_MODEL))
    h = jnp.concatenate([meta, x], axis=1)
    L = h.shape[1]
    for l in range(DEPTH):
        n = rms_norm(h, norm1_g[l])
        proj = n @ w_in[l]
        q = proj[..., :ATTN_W].reshape(B, L, N_Q_HEADS, HEAD_DIM)
        k = proj[..., ATTN_W:ATTN_W + KV_W].reshape(B, L, N_KV_HEADS, HEAD_DIM)
        v = proj[..., ATTN_W + KV_W:ATTN_W + 2 * KV_W].reshape(B, L, N_KV_HEADS, HEAD_DIM)
        u = proj[..., ATTN_W + 2 * KV_W:]
        q = rms_norm(q, q_norm_g[l])
        k = rms_norm(k, k_norm_g[l])
        attn = windowed_attention(q, k, v, attn_sink[l])
        conv = conv_group(u, dw_w[l], dw_b[l], conv_ln_g[l], conv_ln_b[l])
        h = h + jnp.concatenate([attn, conv], axis=-1) @ w_out[l]
        h = h + moe(rms_norm(h, norm2_g[l]), router_w[l], router_b[l], w_gate_up[l],
                    b_gate_up[l], w_down[l], b_down[l])
    return h[:, N_META:]


_drawn_inputs = setup_inputs


def setup_inputs(seed=0):
    import zlib

    import numpy as np

    out = dict(_drawn_inputs(seed))
    spreads = {}
    factors = {'q_norm_g': 3.853,
     'k_norm_g': 4.099,
     'attn_sink': 137.625,
     'b_gate_up': 5.484,
     'b_down': 6.321}
    for name, (base, spread) in spreads.items():
        noise = np.random.default_rng([zlib.crc32(name.encode()), seed]).standard_normal(out[name].shape)
        drawn = base * np.exp(spread * noise) if base else spread * noise
        out[name] = __import__('jax').numpy.asarray(drawn.astype(out[name].dtype))
    for name, factor in factors.items():
        out[name] = (out[name] * factor).astype(out[name].dtype)
    return out
```

```python
from contextlib import ExitStack

import concourse.bass as bass
from concourse import mybir

F32 = mybir.dt.float32
F32R = mybir.dt.float32r
I32 = mybir.dt.int32
U32 = mybir.dt.uint32
ALU = mybir.AluOpType
ACT = mybir.ActivationFunctionType
AX_X = mybir.AxisListType.X
ds = bass.ds

P = 128
D = 1024
KD = D // P
SEQ = 2048
META = 16
L = META + SEQ
TILES = SEQ // P
HEAD = 64
N_Q = 8
N_KV = 2
GROUP = N_Q // N_KV
ATTN = N_Q * HEAD
KV = N_KV * HEAD
QK = ATTN + KV
CONV = D - ATTN
CC = CONV // P
IN_W = ATTN + 2 * KV + 2 * CONV
TAPS = 31
PAD = 16
BAND = 3 * P
KEYS = META + BAND
EXPERTS = 32
TOP = 4
FF = D
PASS = 384
REGION = -(-SEQ // PASS) * PASS
SLOTS = EXPERTS * REGION
ROWS = SEQ * TOP
PT = PASS // P
WIDTHS = list(range(192, PASS + 1, 32))
MAX_PASSES = (SEQ * TOP + EXPERTS * (PASS - 1)) // PASS
TABLE = 64
RMS_EPS = 1e-6
LN_EPS = 1e-5
NEG = -1e30
LIMIT = 7.0
ALPHA = 1.702
assert MAX_PASSES + 2 <= TABLE and IN_W == 1792


def wait(eng, sem, value):
    if isinstance(value, int) and value <= 0:
        return
    eng.wait_ge(sem, value)


class Chain:

    def __init__(self, eng, sem):
        self.eng, self.sem, self.base, self.n = eng, sem, 0, 0

    def begin(self, base):
        self.base, self.n = base, 0

    def after(self, ins):
        self.n += 1
        ins.then_inc(self.sem, 1)
        self.eng.wait_ge(self.sem, self.base + self.n)


def pipeline(eng, n, stages):
    depth = len(stages)
    lead = depth + depth % 2

    for i in range(lead):
        for s in reversed(range(depth)):
            if i >= s:
                stages[s](i - s, (i - s) % 2, (i - s) // 2)
    with eng.Fori(lead // 2, n // 2) as pair:
        for half in range(2):
            for s in reversed(range(depth)):
                off = half - s
                stages[s](pair * 2 + off, off % 2, pair + off // 2)
    for i in range(n, n + depth - 1):
        for s in reversed(range(depth)):
            if i - s < n:
                stages[s](i - s, (i - s) % 2, (i - s) // 2)


class Kernel:
    pass


def build(nc, a, out, stop=None):
    k = Kernel()
    k.nc, k.a, k.out = nc, a, out
    k.hn = nc.dram_tensor("hn_rows", [SEQ, D], F32, kind="Internal").ap()
    k.h2 = nc.dram_tensor("h2_rows", [SEQ, D], F32, kind="Internal").ap()
    k.slot_list = nc.dram_tensor("slot_list", [SLOTS, 2], I32, kind="Internal").ap()
    k.y = [nc.dram_tensor(f"expert_rows{s}", [ROWS, D // 2], F32, kind="Internal").ap() for s in range(2)]
    k.table = nc.dram_tensor("pass_table", [TABLE, 4], I32, kind="Internal").ap()

    with ExitStack() as whole:
        k.ident = whole.enter_context(nc.sbuf_tensor("ident", [P, P], F32))
        k.eps = whole.enter_context(nc.sbuf_tensor("eps", [P, 2], F32))
        k.gates = whole.enter_context(nc.sbuf_tensor("gates", [P, TILES, TOP], F32))
        k.count = whole.enter_context(nc.sbuf_tensor("count", [P, EXPERTS], F32))
        k.tab = whole.enter_context(nc.sbuf_tensor("tab", [1, TABLE * 4], I32))
        with ExitStack() as front:
            def keep(name, shape, dt=F32):
                return front.enter_context(nc.sbuf_tensor(name, shape, dt))

            k.qT = keep("qT", [P, GROUP, SEQ])
            k.conv = keep("conv", [P, CC, L])
            with ExitStack() as mixer:
                def keep2(name, shape, dt=F32):
                    return mixer.enter_context(nc.sbuf_tensor(name, shape, dt))

                k.kT = keep2("kT", [P, META + P + SEQ + P])
                k.v = keep2("v", [P, TILES + 2, KV])
                k.v_meta = keep2("v_meta", [META, KV])
                project(k)
                if stop == "project":
                    return k
                attend(k)
            if stop == "attend":
                return k
            conv_norm(k)
            if stop == "conv_norm":
                return k
            route(k)
        if stop == "route":
            return k
        plan(k)
        experts(k)
        combine(k)
    return k


def project(k):
    nc, a = k.nc, k.a
    PAIR = 2 * P
    ITERS = 1 + SEQ // PAIR
    with ExitStack() as ctx:
        def sb(name, shape, dt=F32):
            return ctx.enter_context(nc.sbuf_tensor("project_" + name, shape, dt))

        def sem(name):
            return ctx.enter_context(nc.semaphore("project_" + name))

        w_in = sb("w_in", [P, KD, IN_W])
        x_rows = [sb(f"x_rows{s}", [P, D]) for s in range(2)]
        xT = sb("xT", [P, KD, PAIR])
        hc = sb("hc", [P, CC, PAD + L + PAD])
        squares = sb("squares", [P, D])
        qk_rows = sb("qk_rows", [P, QK])
        sig = [sb(f"sig{s}", [P, PAIR]) for s in range(2)]
        ss = [sb(f"ss{s}", [P, 1]) for s in range(2)]
        rstd = [sb(f"rstd{s}", [P, 1]) for s in range(2)]
        root = [sb(f"root{s}", [P, 1]) for s in range(2)]
        ss_head = sb("ss_head", [P, N_Q + N_KV])
        root_head = sb("root_head", [P, N_Q + N_KV])
        rstd_head = sb("rstd_head", [P, N_Q + N_KV])
        g1 = sb("g1", [P, KD])
        qg = sb("qg", [P, 1])
        kg = sb("kg", [P, 1])
        taps = sb("taps", [P, CC, TAPS])
        tap_bias = sb("tap_bias", [P, CC])
        tp = ctx.enter_context(nc.psum_tensor("project_tp", [P, 2, 512], F32))
        q_ps = ctx.enter_context(nc.psum_tensor("project_q_ps", [P, ATTN], F32))
        kv_ps = ctx.enter_context(nc.psum_tensor("project_kv_ps", [P, 512], F32))
        u_ps = ctx.enter_context(nc.psum_tensor("project_u_ps", [P, CC, 2, PAIR], F32))

        w_loaded = sem("w_loaded")
        small_loaded = sem("small_loaded")
        taps_loaded = sem("taps_loaded")
        x_loaded = [sem(f"x_loaded{s}") for s in range(2)]
        eps_ready = sem("eps_ready")
        ident_zeroed = sem("ident_zeroed")
        ident_ready = sem("ident_ready")
        pads_ready = sem("pads_ready")
        ss_ready = sem("ss_ready")
        xn_ready = sem("xn_ready")
        xn_turned = sem("xn_turned")
        xT_ready = sem("xT_ready")
        qkv_ready = sem("qkv_ready")
        head_squares = sem("head_squares")
        v_copied = sem("v_copied")
        qk_ready = sem("qk_ready")
        qk_turned = sem("qk_turned")
        qk_stored = sem("qk_stored")
        u_ready = sem("u_ready")
        sig_ready = sem("sig_ready")
        glu_done = sem("glu_done")
        conv_step = sem("conv_step")
        root_ready = sem("root_ready")
        head_sums = sem("head_sums")
        head_root = sem("head_root")
        vec_chain = sem("vec_chain")

        x = a["x"][0]
        w_view = a["w_in"][0].rearrange("(k p) n -> p k n", p=P)

        def rows(n, s):
            return a["meta_tokens"] if isinstance(n, int) and n == 0 else x[ds((n - 1) * PAIR + s * P, P), :]

        with nc.Block() as block:
            @block.sync
            def _(sp):
                def load(n, s, w):
                    wait(sp, xn_turned, 2 * (n - 1) + s + 1)
                    sp.dma_start(x_rows[s][0:w, :], rows(n, s)).then_inc(x_loaded[s], 16)

                for s in range(2):
                    load(0, s, META)
                for kk in range(KD):
                    sp.dma_start(w_in[:, kk, :], w_view[:, kk, :]).then_inc(w_loaded, 16)
                with sp.Fori(1, ITERS) as n:
                    for s in range(2):
                        load(n, s, P)

            @block.gpsimd
            def _(pool):
                pool.memset(k.eps[:, 0:1], RMS_EPS).then_inc(eps_ready, 1)
                pool.memset(k.eps[:, 1:2], LN_EPS).then_inc(eps_ready, 1)
                pool.memset(k.ident[:, :], 0.0).then_inc(ident_zeroed, 1)
                pool.wait_ge(ident_zeroed, 1)
                pool.affine_select(out=k.ident[:, :], in_=k.ident[:, :], compare_op=ALU.not_equal,
                                   fill=1.0, base=0, pattern=[[-1, P]], channel_multiplier=1) \
                    .then_inc(ident_ready, 1)
                pool.memset(hc[:, :, 0:PAD], 0.0).then_inc(pads_ready, 1)
                pool.memset(hc[:, :, PAD + L:], 0.0).then_inc(pads_ready, 1)
                pool.memset(k.kT[:, :], 0.0).then_inc(pads_ready, 1)
                pool.memset(k.v[:, :, :], 0.0).then_inc(pads_ready, 1)

            @block.scalar
            def _(act):
                act.dma_start(g1[:, :], a["norm1_g"]).then_inc(small_loaded, 16)
                for g in range(N_KV):
                    half = slice(g * HEAD, (g + 1) * HEAD)
                    act.dma_start(qg[half, :], a["q_norm_g"]) \
                       .then_inc(small_loaded, 16)
                    act.dma_start(kg[half, :], a["k_norm_g"]) \
                       .then_inc(small_loaded, 16)
                act.dma_start(taps[:, :, :], a["dw_w"].rearrange("(c p) t -> p c t", p=P)).then_inc(taps_loaded, 16)
                act.dma_start(tap_bias[:, :], a["dw_b"]).then_inc(taps_loaded, 16)

                act.wait_ge(eps_ready, 2)

                def iteration(n, w, pos):
                    cols = META if w == META else PAIR
                    for s in range(2):
                        act.wait_ge(x_loaded[s], 16 * (n + 1))
                        wait(act, qk_ready, 2 * (n - 1) + 2)
                        wait(act, ss_ready, 2 * n + s)
                        nc.scalar.activation(squares[0:w, :], x_rows[s][0:w, :], ACT.Square,
                                             accum_out=ss[s][0:w, :]).then_inc(ss_ready, 1)
                    for s in range(2):
                        act.wait_ge(ss_ready, 2 * n + s + 1)
                        nc.scalar.activation(root[s][0:w, :], ss[s][0:w, :], ACT.Sqrt, scale=1.0 / D,
                                             bias=k.eps[0:w, 0:1]).then_inc(root_ready, 1)

                    def head_roots(s):
                        act.wait_ge(head_sums, 2 * n + s + 1)
                        nc.scalar.activation(root_head[0:w, :], ss_head[0:w, :], ACT.Sqrt, scale=1.0 / HEAD,
                                             bias=k.eps[0:w, 0:1]).then_inc(head_root, 1)

                    def heads(s):
                        act.wait_ge(qkv_ready, 2 * n + s + 1)
                        act.wait_ge(ss_ready, 2 * n + 2)
                        wait(act, qk_ready, 2 * n + s)
                        nc.scalar.activation(squares[0:w, 0:ATTN], q_ps[0:w, :], ACT.Square).then_inc(head_squares, 1)
                        nc.scalar.activation(squares[0:w, ATTN:QK], kv_ps[0:w, 0:KV], ACT.Square) \
                          .then_inc(head_squares, 1)
                        if w == META:
                            wait(act, v_copied, s)
                            v_to = k.v_meta[:, :]
                        else:
                            act.wait_ge(pads_ready, 4)
                            v_to = k.v[:, ds((n - 1) * 2 + (s + 1), 1), :].rearrange("p one c -> p (one c)")
                        nc.scalar.activation(v_to, kv_ps[0:w, KV:2 * KV], ACT.Copy).then_inc(v_copied, 1)

                    def gate(c):
                        act.wait_ge(u_ready, CC * n + c + 1)
                        wait(act, glu_done, CC * n + c - 1)
                        nc.scalar.activation(sig[c % 2][:, 0:cols], u_ps[:, c, 1, 0:cols], ACT.Sigmoid) \
                          .then_inc(sig_ready, 1)

                    heads(0)
                    head_roots(0)
                    gate(0)
                    gate(1)
                    heads(1)
                    head_roots(1)
                    gate(2)
                    gate(3)

                iteration(0, META, 0)
                with act.Fori(1, ITERS) as n:
                    iteration(n, P, None)

            @block.tensor
            def _(pe):
                pe.wait_ge(ident_ready, 1)

                def iteration(n, w):
                    cols = META if w == META else PAIR
                    for s in range(2):
                        pe.wait_ge(xn_ready, 2 * n + s + 1)
                        wait(pe, xT_ready, 2 * n + s)
                        wait(pe, qk_stored, 2 * n)
                        for kk in range(KD):
                            mm = nc.tensor.transpose(tp[:, kk // 4, (kk % 4) * P:(kk % 4) * P + w],
                                                     x_rows[s][0:w, kk * P:(kk + 1) * P], k.ident[0:w, 0:w])
                        mm.then_inc(xn_turned, 1)

                    def qkv(s):
                        pe.wait_ge(xT_ready, 2 * n + s + 1)
                        wait(pe, qk_ready, 2 * n + s)
                        wait(pe, v_copied, 2 * n + s)
                        for kk in range(KD):
                            nc.tensor.matmul(q_ps[0:w, :], xT[:, kk, s * w:(s + 1) * w], w_in[:, kk, 0:ATTN],
                                             start=kk == 0, stop=kk == KD - 1)
                        for kk in range(KD):
                            mm = nc.tensor.matmul(kv_ps[0:w, 0:2 * KV], xT[:, kk, s * w:(s + 1) * w],
                                                  w_in[:, kk, ATTN:ATTN + 2 * KV], start=kk == 0, stop=kk == KD - 1)
                        mm.then_inc(qkv_ready, 1)

                    def u(c):
                        pe.wait_ge(xT_ready, 2 * n + 2)
                        wait(pe, glu_done, CC * (n - 1) + c + 1)
                        for half in range(2):
                            first = ATTN + 2 * KV + half * CONV + c * P
                            for kk in range(KD):
                                mm = nc.tensor.matmul(u_ps[:, c, half, 0:cols], w_in[:, kk, first:first + P],
                                                      xT[:, kk, 0:cols], start=kk == 0, stop=kk == KD - 1)
                        mm.then_inc(u_ready, 1)

                    def turn_qk(s):
                        pe.wait_ge(qk_ready, 2 * n + s + 1)
                        pe.wait_ge(xT_ready, 2 * n + 2)
                        wait(pe, qk_stored, 2 * n + s)
                        for i in range(GROUP):
                            nc.tensor.transpose(tp[:, 0, i * P:i * P + w], qk_rows[0:w, i * P:(i + 1) * P],
                                                k.ident[0:w, 0:w])
                        nc.tensor.transpose(tp[:, 1, 0:w], qk_rows[0:w, ATTN:QK], k.ident[0:w, 0:w]) \
                          .then_inc(qk_turned, 1)

                    if w == META:
                        pe.wait_ge(w_loaded, 16 * KD)
                    qkv(0)
                    u(0)
                    turn_qk(0)
                    u(1)
                    qkv(1)
                    u(2)
                    turn_qk(1)
                    u(3)

                iteration(0, META)
                with pe.Fori(1, ITERS) as n:
                    iteration(n, P)

            @block.vector
            def _(dve):
                chain = Chain(dve, vec_chain)
                dve.wait_ge(small_loaded, 16 * 5)
                dve.wait_ge(taps_loaded, 32)
                dve.wait_ge(pads_ready, 4)

                def convolve(conv_base, first, width):
                    for c in range(CC):
                        nc.vector.tensor_scalar(k.conv[:, c, ds(first, width)], hc[:, c, ds(first + 1, width)],
                                                taps[:, c, 0:1], tap_bias[:, c:c + 1], ALU.mult, ALU.add) \
                          .then_inc(conv_step, 1)
                    for t in range(1, TAPS):
                        for c in range(CC):
                            dve.wait_ge(conv_step, conv_base + CC * (t - 1) + c + 1)
                            nc.vector.scalar_tensor_tensor(
                                out=k.conv[:, c, ds(first, width)], in0=hc[:, c, ds(first + 1 + t, width)],
                                scalar=taps[:, c, t:t + 1], in1=k.conv[:, c, ds(first, width)],
                                op0=ALU.mult, op1=ALU.add).then_inc(conv_step, 1)

                def iteration(n, w, pos):
                    cols = META if w == META else PAIR
                    chain.begin(4 * n)
                    for s in range(2):
                        dve.wait_ge(root_ready, 2 * n + s + 1)
                        chain.after(nc.vector.reciprocal(rstd[s][0:w, :], root[s][0:w, :]))
                        nc.vector.tensor_scalar(x_rows[s][0:w, :], x_rows[s][0:w, :], rstd[s][0:w, 0:1], None,
                                                ALU.mult).then_inc(xn_ready, 1)
                    for s in range(2):
                        dve.wait_ge(xn_turned, 2 * n + s + 1)
                        wait(dve, u_ready, CC * n)
                        wait(dve, qkv_ready, 2 * n)
                        for half in range(2):
                            ins = nc.vector.tensor_tensor(
                                xT[:, half * 4:half * 4 + 4, s * w:(s + 1) * w],
                                tp[:, half, :].rearrange("p (k t) -> p k t", t=P)[:, :, 0:w],
                                g1[:, half * 4:half * 4 + 4].unsqueeze(2).to_broadcast([P, 4, w]), ALU.mult)
                        ins.then_inc(xT_ready, 1)

                    def norm_heads(s):
                        dve.wait_ge(head_squares, 2 * (2 * n + s + 1))
                        nc.vector.tensor_reduce(
                            ss_head[0:w, :], squares[0:w, 0:QK].rearrange("p (h d) -> p h d", d=HEAD), AX_X,
                            ALU.add).then_inc(head_sums, 1)
                        dve.wait_ge(head_root, 2 * n + s + 1)
                        chain.after(nc.vector.reciprocal(rstd_head[0:w, :], root_head[0:w, :]))
                        wait(dve, qk_turned, 2 * n + s)
                        nc.vector.tensor_tensor(
                            qk_rows[0:w, 0:ATTN].rearrange("p (i g d) -> p g i d", g=N_KV, d=HEAD),
                            q_ps[0:w, :].rearrange("p (g i d) -> p g i d", g=N_KV, d=HEAD),
                            rstd_head[0:w, 0:N_Q].rearrange("p (g i) -> p g i", g=N_KV).unsqueeze(3)
                            .to_broadcast([w, N_KV, GROUP, HEAD]), ALU.mult)
                        nc.vector.tensor_tensor(
                            qk_rows[0:w, ATTN:QK].rearrange("p (g d) -> p g d", d=HEAD),
                            kv_ps[0:w, 0:KV].rearrange("p (g d) -> p g d", d=HEAD),
                            rstd_head[0:w, N_Q:].unsqueeze(2).to_broadcast([w, N_KV, HEAD]), ALU.mult) \
                          .then_inc(qk_ready, 1)

                    def store_qk(s):
                        dve.wait_ge(qk_turned, 2 * n + s + 1)
                        if isinstance(n, int):
                            q_at, k_at = ds(0, w), ds(0, w)
                        else:
                            q_at, k_at = ds((n - 1) * PAIR + s * P, w), ds((n - 1) * PAIR + s * P + META + P, w)
                        wait(dve, qk_stored, s + 2 * n)
                        nc.vector.tensor_scalar(k.qT[:, :, q_at],
                                                tp[:, 0, :].rearrange("p (i t) -> p i t", t=P)[:, :, 0:w],
                                                qg[:, 0:1], None, ALU.mult)
                        nc.vector.tensor_scalar(k.kT[:, k_at], tp[:, 1, 0:w], kg[:, 0:1], None, ALU.mult) \
                          .then_inc(qk_stored, 1)

                    def glu(c):
                        dve.wait_ge(sig_ready, CC * n + c + 1)
                        at = ds(PAD, cols) if isinstance(n, int) else ds((n - 1) * PAIR + PAD + META, cols)
                        nc.vector.tensor_tensor(hc[:, c, at], u_ps[:, c, 0, 0:cols], sig[c % 2][:, 0:cols],
                                                ALU.mult).then_inc(glu_done, 1)

                    norm_heads(0)
                    glu(0)
                    store_qk(0)
                    glu(1)
                    norm_heads(1)
                    glu(2)
                    store_qk(1)
                    glu(3)

                iteration(0, META, 0)
                with dve.Fori(1, ITERS) as n:
                    iteration(n, P, None)
                    dve.wait_ge(glu_done, CC * n + CC)
                    convolve((n - 1) * CC * TAPS, (n - 1) * PAIR, PAIR)
                convolve((ITERS - 1) * CC * TAPS, SEQ, META)


def attend(k):
    nc, a = k.nc, k.a
    with ExitStack() as ctx:
        def sb(name, shape, dt=F32):
            return ctx.enter_context(nc.sbuf_tensor("attend_" + name, shape, dt))

        def sem(name):
            return ctx.enter_context(nc.semaphore("attend_" + name))

        empty = sb("empty", [P, SLOTS // P, 2], I32)
        dist_i = sb("dist_i", [P, KEYS], I32)
        dist = sb("dist", [P, KEYS])
        far = sb("far", [P, KEYS])
        bias = sb("bias", [P, N_Q, KEYS])
        sink = sb("sink", [P, N_Q])
        scores = [sb(f"scores{s}", [P, GROUP, KEYS]) for s in range(2)]
        probs = [sb(f"probs{s}", [P, GROUP, KEYS]) for s in range(2)]
        top = [sb(f"top{s}", [P, GROUP]) for s in range(2)]
        neg_top = [sb(f"neg_top{s}", [P, GROUP]) for s in range(2)]
        sink_gap = [sb(f"sink_gap{s}", [P, GROUP]) for s in range(2)]
        sink_exp = [sb(f"sink_exp{s}", [P, GROUP]) for s in range(2)]
        total = [sb(f"total{s}", [P, GROUP]) for s in range(2)]
        inverse = [sb(f"inverse{s}", [P, GROUP]) for s in range(2)]
        pT = [sb(f"pT{s}", [P, 512]) for s in range(2)]
        o_rows = sb("o_rows", [P, ATTN])
        q_block = sb("q_block", [P, GROUP, P])
        k_band = sb("k_band", [P, BAND])
        s_ps = ctx.enter_context(nc.psum_tensor("attend_s_ps", [P, GROUP, 512], F32))
        pt_ps = ctx.enter_context(nc.psum_tensor("attend_pt_ps", [P, 2, 512], F32))
        o_ps = ctx.enter_context(nc.psum_tensor("attend_o_ps", [P, ATTN], F32))
        ot_ps = ctx.enter_context(nc.psum_tensor("attend_ot_ps", [P, ATTN], F32))

        empty_made = sem("empty_made")
        empty_stored = sem("empty_stored")
        dist_made = sem("dist_made")
        sink_loaded = sem("sink_loaded")
        q_staged = sem("q_staged")
        scores_ready = sem("scores_ready")
        scores_taken = sem("scores_taken")
        top_ready = sem("top_ready")
        exp_done = sem("exp_done")
        probs_ready = sem("probs_ready")
        probs_turned = sem("probs_turned")
        pT_ready = [sem("pT_even_ready"), sem("pT_odd_ready")]
        pT_used = sem("pT_used")
        o_ready = sem("o_ready")
        o_normed = sem("o_normed")
        o_turned = sem("o_turned")
        o_stored = sem("o_stored")
        bias_chain = sem("bias_chain")
        vec_chain = sem("vec_chain")

        BLOCKS = TILES
        with nc.Block() as block:
            @block.sync
            def _(sp):
                sp.wait_ge(empty_made, 2)
                sp.dma_start(k.slot_list.rearrange("(p n) two -> p (n two)", p=P),
                             empty[:, :, :].rearrange("p n two -> p (n two)")).then_inc(empty_stored, 16)
                sp.wait_ge(empty_stored, 16)

            @block.gpsimd
            def _(pool):
                pool.memset(empty[:, :, 0:1], 0).then_inc(empty_made, 1)
                pool.memset(empty[:, :, 1:2], ROWS).then_inc(empty_made, 1)
                pool.memset(dist_i[:, 0:META], 0).then_inc(dist_made, 1)
                pool.iota(dist_i[:, META:], pattern=[[1, BAND]], base=-P, channel_multiplier=-1) \
                    .then_inc(dist_made, 1)

                def stage(b):
                    wait(pool, scores_ready, 2 * b)
                    pool.tensor_copy(q_block[:, :, :], k.qT[:, :, ds(b * P, P)]).then_inc(q_staged, 1)
                    pool.tensor_copy(k_band[:, :], k.kT[:, ds(b * P + META, BAND)]).then_inc(q_staged, 1)

                stage(0)
                with pool.Fori(1, BLOCKS) as b:
                    stage(b)

            @block.tensor
            def _(pe):
                def score(b, g, u):
                    half = slice(g * HEAD, (g + 1) * HEAD)
                    pe.wait_ge(q_staged, 2 * b + 2)
                    wait(pe, scores_taken, u)
                    for i in range(GROUP):
                        q = q_block[half, i, :]
                        nc.tensor.matmul(s_ps[:, i, 0:META], q, k.kT[half, 0:META], start=True, stop=True)
                        mm = nc.tensor.matmul(s_ps[:, i, META:KEYS], q, k_band[half, :],
                                              start=True, stop=True)
                    mm.then_inc(scores_ready, 1)

                def weigh(b, g, u):
                    cols = slice(g * HEAD, (g + 1) * HEAD)

                    def turn(i):
                        h = u * GROUP + i
                        pe.wait_ge(probs_ready, h + 1)
                        wait(pe, pT_ready[i % 2], 2 * u + i // 2)
                        for j in range(3):
                            nc.tensor.transpose(pt_ps[:, i % 2, j * P:(j + 1) * P],
                                                probs[g][:, i, META + j * P:META + (j + 1) * P], k.ident[:, :])
                        nc.tensor.transpose(pt_ps[0:META, i % 2, BAND:512], probs[g][:, i, 0:META], k.ident[:, :]) \
                          .then_inc(probs_turned, 1)

                    def value(i):
                        h = u * GROUP + i
                        pe.wait_ge(pT_ready[i % 2], 2 * u + (i // 2 + 1))
                        if i == 0:
                            wait(pe, o_normed, u)
                        o = o_ps[:, i * P + g * HEAD:i * P + (g + 1) * HEAD]
                        for j in range(3):
                            nc.tensor.matmul(o, pT[i % 2][:, j * P:(j + 1) * P], k.v[:, ds(b + j, 1), cols],
                                             start=j == 0, stop=False)
                        nc.tensor.matmul(o, pT[i % 2][0:META, BAND:512], k.v_meta[:, cols],
                                         start=False, stop=True).then_inc(pT_used, 1)

                    turn(0)
                    for i in range(GROUP):
                        if i + 1 < GROUP:
                            turn(i + 1)
                        value(i)

                def turn_out(b):
                    pe.wait_ge(o_normed, 2 * b + 2)
                    pe.wait_ge(o_stored, b + 1)
                    for i in range(GROUP):
                        mm = nc.tensor.transpose(ot_ps[:, i * P:(i + 1) * P], o_rows[:, i * P:(i + 1) * P],
                                                 k.ident[:, :])
                    mm.then_inc(o_turned, 1)

                score(0, 0, 0)
                score(0, 1, 1)
                weigh(0, 0, 0)
                with pe.Fori(1, BLOCKS) as b:
                    score(b, 0, 2 * b)
                    weigh(b - 1, 1, 2 * b - 1)
                    score(b, 1, 2 * b + 1)
                    weigh(b, 0, 2 * b)
                    turn_out(b - 1)
                weigh(BLOCKS - 1, 1, 2 * BLOCKS - 1)
                turn_out(BLOCKS - 1)

            @block.scalar
            def _(act):
                act.dma_start(sink[:, :], a["attn_sink"][0:1, :].to_broadcast([P, N_Q])).then_inc(sink_loaded, 16)

                def exps(g, u):
                    act.wait_ge(top_ready, 2 * u + 2)
                    wait(act, probs_turned, GROUP * (u - 1))
                    for i in range(GROUP):
                        nc.scalar.activation(probs[g][:, i, :], scores[g][:, i, :], ACT.Exp,
                                             bias=neg_top[g][:, i:i + 1],
                                             accum_out=total[g][:, i:i + 1]).then_inc(probs_ready, 1)
                    nc.scalar.activation(sink_exp[g][:, :], sink_gap[g][:, :], ACT.Exp).then_inc(exp_done, 1)

                def copies(u):
                    for i in range(0, GROUP, 2):
                        h = u * GROUP + i
                        act.wait_ge(probs_turned, h + 1)
                        wait(act, pT_used, h - 1)
                        nc.scalar.activation(pT[0][:, 0:BAND], pt_ps[:, 0, 0:BAND], ACT.Copy)
                        nc.scalar.activation(pT[0][0:META, BAND:512], pt_ps[0:META, 0, BAND:512], ACT.Copy) \
                          .then_inc(pT_ready[0], 1)

                def store(b):
                    act.wait_ge(o_turned, b + 1)
                    nc.scalar.activation(k.qT[:, :, ds(b * P, P)], ot_ps[:, :].rearrange("p (i t) -> p i t", t=P),
                                         ACT.Copy).then_inc(o_stored, 1)

                act.sem_inc(o_stored, 1)
                exps(0, 0)
                exps(1, 1)
                copies(0)
                with act.Fori(1, BLOCKS) as b:
                    exps(0, 2 * b)
                    copies(2 * b - 1)
                    exps(1, 2 * b + 1)
                    copies(2 * b)
                    store(b - 1)
                copies(2 * BLOCKS - 1)
                store(BLOCKS - 1)

            @block.vector
            def _(dve):
                chain = Chain(dve, vec_chain)
                setup = Chain(dve, bias_chain)
                dve.wait_ge(dist_made, 2)
                dve.wait_ge(sink_loaded, 16)
                setup.after(nc.vector.tensor_copy(dist[:, :], dist_i[:, :]))
                setup.after(nc.vector.tensor_scalar(far[:, :], dist[:, :], -1.0, None, ALU.mult))
                setup.after(nc.vector.tensor_tensor(dist[:, :], dist[:, :], far[:, :], ALU.max))
                setup.after(nc.vector.tensor_scalar(far[:, :], dist[:, :], float(P), NEG, ALU.is_gt, ALU.mult))
                for h in range(N_Q):
                    slope = 2.0 ** (-8.0 * (h + 1) / N_Q)
                    ins = nc.vector.scalar_tensor_tensor(out=bias[:, h, :], in0=dist[:, :], scalar=-slope,
                                                         in1=far[:, :], op0=ALU.mult, op1=ALU.add)
                setup.after(ins)

                def soft(g, u, edge=None):
                    heads = slice(g * GROUP, (g + 1) * GROUP)
                    dve.wait_ge(scores_ready, u + 1)
                    wait(dve, exp_done, u - 1)
                    nc.vector.scalar_tensor_tensor(
                        out=scores[g][:, :, :], in0=s_ps[:, :, 0:KEYS], scalar=HEAD ** -0.5,
                        in1=bias[:, heads, :], op0=ALU.mult, op1=ALU.add).then_inc(scores_taken, 1)
                    dve.wait_ge(scores_taken, u + 1)
                    if edge is not None:
                        cut = META if edge == 0 else META + 2 * P
                        setup.after(nc.vector.memset(scores[g][:, :, cut:cut + P], NEG))
                    chain.after(nc.vector.tensor_reduce(top[g][:, :], scores[g][:, :, :], AX_X, ALU.max))
                    chain.after(nc.vector.tensor_tensor(top[g][:, :], top[g][:, :], sink[:, heads], ALU.max))
                    nc.vector.tensor_scalar(neg_top[g][:, :], top[g][:, :], -1.0, None, ALU.mult) \
                      .then_inc(top_ready, 1)
                    nc.vector.tensor_tensor(sink_gap[g][:, :], sink[:, heads], top[g][:, :],
                                            ALU.subtract).then_inc(top_ready, 1)

                def finish(b, g, u):
                    dve.wait_ge(exp_done, u + 1)
                    chain.after(nc.vector.tensor_tensor(total[g][:, :], total[g][:, :], sink_exp[g][:, :], ALU.add))
                    chain.after(nc.vector.reciprocal(inverse[g][:, :], total[g][:, :]))
                    for i in range(1, GROUP, 2):
                        h = u * GROUP + i
                        dve.wait_ge(probs_turned, h + 1)
                        wait(dve, pT_used, h - 1)
                        nc.vector.tensor_copy(pT[1][:, 0:BAND], pt_ps[:, 1, 0:BAND])
                        nc.vector.tensor_copy(pT[1][0:META, BAND:512], pt_ps[0:META, 1, BAND:512]) \
                          .then_inc(pT_ready[1], 1)
                    dve.wait_ge(pT_used, GROUP * (u + 1))
                    if g == 0:
                        wait(dve, o_turned, b)
                    nc.vector.tensor_tensor(
                        o_rows[:, :].rearrange("p (i g d) -> p g i d", g=N_KV, d=HEAD)[:, g, :, :],
                        o_ps[:, :].rearrange("p (i g d) -> p g i d", g=N_KV, d=HEAD)[:, g, :, :],
                        inverse[g][:, :].unsqueeze(2).to_broadcast([P, GROUP, HEAD]), ALU.mult) \
                      .then_inc(o_normed, 1)

                def around(b, edge=None):
                    soft(0, 2 * b, edge)
                    finish(b - 1, 1, 2 * b - 1)
                    soft(1, 2 * b + 1, edge)
                    finish(b, 0, 2 * b)

                soft(0, 0, edge=0)
                soft(1, 1, edge=0)
                finish(0, 0, 0)
                FIRST, CHAIN = 6, 8
                assert chain.n == FIRST
                with dve.Fori(1, BLOCKS - 1) as b:
                    chain.begin((b - 1) * CHAIN + FIRST)
                    around(b)
                    assert chain.n == CHAIN
                chain.begin((BLOCKS - 2) * CHAIN + FIRST)
                around(BLOCKS - 1, edge=1)
                finish(BLOCKS - 1, 1, 2 * BLOCKS - 1)


def conv_norm(k):
    nc, a = k.nc, k.a
    SPAN = 512
    with ExitStack() as ctx:
        def sb(name, shape, dt=F32):
            return ctx.enter_context(nc.sbuf_tensor("conv_norm_" + name, shape, dt))

        def sem(name):
            return ctx.enter_context(nc.semaphore("conv_norm_" + name))

        ones = sb("ones", [P, P])
        gain = sb("gain", [P, CC])
        shift = sb("shift", [P, CC])
        side = [sb(f"side{s}", [P, CC, SPAN]) for s in range(2)]
        inv = [sb(f"inv{s}", [P, SPAN]) for s in range(2)]
        root = [sb(f"root{s}", [P, SPAN]) for s in range(2)]
        mean_ps = ctx.enter_context(nc.psum_tensor("conv_norm_mean_ps", [P, 2, SPAN], F32))
        var_ps = ctx.enter_context(nc.psum_tensor("conv_norm_var_ps", [P, 2, SPAN], F32))
        ones_ready = sem("ones_ready")
        small_loaded = sem("small_loaded")
        mean_ready = sem("mean_ready")
        centred = sem("centred")
        squared = sem("squared")
        var_ready = sem("var_ready")
        scaled = sem("scaled")
        sigmoid_ready = sem("sigmoid_ready")
        swished = sem("swished")
        root_ready = sem("root_ready")
        vec_chain = sem("vec_chain")

        def z(i, c=None):
            at = ds(META + i * SPAN, SPAN)
            return k.conv[:, :, at] if c is None else k.conv[:, c, at]

        spans = SEQ // SPAN
        with nc.Block() as block:
            @block.gpsimd
            def _(pool):
                pool.memset(ones[:, :], 1.0 / CONV).then_inc(ones_ready, 1)

            @block.tensor
            def _(pe):
                pe.wait_ge(ones_ready, 1)

                def mean(i, par, m):
                    for c in range(CC):
                        mm = nc.tensor.matmul(mean_ps[:, par, :], ones[:, :], z(i, c), start=c == 0, stop=c == CC - 1)
                    mm.then_inc(mean_ready, 1)

                def variance(i, par, m):
                    pe.wait_ge(squared, i + 1)
                    for c in range(CC):
                        mm = nc.tensor.matmul(var_ps[:, par, :], ones[:, :], side[par][:, c, :],
                                              start=c == 0, stop=c == CC - 1)
                    mm.then_inc(var_ready, 1)

                for i in range(spans):
                    if i < 2:
                        mean(i, i % 2, i // 2)
                for i in range(spans):
                    variance(i, i % 2, i // 2)
                    if i + 2 < spans:
                        pe.wait_ge(centred, i + 1)
                        mean(i + 2, i % 2, i // 2)

            @block.scalar
            def _(act):
                act.dma_start(gain[:, :], a["conv_ln_g"]).then_inc(small_loaded, 16)
                act.dma_start(shift[:, :], a["conv_ln_b"]).then_inc(small_loaded, 16)
                act.wait_ge(small_loaded, 32)

                def square(i):
                    act.wait_ge(centred, i + 1)
                    wait(act, swished, i - 1)
                    nc.scalar.activation(side[i % 2][:, :, :], z(i), ACT.Square).then_inc(squared, 1)

                def sigmoid(i):
                    act.wait_ge(scaled, i + 1)
                    for c in range(CC):
                        nc.scalar.activation(side[i % 2][:, c, :], z(i, c), ACT.Sigmoid, scale=gain[:, c:c + 1],
                                             bias=shift[:, c:c + 1]).then_inc(sigmoid_ready, 1)

                def deviation(i):
                    act.wait_ge(var_ready, i + 1)
                    wait(act, scaled, i - 1)
                    nc.scalar.activation(root[i % 2][:, :], var_ps[:, i % 2, :], ACT.Sqrt, bias=k.eps[:, 1:2]) \
                      .then_inc(root_ready, 1)

                square(0)
                for i in range(spans):
                    if i + 1 < spans:
                        square(i + 1)
                    deviation(i)
                    sigmoid(i)

            @block.vector
            def _(dve):
                chain = Chain(dve, vec_chain)
                dve.wait_ge(small_loaded, 32)

                def centre(i):
                    dve.wait_ge(mean_ready, i + 1)
                    nc.vector.tensor_tensor(z(i), z(i), mean_ps[:, i % 2, :].unsqueeze(1).to_broadcast([P, CC, SPAN]),
                                            ALU.subtract).then_inc(centred, 1)

                def scale(i):
                    dve.wait_ge(root_ready, i + 1)
                    chain.after(nc.vector.reciprocal(inv[i % 2][:, :], root[i % 2][:, :]))
                    nc.vector.tensor_tensor(z(i), z(i), inv[i % 2][:, :].unsqueeze(1).to_broadcast([P, CC, SPAN]),
                                            ALU.mult).then_inc(scaled, 1)

                def swish(i):
                    dve.wait_ge(sigmoid_ready, CC * (i + 1))
                    for c in range(CC):
                        ins = nc.vector.tensor_scalar(z(i, c), z(i, c), gain[:, c:c + 1], shift[:, c:c + 1],
                                                      ALU.mult, ALU.add)
                    chain.after(ins)
                    nc.vector.tensor_tensor(z(i), z(i), side[i % 2][:, :, :], ALU.mult).then_inc(swished, 1)

                centre(0)
                for i in range(spans):
                    if i + 1 < spans:
                        centre(i + 1)
                    scale(i)
                    swish(i)


def route(k):
    nc, a = k.nc, k.a
    with ExitStack() as ctx:
        def sb(name, shape, dt=F32):
            return ctx.enter_context(nc.sbuf_tensor("route_" + name, shape, dt))

        def two(name, shape, dt=F32):
            return [sb(f"{name}{s}", shape, dt) for s in range(2)]

        def sem(name):
            return ctx.enter_context(nc.semaphore("route_" + name))

        def sem2(name):
            return [sem(f"{name}{s}") for s in range(2)]

        w_out = sb("w_out", [P, KD, D])
        g2 = sb("g2", [P, D])
        rw = sb("rw", [P, KD, EXPERTS])
        rb = sb("rb", [P, EXPERTS])
        b_down = sb("b_down", [EXPERTS, D])
        before = sb("before", [P, P])
        ones = sb("ones", [P, P])
        col_i = sb("col_i", [P, EXPERTS], I32)
        col = sb("col", [P, EXPERTS])
        token_i = sb("token_i", [P, 1], I32)
        token = sb("token", [P, 1])
        x_t = two("x_t", [P, D])
        mixed = two("mixed", [P, KD, P])
        h2 = two("h2", [P, D])
        hn = two("hn", [P, D])
        h2b = two("h2b", [P, D])
        squares = sb("squares", [P, D])
        ss = two("ss", [P, 1])
        root = two("root", [P, 1])
        rstd = two("rstd", [P, 1])
        hnT = sb("hnT", [P, KD, P])
        logits = sb("logits", [P, EXPERTS])
        best = two("best", [P, 8])
        best_i = sb("best_i", [P, 8], U32)
        pick = two("pick", [P, TOP])
        neg_best = sb("neg_best", [P, 1])
        powers = two("powers", [P, TOP])
        power_sum = two("power_sum", [P, 1])
        inverse = sb("inverse", [P, 1])
        mask = two("mask", [P, TOP, EXPERTS])
        weighted = sb("weighted", [P, TOP, EXPERTS])
        chosen = two("chosen", [P, EXPERTS])
        gate = two("gate", [P, EXPERTS])
        gateT = sb("gateT", [EXPERTS, P])
        rank_all = sb("rank_all", [P, EXPERTS])
        rank_pick = sb("rank_pick", [P, TOP, EXPERTS])
        rank = sb("rank", [P, TOP])
        place = sb("place", [P, TOP])
        place_i = two("place_i", [P, TOP], U32)
        tile_entry = two("tile_entry", [P, TOP, 2], I32)
        choice_i = sb("choice_i", [P, TOP], I32)
        choice = sb("choice", [P, TOP])
        row = sb("row", [P, TOP])
        op_ps = ctx.enter_context(nc.psum_tensor("route_op_ps", [P, D], F32))
        tp_ps = ctx.enter_context(nc.psum_tensor("route_tp_ps", [P, KD, P], F32))
        gb_ps = ctx.enter_context(nc.psum_tensor("route_gb_ps", [P, D], F32))
        lg_ps = ctx.enter_context(nc.psum_tensor("route_lg_ps", [P, 512], F32))
        rk_ps = ctx.enter_context(nc.psum_tensor("route_rk_ps", [P, 512], F32))

        w_loaded = sem("w_loaded")
        small_loaded = sem("small_loaded")
        made = sem("made")
        staged = sem("staged")
        max_begun = sem("max_begun")
        scatter_begun = sem("scatter_begun")
        made_masks = sem("made_masks")
        x_loaded = sem2("x_loaded")
        proj_ready = sem("proj_ready")
        h2_ready = sem("h2_ready")
        ss_ready = sem("ss_ready")
        hn_ready = sem("hn_ready")
        hn_stored = sem2("hn_stored")
        hn_turned = sem("hn_turned")
        hnT_ready = sem("hnT_ready")
        router_ready = sem("router_ready")
        logits_taken = sem("logits_taken")
        best_ready = sem("best_ready")
        powers_ready = sem("powers_ready")
        picked = sem("picked")
        rank_ready = sem("rank_ready")
        rank_taken = sem("rank_taken")
        gateT_ready = sem("gateT_ready")
        bias_ready = sem("bias_ready")
        h2b_ready = sem("h2b_ready")
        h2b_stored = sem2("h2b_stored")
        placed = sem("placed")
        scattered = sem2("scattered")
        vec_setup = sem("vec_setup")
        root_ready = sem("root_ready")
        chain0, chain1, chain2 = sem("vec_chain_norm"), sem("vec_chain_pick"), sem("vec_chain_place")

        x = a["x"][0]
        w_attn = a["w_out"][0, 0:ATTN].rearrange("(g i d) n -> g d i n", g=N_KV, d=HEAD)
        w_conv = a["w_out"][0, ATTN:].rearrange("(c p) n -> p c n", p=P)

        with nc.Block() as block:
            @block.sync
            def _(sp):
                for g in range(N_KV):
                    sp.dma_start(w_out[g * HEAD:(g + 1) * HEAD, 0:GROUP, :], w_attn[g]).then_inc(w_loaded, 16)
                sp.dma_start(w_out[:, GROUP:, :], w_conv).then_inc(w_loaded, 16)

                def load(t, par, m):
                    wait(sp, h2_ready, t - 1)
                    sp.dma_start(x_t[par][:, :], x[ds(t * P, P), :]).then_inc(x_loaded[par], 16)

                def store_hn(t, par, m):
                    sp.wait_ge(hn_ready, t + 1)
                    sp.dma_start(k.hn[ds(t * P, P), :], hn[par][:, :]).then_inc(hn_stored[par], 16)

                def store_h2(t, par, m):
                    sp.wait_ge(h2b_ready, t + 1)
                    sp.dma_start(k.h2[ds(t * P, P), :], h2b[par][:, :]).then_inc(h2b_stored[par], 16)

                def nothing(t, par, m):
                    pass

                pipeline(sp, TILES, [load, store_hn, nothing, store_h2])
                for s in range(2):
                    sp.wait_ge(hn_stored[s], 16 * (TILES // 2))
                    sp.wait_ge(h2b_stored[s], 16 * (TILES // 2))

            @block.gpsimd
            def _(pool):
                pool.memset(ones[:, :], 1.0).then_inc(made, 1)
                pool.iota(col_i[:, :], pattern=[[1, EXPERTS]], base=0, channel_multiplier=0).then_inc(made, 1)
                pool.iota(token_i[:, :], pattern=[[0, 1]], base=0, channel_multiplier=1).then_inc(made, 1)
                pool.iota(choice_i[:, :], pattern=[[1, TOP]], base=0, channel_multiplier=0).then_inc(made, 1)
                pool.wait_ge(made, 4)
                pool.affine_select(out=before[:, :], in_=ones[:, :], compare_op=ALU.is_gt, fill=0.0, base=0,
                                   pattern=[[1, P]], channel_multiplier=-1).then_inc(made_masks, 1)

                def stage(t, par, m):
                    wait(pool, proj_ready, t - 1)
                    pool.tensor_copy(mixed[par][:, 0:GROUP, :], k.qT[:, :, ds(t * P, P)]).then_inc(staged, 1)
                    pool.tensor_copy(mixed[par][:, GROUP:, :], k.conv[:, :, ds(t * P + META, P)]).then_inc(staged, 1)

                def nothing(t, par, m):
                    pass

                def scatter(t, par, m):
                    pool.wait_ge(placed, t + 1)
                    pool.sem_inc(scatter_begun, 1)
                    for j in range(TOP):
                        pool.indirect_dma_start(
                            k.slot_list, bass.IndirectOffsetOnAxis(ap=place_i[par][:, j:j + 1], axis=0),
                            tile_entry[par][:, j, :], None).then_inc(scattered[par], 16)

                pipeline(pool, TILES, [stage, nothing, scatter])
                for s in range(2):
                    pool.wait_ge(scattered[s], 16 * TOP * (TILES // 2))

            @block.scalar
            def _(act):
                act.dma_start(rw[:, :, :], a["router_w"][0].rearrange("(k p) e -> p k e", p=P)).then_inc(small_loaded, 16)
                act.dma_start(rb[:, :], a["router_b"][0:1, :].to_broadcast([P, EXPERTS])).then_inc(small_loaded, 16)
                act.dma_start(g2[:, :], a["norm2_g"][0:1, :].to_broadcast([P, D])).then_inc(small_loaded, 16)
                act.dma_start(b_down[:, :], a["b_down"][0]).then_inc(small_loaded, 16)

                def square(t, par, m):
                    act.wait_ge(h2_ready, t + 1)
                    wait(act, ss_ready, t)
                    nc.scalar.activation(squares[:, :], h2[par][:, :], ACT.Square, accum_out=ss[par][:, :]) \
                      .then_inc(ss_ready, 1)
                    act.wait_ge(ss_ready, t + 1)
                    nc.scalar.activation(root[par][:, :], ss[par][:, :], ACT.Sqrt, scale=1.0 / D,
                                         bias=k.eps[:, 0:1]).then_inc(root_ready, 1)

                def router(t, par, m):
                    act.wait_ge(hn_turned, t + 1)
                    wait(act, router_ready, t)
                    nc.scalar.activation(hnT[:, :, :], tp_ps[:, :, :], ACT.Copy).then_inc(hnT_ready, 1)
                    act.wait_ge(best_ready, t + 1)
                    nc.scalar.activation(powers[par][:, :], best[par][:, 0:TOP], ACT.Exp, bias=neg_best[:, 0:1],
                                         accum_out=power_sum[par][:, :]).then_inc(powers_ready, 1)

                def gate_up(t, par, m):
                    act.wait_ge(rank_ready, t + 1)
                    wait(act, bias_ready, t)
                    nc.scalar.activation(gateT[:, :], lg_ps[0:EXPERTS, P:2 * P], ACT.Copy).then_inc(gateT_ready, 1)

                pipeline(act, TILES, [square, router, gate_up])

            @block.tensor
            def _(pe):
                pe.wait_ge(w_loaded, 48)
                pe.wait_ge(small_loaded, 64)
                pe.wait_ge(made_masks, 1)

                def project_out(t, par, m):
                    pe.wait_ge(staged, 2 * t + 2)
                    wait(pe, h2_ready, t)
                    for half in range(2):
                        for kk in range(KD):
                            mm = nc.tensor.matmul(op_ps[:, half * 512:(half + 1) * 512], mixed[par][:, kk, :],
                                                  w_out[:, kk, half * 512:(half + 1) * 512],
                                                  start=kk == 0, stop=kk == KD - 1)
                    mm.then_inc(proj_ready, 1)

                def router(t, par, m):
                    pe.wait_ge(hn_ready, t + 1)
                    wait(pe, hnT_ready, t)
                    for kk in range(KD):
                        mm = nc.tensor.transpose(tp_ps[:, kk, :], hn[par][:, kk * P:(kk + 1) * P], k.ident[:, :])
                    mm.then_inc(hn_turned, 1)
                    pe.wait_ge(hnT_ready, t + 1)
                    wait(pe, logits_taken, t)
                    for kk in range(KD):
                        mm = nc.tensor.matmul(lg_ps[:, 0:EXPERTS], hnT[:, kk, :], rw[:, kk, :],
                                              start=kk == 0, stop=kk == KD - 1)
                    mm.then_inc(router_ready, 1)

                def ranks(t, par, m):
                    pe.wait_ge(picked, 2 * t + 2)
                    wait(pe, rank_taken, t)
                    wait(pe, gateT_ready, t)
                    nc.tensor.matmul(rk_ps[:, 0:EXPERTS], before[:, :], chosen[par][:, :], start=True, stop=True)
                    nc.tensor.matmul(rk_ps[:, EXPERTS:2 * EXPERTS], ones[:, :], chosen[par][:, :],
                                     start=True, stop=True)
                    nc.tensor.transpose(lg_ps[0:EXPERTS, P:2 * P], gate[par][:, :], k.ident[:, :]) \
                      .then_inc(rank_ready, 1)
                    pe.wait_ge(gateT_ready, t + 1)
                    wait(pe, h2b_ready, t)
                    for half in range(2):
                        mm = nc.tensor.matmul(gb_ps[:, half * 512:(half + 1) * 512], gateT[:, :],
                                              b_down[:, half * 512:(half + 1) * 512], start=True, stop=True)
                    mm.then_inc(bias_ready, 1)

                pipeline(pe, TILES, [project_out, router, ranks])

            @block.vector
            def _(dve):
                setup = Chain(dve, vec_setup)
                norm, choose, put = Chain(dve, chain0), Chain(dve, chain1), Chain(dve, chain2)
                CHOOSE, PUT = 7, 6
                dve.wait_ge(small_loaded, 64)
                dve.wait_ge(made, 4)
                nc.vector.tensor_copy(choice[:, :], choice_i[:, :])
                nc.vector.tensor_copy(col[:, :], col_i[:, :])
                nc.vector.tensor_copy(token[:, :], token_i[:, :])
                setup.after(nc.vector.memset(k.count[:, :], 0.0))

                def residual(t, par, m):
                    dve.wait_ge(proj_ready, t + 1)
                    dve.wait_ge(x_loaded[par], 16 * (m + 1))
                    nc.vector.tensor_tensor(h2[par][:, :], op_ps[:, :], x_t[par][:, :], ALU.add).then_inc(h2_ready, 1)
                    dve.wait_ge(root_ready, t + 1)
                    norm.begin(t)
                    norm.after(nc.vector.reciprocal(rstd[par][:, :], root[par][:, :]))
                    wait(dve, hn_stored[par], 16 * m)
                    nc.vector.scalar_tensor_tensor(out=hn[par][:, :], in0=h2[par][:, :], scalar=rstd[par][:, 0:1],
                                                   in1=g2[:, :], op0=ALU.mult, op1=ALU.mult).then_inc(hn_ready, 1)

                def pick_top(t, par, m):
                    choose.begin(t * CHOOSE)
                    dve.wait_ge(router_ready, t + 1)
                    nc.vector.tensor_tensor(logits[:, :], lg_ps[:, 0:EXPERTS], rb[:, :], ALU.add) \
                      .then_inc(logits_taken, 1)
                    dve.wait_ge(logits_taken, t + 1)
                    dve.sem_inc(max_begun, 1)
                    choose.after(nc.vector.max(best[par][:, :], logits[:, :]))
                    nc.vector.tensor_scalar(neg_best[:, :], best[par][:, 0:1], -1.0, None, ALU.mult) \
                      .then_inc(best_ready, 1)
                    choose.after(nc.vector.max_index(best_i[:, :], best[par][:, :], logits[:, :]))
                    choose.after(nc.vector.tensor_copy(pick[par][:, :], best_i[:, 0:TOP]))
                    choose.after(nc.vector.tensor_tensor(
                        mask[par][:, :, :], col[:, :].unsqueeze(1).to_broadcast([P, TOP, EXPERTS]),
                        pick[par][:, :].unsqueeze(2).to_broadcast([P, TOP, EXPERTS]), ALU.is_equal))
                    nc.vector.tensor_reduce(chosen[par][:, :], mask[par][:, :, :].rearrange("p j e -> p e j"),
                                            AX_X, ALU.add).then_inc(picked, 1)
                    dve.wait_ge(powers_ready, t + 1)
                    choose.after(nc.vector.reciprocal(inverse[:, :], power_sum[par][:, :]))
                    choose.after(nc.vector.tensor_scalar(powers[par][:, :], powers[par][:, :], inverse[:, 0:1], None,
                                                         ALU.mult))
                    nc.vector.tensor_copy(k.gates[:, ds(t, 1), :].rearrange("p one j -> p (one j)"), powers[par][:, :])
                    choose.after(nc.vector.tensor_tensor(
                        weighted[:, :, :], mask[par][:, :, :],
                        powers[par][:, :].unsqueeze(2).to_broadcast([P, TOP, EXPERTS]), ALU.mult))
                    nc.vector.tensor_reduce(gate[par][:, :], weighted[:, :, :].rearrange("p j e -> p e j"),
                                            AX_X, ALU.add).then_inc(picked, 1)
                    assert choose.n == CHOOSE, choose.n

                def put_rows(t, par, m):
                    put.begin(t * PUT)
                    dve.wait_ge(rank_ready, t + 1)
                    put.after(nc.vector.tensor_tensor(rank_all[:, :], rk_ps[:, 0:EXPERTS], k.count[:, :], ALU.add))
                    nc.vector.tensor_tensor(k.count[:, :], rk_ps[:, EXPERTS:2 * EXPERTS], k.count[:, :], ALU.add) \
                      .then_inc(rank_taken, 1)
                    put.after(nc.vector.tensor_tensor(
                        rank_pick[:, :, :], mask[par][:, :, :],
                        rank_all[:, :].unsqueeze(1).to_broadcast([P, TOP, EXPERTS]), ALU.mult))
                    put.after(nc.vector.tensor_reduce(rank[:, :], rank_pick[:, :, :], AX_X, ALU.add))
                    put.after(nc.vector.scalar_tensor_tensor(out=place[:, :], in0=pick[par][:, :],
                                                             scalar=float(REGION), in1=rank[:, :],
                                                             op0=ALU.mult, op1=ALU.add))
                    wait(dve, scattered[par], 16 * TOP * m)
                    nc.vector.tensor_copy(place_i[par][:, :], place[:, :])
                    put.after(nc.vector.scalar_tensor_tensor(
                        out=row[:, :], in0=token[:, 0:1].to_broadcast([P, TOP]), scalar=float(TOP), in1=choice[:, :],
                        op0=ALU.mult, op1=ALU.add))
                    nc.vector.tensor_copy(tile_entry[par][:, :, 0], token[:, 0:1].to_broadcast([P, TOP]))
                    nc.vector.tensor_copy(tile_entry[par][:, :, 1], row[:, :]).then_inc(placed, 1)
                    dve.wait_ge(placed, t + 1)
                    put.after(nc.vector.tensor_scalar(token[:, :], token[:, :], float(P), None, ALU.add))
                    dve.wait_ge(bias_ready, t + 1)
                    wait(dve, h2b_stored[par], 16 * m)
                    nc.vector.tensor_tensor(h2b[par][:, :], gb_ps[:, :], h2[par][:, :], ALU.add) \
                      .then_inc(h2b_ready, 1)
                    assert put.n == PUT

                pipeline(dve, TILES, [residual, pick_top, put_rows])


def plan(k):
    nc = k.nc
    with ExitStack() as ctx:
        def sb(name, shape, dt=F32):
            return ctx.enter_context(nc.sbuf_tensor("plan_" + name, shape, dt))

        def sem(name):
            return ctx.enter_context(nc.semaphore("plan_" + name))

        T = TABLE
        row_i = sb("row_i", [T, 1], I32)
        col_i = sb("col_i", [T, EXPERTS], I32)
        col = sb("col", [T, EXPERTS])
        row = sb("row", [T, 1])
        ones = sb("ones", [T, EXPERTS])
        passes = sb("passes", [T, EXPERTS])
        upto = sb("upto", [T, EXPERTS])
        past = sb("past", [T, EXPERTS])
        past_passes = sb("past_passes", [T, EXPERTS])
        expert = sb("expert", [T, 1])
        used = sb("used", [T, 1])
        chunk = sb("chunk", [T, 1])
        entry = sb("entry", [T, 4])
        entry_i = sb("entry_i", [T, 4], I32)
        rows_made = sem("rows_made")
        vec_chain = sem("vec_chain")
        table_ready = sem("table_ready")
        table_stored = sem("table_stored")
        table_loaded = sem("table_loaded")
        with nc.Block() as block:
            @block.gpsimd
            def _(pool):
                pool.iota(row_i[:, :], pattern=[[0, 1]], base=0, channel_multiplier=1).then_inc(rows_made, 1)
                pool.memset(ones[:, :], 1.0).then_inc(rows_made, 1)
                pool.iota(col_i[:, :], pattern=[[1, EXPERTS]], base=0, channel_multiplier=0).then_inc(rows_made, 1)

            @block.vector
            def _(dve):
                chain = Chain(dve, vec_chain)
                count = k.count[0:T, :]
                dve.wait_ge(rows_made, 3)
                chain.after(nc.vector.tensor_copy(row[:, :], row_i[:, :]))
                chain.after(nc.vector.tensor_copy(col[:, :], col_i[:, :]))
                chain.after(nc.vector.tensor_scalar(passes[:, :], count, 0.0, None, ALU.is_gt))
                for j in range(1, -(-REGION // PASS)):
                    chain.after(nc.vector.scalar_tensor_tensor(out=passes[:, :], in0=count, scalar=float(j * PASS),
                                                               in1=passes[:, :], op0=ALU.is_gt, op1=ALU.add))
                chain.after(nc.vector.tensor_tensor_scan(upto[:, :], ones[:, :], passes[:, :], 0.0,
                                                         ALU.mult, ALU.add))
                chain.after(nc.vector.tensor_scalar(past[:, :], upto[:, :], row[:, 0:1], None, ALU.is_le))
                chain.after(nc.vector.tensor_reduce(expert[:, :], past[:, :], AX_X, ALU.add))
                chain.after(nc.vector.tensor_tensor(past_passes[:, :], past[:, :], passes[:, :], ALU.mult))
                chain.after(nc.vector.tensor_reduce(used[:, :], past_passes[:, :], AX_X, ALU.add))
                chain.after(nc.vector.tensor_scalar(entry[:, 0:1], expert[:, :], float(EXPERTS - 1), None, ALU.min))
                chain.after(nc.vector.tensor_tensor(chunk[:, :], row[:, :], used[:, :], ALU.subtract))
                chain.after(nc.vector.tensor_scalar(chunk[:, :], chunk[:, :], float(PASS), None, ALU.mult))
                chain.after(nc.vector.scalar_tensor_tensor(out=entry[:, 1:2], in0=entry[:, 0:1],
                                                           scalar=float(REGION), in1=chunk[:, :],
                                                           op0=ALU.mult, op1=ALU.add))
                chain.after(nc.vector.tensor_scalar(entry[:, 1:2], entry[:, 1:2], float(SLOTS - PASS), None, ALU.min))
                chain.after(nc.vector.tensor_copy(entry[:, 2:3], upto[:, EXPERTS - 1:EXPERTS]))
                chain.after(nc.vector.tensor_scalar(past[:, :], col[:, :], entry[:, 0:1], None, ALU.is_equal))
                chain.after(nc.vector.tensor_tensor(past[:, :], past[:, :], count, ALU.mult))
                chain.after(nc.vector.tensor_reduce(expert[:, :], past[:, :], AX_X, ALU.add))
                chain.after(nc.vector.tensor_tensor(entry[:, 3:4], expert[:, :], chunk[:, :], ALU.subtract))
                chain.after(nc.vector.tensor_scalar(entry[:, 3:4], entry[:, 3:4], 0.0, None, ALU.max))
                nc.vector.tensor_copy(entry_i[:, :], entry[:, :]).then_inc(table_ready, 1)

            @block.sync
            def _(sp):
                sp.wait_ge(table_ready, 1)
                sp.dma_start(k.table, entry_i[:, :]).then_inc(table_stored, 16)
                sp.wait_ge(table_stored, 16)
                sp.dma_start(k.tab[:, :], k.table.rearrange("r c -> (r c)").rearrange("(one n) -> one n", one=1)) \
                  .then_inc(table_loaded, 16)
                sp.wait_ge(table_loaded, 16)


def pass_count(k, eng):
    return eng.value_load(k.tab[0:1, 2:3], min_val=1, max_val=MAX_PASSES)


def pass_expert(k, eng, p):
    return eng.value_load(k.tab[0:1, ds(p * 4, 1)], min_val=0, max_val=EXPERTS - 1)


def pass_rows(k, eng, p):
    return eng.value_load(k.tab[0:1, ds(p * 4 + 3, 1)], min_val=0, max_val=SEQ)


def pass_slot(k, eng, p):
    return eng.value_load(k.tab[0:1, ds(p * 4 + 1, 1)], min_val=0, max_val=SLOTS - PASS)


def experts(k):
    nc, a = k.nc, k.a
    CHUNKS = 6
    BUFFERS = 3
    LEAD = 2
    HALF = 512
    F = FF // P
    with ExitStack() as ctx:
        def sb(name, shape, dt=F32):
            return ctx.enter_context(nc.sbuf_tensor("experts_" + name, shape, dt))

        def two(name, shape, dt=F32):
            return [sb(f"{name}{s}", shape, dt) for s in range(2)]

        def sem(name):
            return ctx.enter_context(nc.semaphore("experts_" + name))

        def sem2(name):
            return [sem(f"{name}{s}") for s in range(2)]

        raw = [sb(f"raw{s}", [P, KD // 2, HALF]) for s in range(3)]
        wh = [sb(f"wh{s}", [P, KD, HALF], F32R) for s in range(3)]
        wl = [sb(f"wl{s}", [P, KD, HALF], F32R) for s in range(3)]
        xs = sb("xs", [P, PT, D])
        xh = sb("xh", [P, KD, PASS], F32R)
        xl = sb("xl", [P, KD, PASS], F32R)
        ah = sb("ah", [P, F, PASS], F32R)
        al = sb("al", [P, F, PASS], F32R)
        index = sb("index", [P, PT, 2], I32)
        to_row = sb("to_row", [P, PT], I32)
        g_act = two("g_act", [P, PASS])
        u_act = two("u_act", [P, PASS])
        sg = two("sg", [P, PASS])
        gs = two("gs", [P, PASS])
        act_f = two("act_f", [P, PASS])
        y_rows = two("y_rows", [P, HALF])
        bias_rows = sb("bias_rows", [EXPERTS, 2 * FF // 4])
        bias_gu = sb("bias_gu", [P, 2 * F, EXPERTS])
        gu_ps = ctx.enter_context(nc.psum_tensor("experts_gu_ps", [P, 2, 2, 512], F32))
        dn_ps = ctx.enter_context(nc.psum_tensor("experts_dn_ps", [P, 2, 512], F32))
        xt_ps = ctx.enter_context(nc.psum_tensor("experts_xt_ps", [P, 2, 512], F32))

        bias_loaded = sem("bias_loaded")
        bias_turned = sem("bias_turned")
        bias_copied = sem("bias_copied")
        w_loaded = [sem(f"w_loaded{s}") for s in range(3)]
        high_ready = sem("high_ready")
        low_ready = sem("low_ready")
        index_loaded = sem("index_loaded")
        gather_begun = sem("gather_begun")
        gathered = sem("gathered")
        rows_kept = sem("rows_kept")
        x_turned = sem("x_turned")
        xh_ready = sem("xh_ready")
        xl_ready = sem("xl_ready")
        banks_cleared = sem("banks_cleared")
        gu_ready = sem("gu_ready")
        g_ready = sem("g_ready")
        gu_taken = sem("gu_taken")
        sg_ready = sem("sg_ready")
        gs_ready = sem("gs_ready")
        act_ready = sem("act_ready")
        ah_ready = sem("ah_ready")
        al_ready = sem("al_ready")
        dn_ready = sem("dn_ready")
        y_ready = sem("y_ready")
        y_stored = sem2("y_stored")
        y_free = sem("y_free")

        w_gu = a["w_gate_up"][0].rearrange("e (k p) f -> e p k f", p=P)
        w_dn = a["w_down"][0].rearrange("e (k p) f -> e p k f", p=P)

        with nc.Block() as block:
            @block.sync
            def _(sp):
                BQ = 2 * FF // 4
                for q in range(4):
                    wait(sp, bias_turned, q)
                    sp.dma_start(bias_rows[:, :], a["b_gate_up"][0, :, q * BQ:(q + 1) * BQ]) \
                      .then_inc(bias_loaded, 16)

                def load(e, c, part, j):
                    sp.wait_ge(low_ready, j + 1)
                    to = (2 * c + part) % 3
                    ks = slice(part * 4, part * 4 + 4)
                    if c < 4:
                        for side in range(2):
                            first = side * FF + c * 256
                            sp.dma_start(raw[to][:, :, side * 256:(side + 1) * 256],
                                         w_gu[ds(e, 1), :, ks, first:first + 256]
                                         .rearrange("one p k f -> p (one k) f")).then_inc(w_loaded[to], 16)
                    else:
                        for side in range(2):
                            k0 = part * 4 + side * 2
                            sp.dma_start(raw[to][:, side * 2:side * 2 + 2, :],
                                         w_dn[ds(e, 1), :, k0:k0 + 2, (c - 4) * HALF:(c - 3) * HALF]
                                         .rearrange("one p k f -> p (one k) f")).then_inc(w_loaded[to], 16)

                total = pass_count(k, sp)
                first = pass_expert(k, sp, 0)
                for c in range(LEAD):
                    for part in range(2):
                        load(first, c, part, 2 * c + part)
                with sp.Fori(0, total) as p:
                    e = pass_expert(k, sp, p)
                    for c in range(LEAD, CHUNKS):
                        for part in range(2):
                            load(e, c, part, p * (2 * CHUNKS) + (2 * c + part))
                    e_next = pass_expert(k, sp, p + 1)
                    for c in range(LEAD):
                        for part in range(2):
                            load(e_next, c, part, p * (2 * CHUNKS) + (2 * (CHUNKS + c) + part))

            @block.gpsimd
            def _(pool):
                def gather(p, n):
                    slot = pass_slot(k, pool, p)
                    pool.dma_start(index[:, :, :], k.slot_list[ds(slot, PASS), :].rearrange("(t p) two -> p t two", p=P)) \
                        .then_inc(index_loaded, 16)
                    pool.wait_ge(index_loaded, 16 * n)
                    pool.sem_inc(gather_begun, 1)
                    for t in range(PT):
                        pool.indirect_dma_start(xs[:, t, :], None, k.hn,
                                                bass.IndirectOffsetOnAxis(ap=index[:, t, 0:1], axis=0)) \
                            .then_inc(gathered, 16)

                def keep_rows(n):
                    pool.sem_inc(gather_begun, 1)
                    pool.tensor_copy(to_row[:, :], index[:, :, 1]).then_inc(rows_kept, 1)
                    pool.wait_ge(rows_kept, n)
                    pool.sem_inc(gather_begun, 1)

                total = pass_count(k, pool)
                gather(0, 1)
                pool.wait_ge(x_turned, 2 * PT)
                keep_rows(1)
                gather(1, 2)
                with pool.Fori(0, total) as p:
                    for f in range(F):
                        pool.wait_ge(sg_ready, p * F + (f + 1))
                        pool.tensor_tensor(gs[f % 2][:, :], g_act[f % 2][:, :], sg[f % 2][:, :], ALU.mult).then_inc(gs_ready, 1)
                    for q in range(2 * PT):
                        half, t = q // PT, q % PT
                        pool.wait_ge(y_ready, p * (2 * PT) + (q + 3))
                        pool.sem_inc(gather_begun, 1)
                        pool.indirect_dma_start(k.y[half], bass.IndirectOffsetOnAxis(ap=to_row[:, t:t + 1], axis=0),
                                                y_rows[q % 2][:, :], None, bounds_check=ROWS - 1, oob_is_err=False) \
                            .then_inc(y_stored[q % 2], 16)
                        pool.wait_ge(y_stored[q % 2], (p * PT + (q // 2 + 1)) * 16)
                        pool.sem_inc(y_free, 1)
                    pool.wait_ge(x_turned, p * (2 * PT) + 4 * PT)
                    keep_rows(p + 2)
                    gather(p + 2, p + 3)
                pool.wait_ge(gathered, (total + 2) * (16 * PT))

            @block.scalar
            def _(act):
                def high(p, c, part):
                    if c >= BUFFERS:
                        act.wait_ge(gu_ready, p * F + 2 * (c - BUFFERS + 1))
                    elif not isinstance(p, int) and c == 0:
                        act.wait_ge(gu_ready, (p - 1) * F + F)
                    elif not isinstance(p, int) and c == 1:
                        act.wait_ge(dn_ready, (p - 1) * (2 * PT) + PT)
                    of = (2 * c + part) % 3
                    act.wait_ge(w_loaded[of], (p * (2 * CHUNKS // 3) + ((2 * c + part) // 3 + 1)) * 32)
                    nc.scalar.activation(wh[c % 3][:, part * 4:part * 4 + 4, :], raw[of][:, :, :], ACT.Copy) \
                      .then_inc(high_ready, 1)

                def x_high(p, q):
                    act.wait_ge(x_turned, p * (2 * PT) + (q + 1))
                    k0, t = q % 2 * 4, q // 2
                    nc.scalar.activation(xh[:, k0:k0 + 4, t * P:(t + 1) * P],
                                         xt_ps[:, q % 2, :].rearrange("p (k t) -> p k t", t=P), ACT.Copy) \
                      .then_inc(xh_ready, 1)

                act.sem_inc(y_ready, 2)
                act.sem_inc(y_free, 2)
                total = pass_count(k, act)
                for c in range(LEAD):
                    for part in range(2):
                        high(0, c, part)
                for q in range(2 * PT):
                    x_high(0, q)
                with act.Fori(0, total) as p:
                    def act_high(f):
                        act.wait_ge(act_ready, p * F + (f + 1))
                        nc.scalar.activation(ah[:, f, :], act_f[f % 2][:, :], ACT.Copy).then_inc(ah_ready, 1)

                    for f in range(F):
                        act.wait_ge(g_ready, p * F + (f + 1))
                        nc.scalar.activation(sg[f % 2][:, :], g_act[f % 2][:, :], ACT.Sigmoid, scale=ALPHA) \
                          .then_inc(sg_ready, 1)
                        if f >= 1:
                            act_high(f - 1)
                        if f < F - 1:
                            high(p, LEAD + f // 2, f % 2)
                    act_high(F - 1)
                    x_high(p + 1, 0)
                    x_high(p + 1, 1)
                    high(p, CHUNKS - 1, 1)
                    for q in range(2 * PT):
                        act.wait_ge(dn_ready, p * (2 * PT) + (q + 1))
                        act.wait_ge(y_free, p * (2 * PT) + (q + 1))
                        nc.scalar.activation(y_rows[q % 2][:, :], dn_ps[:, q % 2, :], ACT.Copy).then_inc(y_ready, 1)
                        if q + 2 < 2 * PT:
                            x_high(p + 1, q + 2)
                        if q < 2 * LEAD:
                            high(p + 1, q // 2, q % 2)

            @block.tensor
            def _(pe):
                total = pass_count(k, pe)
                for q in range(4):
                    pe.wait_ge(bias_loaded, 16 * (q + 1))
                    wait(pe, bias_copied, q)
                    for i in range(4):
                        mm = nc.tensor.transpose(xt_ps[:, 0, i * EXPERTS:(i + 1) * EXPERTS],
                                                 bias_rows[:, i * P:(i + 1) * P], k.ident[0:EXPERTS, 0:EXPERTS])
                    mm.then_inc(bias_turned, 1)
                pe.wait_ge(bias_copied, 4)

                def turn(p, q):
                    k0, t = q % 2 * 4, q // 2
                    pe.wait_ge(gathered, (p + 1) * (16 * PT))
                    pe.wait_ge(xl_ready, p * (2 * PT) + (q + 1))
                    for i in range(4):
                        mm = nc.tensor.transpose(xt_ps[:, q % 2, i * P:(i + 1) * P],
                                                 xs[:, t, (k0 + i) * P:(k0 + i + 1) * P], k.ident[:, :])
                    mm.then_inc(x_turned, 1)

                for q in range(2 * PT):
                    turn(0, q)
                def gate_up(p, width):
                    for c in range(4):
                        h, lo = wh[c % 3], wl[c % 3]
                        pe.wait_ge(low_ready, p * (2 * CHUNKS) + (2 * c + 2 + 3))
                        for f2 in range(2):
                            f = 2 * c + f2
                            pe.wait_ge(gu_taken, p * F + (f + 1))
                            for part in range(2):
                                at = slice(part * 256 + f2 * P, part * 256 + (f2 + 1) * P)
                                o = gu_ps[:, f2, part, 0:width]
                                for kk in range(KD):
                                    nc.tensor.matmul(o, h[:, kk, at], xh[:, kk, 0:width], start=kk == 0, stop=False)
                                    nc.tensor.matmul(o, h[:, kk, at], xl[:, kk, 0:width], start=False, stop=False)
                                    mm = nc.tensor.matmul(o, lo[:, kk, at], xh[:, kk, 0:width], start=False,
                                                          stop=kk == KD - 1)
                            mm.then_inc(gu_ready, 1)

                def by_width(p, rows, widths):
                    if len(widths) == 1:
                        gate_up(p, widths[0])
                        return
                    mid = len(widths) // 2
                    with pe.If(rows > widths[mid - 1]):
                        by_width(p, rows, widths[mid:])
                    with pe.Else():
                        by_width(p, rows, widths[:mid])

                def down(p, q, wait_rows):
                    half, t = q // PT, q % PT
                    h, lo = wh[(4 + half) % 3], wl[(4 + half) % 3]
                    o = dn_ps[:, q % 2, :]
                    for f in range(F):
                        if wait_rows:
                            pe.wait_ge(al_ready, p * F + (f + 1))
                        at = slice(t * P, (t + 1) * P)
                        nc.tensor.matmul(o, ah[:, f, at], h[:, f, :], start=f == 0, stop=False)
                        nc.tensor.matmul(o, ah[:, f, at], lo[:, f, :], start=False, stop=False)
                        mm = nc.tensor.matmul(o, al[:, f, at], h[:, f, :], start=False, stop=f == F - 1)
                    mm.then_inc(dn_ready, 1)

                pe.wait_ge(banks_cleared, 2)
                with pe.Fori(0, total) as p:
                    rows = pass_rows(k, pe, p)
                    pe.wait_ge(xl_ready, p * (2 * PT) + (2 * PT + 2))
                    by_width(p, rows, WIDTHS)
                    turn(p + 1, 0)
                    for q in range(2 * PT):
                        half, t = q // PT, q % PT
                        if q + 1 < 2 * PT:
                            turn(p + 1, q + 1)
                        if t == 0:
                            pe.wait_ge(low_ready, p * (2 * CHUNKS) + (2 * (4 + half) + 2 + 3))
                        pe.wait_ge(y_ready, p * (2 * PT) + (q + 1))
                        if t == 0:
                            down(p, q, q == 0)
                        else:
                            with pe.If(rows > t * P):
                                down(p, q, False)
                            with pe.Else():
                                pe.wait_ge(dn_ready, p * (2 * PT) + q)
                                pe.sem_inc(dn_ready, 1)

            @block.vector
            def _(dve):
                def low(p, c, part):
                    dve.wait_ge(high_ready, p * (2 * CHUNKS) + (2 * c + part + 1))
                    ks = slice(part * 4, part * 4 + 4)
                    nc.vector.tensor_tensor(wl[c % 3][:, ks, :], raw[(2 * c + part) % 3][:, :, :],
                                            wh[c % 3][:, ks, :].bitcast(F32), ALU.subtract) \
                      .then_inc(low_ready, 1)

                def x_low(p, q):
                    dve.wait_ge(xh_ready, p * (2 * PT) + (q + 1))
                    k0, t = q % 2 * 4, q // 2
                    at = slice(t * P, (t + 1) * P)
                    nc.vector.tensor_tensor(xl[:, k0:k0 + 4, at],
                                            xt_ps[:, q % 2, :].rearrange("p (k t) -> p k t", t=P),
                                            xh[:, k0:k0 + 4, at].bitcast(F32), ALU.subtract).then_inc(xl_ready, 1)

                dve.sem_inc(low_ready, 3)
                dve.sem_inc(xl_ready, 2)
                dve.sem_inc(gu_taken, 2)
                total = pass_count(k, dve)
                for q in range(4):
                    dve.wait_ge(bias_turned, q + 1)
                    nc.vector.tensor_scalar(bias_gu[:, 4 * q:4 * q + 4, :],
                                            xt_ps[:, 0, 0:4 * EXPERTS].rearrange("p (c e) -> p c e", e=EXPERTS),
                                            1.0 if q >= 2 else 0.0, None, ALU.add).then_inc(bias_copied, 1)
                dve.wait_ge(bias_copied, 4)
                nc.vector.memset(gu_ps[:, :, :, :], 0.0).then_inc(banks_cleared, 1)
                nc.vector.memset(dn_ps[:, :, :], 0.0).then_inc(banks_cleared, 1)
                for c in range(LEAD):
                    for part in range(2):
                        low(0, c, part)
                for q in range(2 * PT):
                    x_low(0, q)
                with dve.Fori(0, total) as p:
                    e = pass_expert(k, dve, p)

                    def take(f):
                        dve.wait_ge(gu_ready, p * F + (f + 1))
                        nc.vector.tensor_scalar(g_act[f % 2][:, :], gu_ps[:, f % 2, 0, 0:PASS],
                                                bias_gu[:, f, ds(e, 1)], LIMIT, ALU.add, ALU.min) \
                          .then_inc(g_ready, 1)
                        nc.vector.tensor_scalar(u_act[f % 2][:, :], gu_ps[:, f % 2, 1, 0:PASS],
                                                bias_gu[:, F + f, ds(e, 1)], LIMIT + 1.0, ALU.add, ALU.min) \
                          .then_inc(gu_taken, 1)

                    def act_mul(f):
                        dve.wait_ge(gu_taken, p * F + (f + 3))
                        dve.wait_ge(gs_ready, p * F + (f + 1))
                        nc.vector.scalar_tensor_tensor(out=act_f[f % 2][:, :], in0=u_act[f % 2][:, :],
                                                       scalar=1.0 - LIMIT, in1=gs[f % 2][:, :],
                                                       op0=ALU.max, op1=ALU.mult).then_inc(act_ready, 1)

                    def act_low(f):
                        dve.wait_ge(ah_ready, p * F + (f + 1))
                        nc.vector.tensor_tensor(al[:, f, :], act_f[f % 2][:, :], ah[:, f, :].bitcast(F32),
                                                ALU.subtract).then_inc(al_ready, 1)

                    for f in range(F):
                        take(f)
                        if f >= 1:
                            act_mul(f - 1)
                            if f < F - 1:
                                low(p, LEAD + (f - 1) // 2, (f - 1) % 2)
                            act_low(f - 1)
                    act_mul(F - 1)
                    act_low(F - 1)
                    x_low(p + 1, 0)
                    x_low(p + 1, 1)
                    low(p, CHUNKS - 1, 0)
                    low(p, CHUNKS - 1, 1)
                    for q in range(2 * PT):
                        if q + 2 < 2 * PT:
                            x_low(p + 1, q + 2)
                        if q < 2 * LEAD:
                            low(p + 1, q // 2, q % 2)


def combine(k):
    nc = k.nc
    out = k.out[0]
    with ExitStack() as ctx:
        def two(name, shape, dt=F32):
            return [ctx.enter_context(nc.sbuf_tensor(f"combine_{name}{s}", shape, dt)) for s in range(2)]

        def sem(name):
            return ctx.enter_context(nc.semaphore("combine_" + name))

        def sem2(name):
            return [sem(f"{name}{s}") for s in range(2)]

        HALF = D // 2
        h2 = two("h2", [P, D])
        rows = two("rows", [P, 2, TOP, HALF])
        h2_loaded = sem2("h2_loaded")
        rows_loaded = sem2("rows_loaded")
        summed = sem("summed")
        out_stored = sem2("out_stored")
        vec_chain = sem("vec_chain")

        def nothing(t, par, m):
            pass

        with nc.Block() as block:
            @block.sync
            def _(sp):
                def load(t, par, m):
                    wait(sp, summed, 2 * (t - 1))
                    for half in range(2):
                        sp.dma_start(rows[par][:, half, :, :].rearrange("p j c -> p (j c)"),
                                     k.y[half][ds(t * (P * TOP), P * TOP), :].rearrange("(p j) c -> p (j c)", j=TOP)) \
                          .then_inc(rows_loaded[par], 16)

                pipeline(sp, TILES, [load, nothing])

            @block.scalar
            def _(act):
                def load(t, par, m):
                    wait(act, out_stored[par], 16 * m)
                    act.dma_start(h2[par][:, :], k.h2[ds(t * P, P), :]).then_inc(h2_loaded[par], 16)

                def store(t, par, m):
                    act.wait_ge(summed, 2 * t + 2)
                    act.dma_start(out[ds(t * P, P), :], h2[par][:, :]).then_inc(out_stored[par], 16)

                pipeline(act, TILES, [load, store])
                for s in range(2):
                    act.wait_ge(out_stored[s], 16 * (TILES // 2))

            @block.vector
            def _(dve):
                chain = Chain(dve, vec_chain)

                def add(t, par, m):
                    chain.begin(t * (TOP - 1))
                    dve.wait_ge(h2_loaded[par], 16 * (m + 1))
                    dve.wait_ge(rows_loaded[par], 32 * (m + 1))
                    for j in range(TOP):
                        for half in range(2):
                            cols = slice(half * HALF, (half + 1) * HALF)
                            ins = nc.vector.scalar_tensor_tensor(
                                out=h2[par][:, cols], in0=rows[par][:, half, j, :],
                                scalar=k.gates[:, ds(t, 1), j:j + 1].rearrange("p one j -> p (one j)"),
                                in1=h2[par][:, cols], op0=ALU.mult, op1=ALU.add)
                            if j == TOP - 1:
                                ins.then_inc(summed, 1)
                        if j < TOP - 1:
                            chain.after(ins)

                pipeline(dve, TILES, [add, nothing])


NAMES = ["x", "meta_tokens", "norm1_g", "w_in", "q_norm_g", "k_norm_g", "attn_sink", "dw_w", "dw_b", "conv_ln_g",
         "conv_ln_b", "w_out", "norm2_g", "router_w", "router_b", "w_gate_up", "b_gate_up", "w_down", "b_down"]


def lay_out(inputs):
    import numpy as np

    arrays = {name: np.asarray(inputs[name]) for name in NAMES}
    for name in ("norm1_g", "dw_b", "conv_ln_g", "conv_ln_b"):
        arrays[name] = arrays[name][0].reshape(-1, P).T
    for name in ("q_norm_g", "k_norm_g"):
        arrays[name] = arrays[name][0].reshape(HEAD, 1)
    arrays["dw_w"] = arrays["dw_w"][0, :, 0, :].T
    return {"in_" + name: np.ascontiguousarray(v) for name, v in arrays.items()}


def kernel(**inputs):
    import concourse.bacc as bacc
    from concourse.bass_utils import run_bass_kernel_spmd

    nc = bacc.Bacc("TRN2", target_bir_lowering=False, num_devices=1)
    arrays = lay_out(inputs)
    aps = {name[3:]: nc.dram_tensor(name, a.shape, mybir.dt.from_np(a.dtype), kind="ExternalInput").ap()
           for name, a in arrays.items()}
    out = nc.dram_tensor("out", (1, SEQ, D), F32, kind="ExternalOutput").ap()
    build(nc, aps, out)
    result = run_bass_kernel_spmd(nc, [arrays], core_ids=[0])
    return result.results[0]["out"]
```

```python
from contextlib import ExitStack

import concourse.bass as bass
from concourse import mybir

F32 = mybir.dt.float32
F32R = mybir.dt.float32r
I32 = mybir.dt.int32
U32 = mybir.dt.uint32
ALU = mybir.AluOpType
ACT = mybir.ActivationFunctionType
AX_X = mybir.AxisListType.X
ds = bass.ds

P = 128
D = 1024
KD = D // P
SEQ = 2048
META = 16
L = META + SEQ
TILES = SEQ // P
HEAD = 64
N_Q = 8
N_KV = 2
GROUP = N_Q // N_KV
ATTN = N_Q * HEAD
KV = N_KV * HEAD
QK = ATTN + KV
CONV = D - ATTN
CC = CONV // P
IN_W = ATTN + 2 * KV + 2 * CONV
TAPS = 31
PAD = 16
BAND = 3 * P
KEYS = META + BAND
EXPERTS = 32
TOP = 4
FF = D
PASS = 384
REGION = -(-SEQ // PASS) * PASS
SLOTS = EXPERTS * REGION
ROWS = SEQ * TOP
PT = PASS // P
WIDTHS = list(range(192, PASS + 1, 16))
MAX_PASSES = (SEQ * TOP + EXPERTS * (PASS - 1)) // PASS
TABLE = 64
RMS_EPS = 1e-6
LN_EPS = 1e-5
NEG = -1e30
LIMIT = 7.0
ALPHA = 1.702
assert MAX_PASSES + 2 <= TABLE and IN_W == 1792


def wait(eng, sem, value):
    if isinstance(value, int) and value <= 0:
        return
    eng.wait_ge(sem, value)


class Chain:

    def __init__(self, eng, sem):
        self.eng, self.sem, self.base, self.n = eng, sem, 0, 0

    def begin(self, base):
        self.base, self.n = base, 0

    def after(self, ins):
        self.n += 1
        ins.then_inc(self.sem, 1)
        self.eng.wait_ge(self.sem, self.base + self.n)


def pipeline(eng, n, stages):
    depth = len(stages)
    lead = depth + depth % 2

    for i in range(lead):
        for s in reversed(range(depth)):
            if i >= s:
                stages[s](i - s, (i - s) % 2, (i - s) // 2)
    with eng.Fori(lead // 2, n // 2) as pair:
        for half in range(2):
            for s in reversed(range(depth)):
                off = half - s
                stages[s](pair * 2 + off, off % 2, pair + off // 2)
    for i in range(n, n + depth - 1):
        for s in reversed(range(depth)):
            if i - s < n:
                stages[s](i - s, (i - s) % 2, (i - s) // 2)


class Kernel:
    pass


def build(nc, a, out, stop=None):
    k = Kernel()
    k.nc, k.a, k.out = nc, a, out
    k.hn = nc.dram_tensor("hn_rows", [SEQ, D], F32, kind="Internal").ap()
    k.h2 = nc.dram_tensor("h2_rows", [SEQ, D], F32, kind="Internal").ap()
    k.slot_list = nc.dram_tensor("slot_list", [SLOTS, 2], I32, kind="Internal").ap()
    k.y = [nc.dram_tensor(f"expert_rows{s}", [ROWS, D // 2], F32, kind="Internal").ap() for s in range(2)]
    k.table = nc.dram_tensor("pass_table", [TABLE, 4], I32, kind="Internal").ap()

    with ExitStack() as whole:
        k.ident = whole.enter_context(nc.sbuf_tensor("ident", [P, P], F32))
        k.eps = whole.enter_context(nc.sbuf_tensor("eps", [P, 2], F32))
        k.gates = whole.enter_context(nc.sbuf_tensor("gates", [P, TILES, TOP], F32))
        k.count = whole.enter_context(nc.sbuf_tensor("count", [P, EXPERTS], F32))
        k.tab = whole.enter_context(nc.sbuf_tensor("tab", [1, TABLE * 4], I32))
        with ExitStack() as front:
            def keep(name, shape, dt=F32):
                return front.enter_context(nc.sbuf_tensor(name, shape, dt))

            k.qT = keep("qT", [P, GROUP, SEQ])
            k.conv = keep("conv", [P, CC, L])
            k.taps = keep("taps", [P, CC, TAPS])
            k.tap_bias = keep("tap_bias", [P, CC])
            with ExitStack() as mixer:
                def keep2(name, shape, dt=F32):
                    return mixer.enter_context(nc.sbuf_tensor(name, shape, dt))

                k.kT = keep2("kT", [P, META + P + SEQ + P])
                k.v = keep2("v", [P, TILES + 2, KV])
                k.v_meta = keep2("v_meta", [META, KV])
                k.hc = keep2("hc", [P, CC, PAD + L + PAD])
                project(k)
                if stop == "project":
                    return k
                attend(k)
            if stop == "attend":
                return k
            conv_norm(k)
            if stop == "conv_norm":
                return k
            route(k)
        if stop == "route":
            return k
        plan(k)
        experts(k)
        combine(k)
    return k


def conv_steps(k, dve, conv_step, done, first, width):
    def start(c):
        k.nc.vector.tensor_scalar(k.conv[:, c, ds(first, width)], k.hc[:, c, ds(first + 1, width)],
                                  k.taps[:, c, 0:1], k.tap_bias[:, c:c + 1], ALU.mult, ALU.add) \
         .then_inc(conv_step, 1)

    def add(t, c):
        dve.wait_ge(conv_step, done + (CC * (t - 1) + c + 1))
        k.nc.vector.scalar_tensor_tensor(
            out=k.conv[:, c, ds(first, width)], in0=k.hc[:, c, ds(first + (1 + t), width)],
            scalar=k.taps[:, c, t:t + 1], in1=k.conv[:, c, ds(first, width)],
            op0=ALU.mult, op1=ALU.add).then_inc(conv_step, 1)

    for c in range(CC):
        yield lambda c=c: start(c)
    for t in range(1, TAPS):
        for c in range(CC):
            yield lambda t=t, c=c: add(t, c)


def project(k):
    nc, a = k.nc, k.a
    PAIR = 2 * P
    ITERS = 1 + SEQ // PAIR
    with ExitStack() as ctx:
        def sb(name, shape, dt=F32):
            return ctx.enter_context(nc.sbuf_tensor("project_" + name, shape, dt))

        def sem(name):
            return ctx.enter_context(nc.semaphore("project_" + name))

        w_in = sb("w_in", [P, KD, IN_W])
        x_rows = [sb(f"x_rows{s}", [P, D]) for s in range(2)]
        xT = [sb(f"xT{s}", [P, KD, PAIR]) for s in range(2)]
        squares = sb("squares", [P, D])
        qk_rows = sb("qk_rows", [P, QK])
        sig = [sb(f"sig{s}", [P, PAIR]) for s in range(2)]
        ss = [sb(f"ss{s}", [P, 1]) for s in range(2)]
        rstd = [sb(f"rstd{s}", [P, 1]) for s in range(2)]
        root = [sb(f"root{s}", [P, 1]) for s in range(2)]
        ss_head = sb("ss_head", [P, N_Q + N_KV])
        root_head = sb("root_head", [P, N_Q + N_KV])
        rstd_head = sb("rstd_head", [P, N_Q + N_KV])
        g1 = sb("g1", [P, KD])
        qg = sb("qg", [P, 1])
        kg = sb("kg", [P, 1])
        tp = ctx.enter_context(nc.psum_tensor("project_tp", [P, 2, 512], F32))
        q_ps = ctx.enter_context(nc.psum_tensor("project_q_ps", [P, ATTN], F32))
        kv_ps = ctx.enter_context(nc.psum_tensor("project_kv_ps", [P, 512], F32))
        u_ps = ctx.enter_context(nc.psum_tensor("project_u_ps", [P, CC, 2, PAIR], F32))

        w_loaded = [sem(f"w_loaded{kk}") for kk in range(KD)]
        w_scaled = sem("w_scaled")
        small_loaded = sem("small_loaded")
        taps_loaded = sem("taps_loaded")
        x_loaded = [sem(f"x_loaded{s}") for s in range(2)]
        eps_ready = sem("eps_ready")
        ident_zeroed = sem("ident_zeroed")
        ident_ready = sem("ident_ready")
        pads_ready = sem("pads_ready")
        ss_ready = sem("ss_ready")
        xn_ready = sem("xn_ready")
        xn_turned = sem("xn_turned")
        xT_ready = sem("xT_ready")
        qkv_ready = sem("qkv_ready")
        head_squares = sem("head_squares")
        v_copied = sem("v_copied")
        qk_ready = sem("qk_ready")
        qk_turned = sem("qk_turned")
        qk_stored = sem("qk_stored")
        u_ready = sem("u_ready")
        sig_ready = sem("sig_ready")
        glu_done = sem("glu_done")
        conv_step = sem("conv_step")
        root_ready = sem("root_ready")
        head_sums = sem("head_sums")
        head_root_ready = sem("head_root_ready")
        vec_chain = sem("vec_chain")

        x = a["x"][0]
        w_view = a["w_in"][0].rearrange("(k p) n -> p k n", p=P)
        LAST = ITERS - 1

        def run(eng, iteration):
            iteration(0, 0, META)
            with eng.Fori(0, (LAST - 2) // 2) as pair:
                for i in range(2):
                    iteration(pair * 2 + (i + 1), (i + 1) % 2, P)
            for n in (LAST - 1, LAST):
                iteration(n, n % 2, P)

        def has(n, more):
            return not isinstance(n, int) or n + more <= LAST

        with nc.Block() as block:
            @block.sync
            def _(sp):
                def load(n, s):
                    wait(sp, xn_turned, 2 * (n - 1) + (s + 1))
                    if isinstance(n, int) and n == 0:
                        sp.dma_start(x_rows[s][0:META, :], a["meta_tokens"]).then_inc(x_loaded[s], 16)
                    else:
                        sp.dma_start(x_rows[s][:, :], x[ds((n - 1) * PAIR + s * P, P), :]).then_inc(x_loaded[s], 16)

                for s in range(2):
                    load(0, s)
                for kk in range(KD):
                    sp.dma_start(w_in[:, kk, :], w_view[:, kk, :]).then_inc(w_loaded[kk], 16)
                with sp.Fori(1, ITERS) as n:
                    for s in range(2):
                        load(n, s)

            @block.gpsimd
            def _(pool):
                pool.memset(k.eps[:, 0:1], RMS_EPS).then_inc(eps_ready, 1)
                pool.memset(k.eps[:, 1:2], LN_EPS).then_inc(eps_ready, 1)
                pool.memset(k.ident[:, :], 0.0).then_inc(ident_zeroed, 1)
                pool.wait_ge(ident_zeroed, 1)
                pool.affine_select(out=k.ident[:, :], in_=k.ident[:, :], compare_op=ALU.not_equal,
                                   fill=1.0, base=0, pattern=[[-1, P]], channel_multiplier=1) \
                    .then_inc(ident_ready, 1)
                pool.memset(k.hc[:, :, 0:PAD], 0.0).then_inc(pads_ready, 1)
                pool.memset(k.hc[:, :, PAD + L:], 0.0).then_inc(pads_ready, 1)
                pool.memset(k.kT[:, :], 0.0).then_inc(pads_ready, 1)
                pool.memset(k.v[:, :, :], 0.0).then_inc(pads_ready, 1)

            @block.scalar
            def _(act):
                act.dma_start(g1[:, :], a["norm1_g"]).then_inc(small_loaded, 16)
                for g in range(N_KV):
                    half = slice(g * HEAD, (g + 1) * HEAD)
                    act.dma_start(qg[half, :], a["q_norm_g"]) \
                       .then_inc(small_loaded, 16)
                    act.dma_start(kg[half, :], a["k_norm_g"]) \
                       .then_inc(small_loaded, 16)
                act.dma_start(k.taps[:, :, :], a["dw_w"].rearrange("(c p) t -> p c t", p=P)).then_inc(taps_loaded, 16)
                act.dma_start(k.tap_bias[:, :], a["dw_b"]).then_inc(taps_loaded, 16)

                act.wait_ge(eps_ready, 2)

                def row_root(n, s, w=P):
                    act.wait_ge(x_loaded[s], 16 * (n + 1))
                    if s == 0:
                        wait(act, head_sums, 2 * (n - 2) + 1)
                    else:
                        wait(act, head_sums, 2 * (n - 2) + 2)
                    nc.scalar.activation(squares[0:w, :], x_rows[s][0:w, :], ACT.Square,
                                         accum_out=ss[s][0:w, :]).then_inc(ss_ready, 1)
                    act.wait_ge(ss_ready, 2 * n + (s + 1))
                    nc.scalar.activation(root[s][0:w, :], ss[s][0:w, :], ACT.Sqrt, scale=1.0 / D,
                                         bias=k.eps[0:w, 0:1]).then_inc(root_ready, 1)

                def copy_x(n, par, s, w):
                    act.wait_ge(xn_turned, 2 * n + (s + 1))
                    for half in range(2):
                        ins = nc.scalar.activation(xT[par][:, half * 4:half * 4 + 4, s * w:(s + 1) * w],
                                                   tp[:, half, :].rearrange("p (k t) -> p k t", t=P)[:, :, 0:w],
                                                   ACT.Copy)
                    ins.then_inc(xT_ready, 1)

                def iteration(n, par, w):
                    cols = META if w == META else PAIR

                    def head_root(s):
                        act.wait_ge(head_sums, 2 * n + (s + 1))
                        nc.scalar.activation(root_head[0:w, :], ss_head[0:w, :], ACT.Sqrt, scale=1.0 / HEAD,
                                             bias=k.eps[0:w, 0:1]).then_inc(head_root_ready, 1)

                    def heads(s):
                        act.wait_ge(qkv_ready, 2 * n + (s + 1))
                        wait(act, head_sums, 2 * n + s)
                        nc.scalar.activation(squares[0:w, 0:ATTN], q_ps[0:w, :], ACT.Square).then_inc(head_squares, 1)
                        nc.scalar.activation(squares[0:w, ATTN:QK], kv_ps[0:w, 0:KV], ACT.Square) \
                          .then_inc(head_squares, 1)
                        if w == META:
                            wait(act, v_copied, s)
                            v_to = k.v_meta[:, :]
                        else:
                            v_to = k.v[:, ds((n - 1) * 2 + (s + 1), 1), :].rearrange("p one c -> p (one c)")
                        nc.scalar.activation(v_to, kv_ps[0:w, KV:2 * KV], ACT.Copy).then_inc(v_copied, 1)

                    def store_qk(s):
                        act.wait_ge(qk_turned, 2 * n + (s + 1))
                        if w == META:
                            wait(act, qk_stored, s)
                            q_at, k_at = ds(0, w), ds(0, w)
                        else:
                            q_at, k_at = ds((n - 1) * PAIR + s * P, w), ds((n - 1) * PAIR + (s * P + META + P), w)
                        if w != META:
                            nc.scalar.activation(k.qT[:, :, q_at],
                                                 tp[:, 0, :].rearrange("p (i t) -> p i t", t=P)[:, :, 0:w],
                                                 ACT.Copy, scale=qg[:, 0:1])
                        nc.scalar.activation(k.kT[:, k_at], tp[:, 1, 0:w], ACT.Copy, scale=kg[:, 0:1]) \
                          .then_inc(qk_stored, 1)

                    def gate(c):
                        act.wait_ge(u_ready, CC * n + (c + 1))
                        wait(act, glu_done, CC * n + (c - 1))
                        nc.scalar.activation(sig[c % 2][:, 0:cols], u_ps[:, c, 1, 0:cols], ACT.Sigmoid) \
                          .then_inc(sig_ready, 1)

                    if has(n, 1):
                        row_root(n + 1, 1)
                    heads(0)
                    if has(n, 1):
                        copy_x(n + 1, 1 - par, 0, P)
                    head_root(0)
                    if has(n, 2):
                        row_root(n + 2, 0)
                    heads(1)
                    store_qk(0)
                    head_root(1)
                    gate(0)
                    gate(1)
                    if has(n, 1):
                        copy_x(n + 1, 1 - par, 1, P)
                    gate(2)
                    store_qk(1)
                    gate(3)

                row_root(0, 0, META)
                row_root(0, 1, META)
                copy_x(0, 0, 0, META)
                copy_x(0, 0, 1, META)
                row_root(1, 0)
                act.wait_ge(small_loaded, 16 * 5)
                act.wait_ge(pads_ready, 4)
                run(act, iteration)

            @block.tensor
            def _(pe):
                pe.wait_ge(ident_ready, 1)

                def turn_x(n, s, w):
                    pe.wait_ge(xn_ready, 2 * n + (s + 1))
                    wait(pe, qk_stored, 2 * (n - 1) + s)
                    if isinstance(n, int) and n == 0:
                        wait(pe, xT_ready, s)
                    for kk in range(KD):
                        mm = nc.tensor.transpose(tp[:, kk // 4, (kk % 4) * P:(kk % 4) * P + w],
                                                 x_rows[s][0:w, kk * P:(kk + 1) * P], k.ident[0:w, 0:w])
                    mm.then_inc(xn_turned, 1)

                def iteration(n, par, w):
                    cols = META if w == META else PAIR

                    def qkv(s):
                        pe.wait_ge(xT_ready, 2 * n + (s + 1))
                        wait(pe, qk_ready, 2 * n + s)
                        wait(pe, v_copied, 2 * n + s)
                        for kk in range(KD):
                            if w == META and s == 0:
                                pe.wait_ge(w_scaled, kk + 1)
                            nc.tensor.matmul(q_ps[0:w, :], xT[par][:, kk, s * w:(s + 1) * w], w_in[:, kk, 0:ATTN],
                                             start=kk == 0, stop=kk == KD - 1)
                        for kk in range(KD):
                            mm = nc.tensor.matmul(kv_ps[0:w, 0:2 * KV], xT[par][:, kk, s * w:(s + 1) * w],
                                                  w_in[:, kk, ATTN:ATTN + 2 * KV], start=kk == 0, stop=kk == KD - 1)
                        mm.then_inc(qkv_ready, 1)

                    def u(c):
                        pe.wait_ge(xT_ready, 2 * n + 2)
                        wait(pe, glu_done, CC * (n - 1) + (c + 1))
                        for half in range(2):
                            first = ATTN + 2 * KV + half * CONV + c * P
                            for kk in range(KD):
                                mm = nc.tensor.matmul(u_ps[:, c, half, 0:cols], w_in[:, kk, first:first + P],
                                                      xT[par][:, kk, 0:cols], start=kk == 0, stop=kk == KD - 1)
                        mm.then_inc(u_ready, 1)

                    def turn_qk(s):
                        pe.wait_ge(qk_ready, 2 * n + (s + 1))
                        if has(n, 1):
                            pe.wait_ge(xT_ready, 2 * n + (s + 3))
                        else:
                            pe.wait_ge(qk_stored, 2 * n + s)
                        for i in range(GROUP):
                            nc.tensor.transpose(tp[:, 0, i * P:i * P + w], qk_rows[0:w, i * P:(i + 1) * P],
                                                k.ident[0:w, 0:w])
                        nc.tensor.transpose(tp[:, 1, 0:w], qk_rows[0:w, ATTN:QK], k.ident[0:w, 0:w]) \
                          .then_inc(qk_turned, 1)

                    qkv(0)
                    if has(n, 1):
                        turn_x(n + 1, 0, P)
                    u(0)
                    qkv(1)
                    turn_qk(0)
                    u(1)
                    if has(n, 1):
                        turn_x(n + 1, 1, P)
                    u(2)
                    turn_qk(1)
                    u(3)

                turn_x(0, 0, META)
                turn_x(0, 1, META)
                run(pe, iteration)

            @block.vector
            def _(dve):
                chain = Chain(dve, vec_chain)

                def scale_rows(n, s, w=P):
                    dve.wait_ge(root_ready, 2 * n + (s + 1))
                    chain.after(nc.vector.reciprocal(rstd[s][0:w, :], root[s][0:w, :]))
                    nc.vector.tensor_scalar(x_rows[s][0:w, :], x_rows[s][0:w, :], rstd[s][0:w, 0:1], None,
                                            ALU.mult).then_inc(xn_ready, 1)

                def iteration(n, par, w):
                    cols = META if w == META else PAIR
                    steps = list(conv_steps(k, dve, conv_step, (n - 2) * (CC * TAPS), (n - 2) * PAIR, PAIR)) \
                        if not isinstance(n, int) or n >= 2 else []

                    def convolve(count):
                        for step in steps[:count]:
                            step()
                        del steps[:count]

                    def norm_heads(s):
                        dve.wait_ge(head_squares, 4 * n + 2 * (s + 1))
                        nc.vector.tensor_reduce(
                            ss_head[0:w, :], squares[0:w, 0:QK].rearrange("p (h d) -> p h d", d=HEAD), AX_X,
                            ALU.add).then_inc(head_sums, 1)
                        convolve(4)
                        dve.wait_ge(head_root_ready, 2 * n + (s + 1))
                        chain.after(nc.vector.reciprocal(rstd_head[0:w, :], root_head[0:w, :]))
                        wait(dve, qk_turned, 2 * n + s)
                        nc.vector.tensor_tensor(
                            qk_rows[0:w, 0:ATTN].rearrange("p (i g d) -> p g i d", g=N_KV, d=HEAD),
                            q_ps[0:w, :].rearrange("p (g i d) -> p g i d", g=N_KV, d=HEAD),
                            rstd_head[0:w, 0:N_Q].rearrange("p (g i) -> p g i", g=N_KV).unsqueeze(3)
                            .to_broadcast([w, N_KV, GROUP, HEAD]), ALU.mult)
                        nc.vector.tensor_tensor(
                            qk_rows[0:w, ATTN:QK].rearrange("p (g d) -> p g d", d=HEAD),
                            kv_ps[0:w, 0:KV].rearrange("p (g d) -> p g d", d=HEAD),
                            rstd_head[0:w, N_Q:].unsqueeze(2).to_broadcast([w, N_KV, HEAD]), ALU.mult) \
                          .then_inc(qk_ready, 1)

                    def glu(c):
                        dve.wait_ge(sig_ready, CC * n + (c + 1))
                        at = ds(PAD, cols) if w == META else ds((n - 1) * PAIR + (PAD + META), cols)
                        nc.vector.tensor_tensor(k.hc[:, c, at], u_ps[:, c, 0, 0:cols], sig[c % 2][:, 0:cols],
                                                ALU.mult).then_inc(glu_done, 1)

                    if steps:
                        dve.wait_ge(glu_done, CC * n)
                    convolve(8)
                    if has(n, 1):
                        scale_rows(n + 1, 1)
                    convolve(20)
                    norm_heads(0)
                    convolve(12)
                    if has(n, 2):
                        scale_rows(n + 2, 0)
                    convolve(28)
                    norm_heads(1)
                    convolve(8)
                    glu(0)
                    glu(1)
                    convolve(20)
                    glu(2)
                    convolve(20)
                    glu(3)
                    assert not steps

                scale_rows(0, 0, META)
                scale_rows(0, 1, META)
                dve.wait_ge(small_loaded, 16 * 5)
                for kk in range(KD):
                    if kk == KD // 2:
                        scale_rows(1, 0)
                    dve.wait_ge(w_loaded[kk], 16)
                    nc.vector.tensor_scalar(w_in[:, kk, :], w_in[:, kk, :], g1[:, kk:kk + 1], None, ALU.mult) \
                      .then_inc(w_scaled, 1)
                dve.wait_ge(taps_loaded, 32)
                dve.wait_ge(pads_ready, 4)
                LOOPED = (LAST - 3) // 2
                counts = [chain.n]
                iteration(0, 0, META)
                counts.append(chain.n)
                iteration(1, 1, P)
                per = chain.n - counts[1]
                start = chain.n
                with dve.Fori(0, LOOPED) as pair:
                    for i in range(2):
                        chain.begin((pair * 2 + i) * per + start)
                        iteration(pair * 2 + (i + 2), i, P)
                        assert chain.n == per
                chain.begin(2 * LOOPED * per + start)
                for n in range(2 + 2 * LOOPED, ITERS):
                    iteration(n, n % 2, P)


def attend(k):
    nc, a = k.nc, k.a
    with ExitStack() as ctx:
        def sb(name, shape, dt=F32):
            return ctx.enter_context(nc.sbuf_tensor("attend_" + name, shape, dt))

        def sem(name):
            return ctx.enter_context(nc.semaphore("attend_" + name))

        empty = sb("empty", [P, SLOTS // P, 2], I32)
        dist_i = sb("dist_i", [P, KEYS], I32)
        dist = sb("dist", [P, KEYS])
        far = sb("far", [P, KEYS])
        bias = sb("bias", [P, N_Q, KEYS])
        sink = sb("sink", [P, N_Q])
        scores = [sb(f"scores{s}", [P, GROUP, KEYS]) for s in range(2)]
        probs = [sb(f"probs{s}", [P, GROUP, KEYS]) for s in range(2)]
        top = [sb(f"top{s}", [P, GROUP]) for s in range(2)]
        neg_top = [sb(f"neg_top{s}", [P, GROUP]) for s in range(2)]
        sink_gap = [sb(f"sink_gap{s}", [P, GROUP]) for s in range(2)]
        sink_exp = [sb(f"sink_exp{s}", [P, GROUP]) for s in range(2)]
        total = [sb(f"total{s}", [P, GROUP]) for s in range(2)]
        inverse = [sb(f"inverse{s}", [P, GROUP]) for s in range(2)]
        pT = [sb(f"pT{s}", [P, 512]) for s in range(2)]
        o_rows = sb("o_rows", [P, ATTN])
        q_block = sb("q_block", [P, GROUP, P])
        k_band = sb("k_band", [P, BAND])
        s_ps = ctx.enter_context(nc.psum_tensor("attend_s_ps", [P, GROUP, 512], F32))
        pt_ps = ctx.enter_context(nc.psum_tensor("attend_pt_ps", [P, 2, 512], F32))
        o_ps = ctx.enter_context(nc.psum_tensor("attend_o_ps", [P, ATTN], F32))
        ot_ps = ctx.enter_context(nc.psum_tensor("attend_ot_ps", [P, ATTN], F32))

        empty_made = sem("empty_made")
        empty_stored = sem("empty_stored")
        dist_made = sem("dist_made")
        sink_loaded = sem("sink_loaded")
        q_staged = sem("q_staged")
        scores_ready = sem("scores_ready")
        scores_taken = sem("scores_taken")
        top_ready = sem("top_ready")
        top_step = sem("top_step")
        inverse_ready = sem("inverse_ready")
        exp_done = sem("exp_done")
        probs_ready = sem("probs_ready")
        bank_cleared = sem("bank_cleared")
        probs_turned = sem("probs_turned")
        pT_ready = sem("pT_ready")
        pT_used = sem("pT_used")
        o_ready = sem("o_ready")
        o_normed = sem("o_normed")
        o_turned = sem("o_turned")
        o_stored = sem("o_stored")
        bias_chain = sem("bias_chain")
        conv_step = sem("conv_step")
        PAIR = 2 * P

        BLOCKS = TILES

        def run(eng, body, peeled=0):
            body(0)
            body(1)
            with eng.Fori(2, BLOCKS - peeled) as b:
                body(b)
            for b in range(BLOCKS - peeled, BLOCKS + 2):
                body(b)

        def has(b):
            return not isinstance(b, int) or 0 <= b < BLOCKS

        def back(b, n):
            if isinstance(b, int):
                return b - n if 0 <= b - n < BLOCKS else None
            return b - n

        with nc.Block() as block:
            @block.sync
            def _(sp):
                sp.wait_ge(empty_made, 2)
                sp.dma_start(k.slot_list.rearrange("(p n) two -> p (n two)", p=P),
                             empty[:, :, :].rearrange("p n two -> p (n two)")).then_inc(empty_stored, 16)
                sp.wait_ge(empty_stored, 16)

            @block.gpsimd
            def _(pool):
                pool.memset(dist_i[:, 0:META], 0).then_inc(dist_made, 1)
                pool.iota(dist_i[:, META:], pattern=[[1, BAND]], base=-P, channel_multiplier=-1) \
                    .then_inc(dist_made, 1)

                def stage(b):
                    wait(pool, scores_ready, 2 * b)
                    pool.tensor_copy(q_block[:, :, :], k.qT[:, :, ds(b * P, P)]).then_inc(q_staged, 1)
                    pool.tensor_copy(k_band[:, :], k.kT[:, ds(b * P + META, BAND)]).then_inc(q_staged, 1)

                stage(0)
                pool.memset(empty[:, :, 0:1], 0).then_inc(empty_made, 1)
                pool.memset(empty[:, :, 1:2], ROWS).then_inc(empty_made, 1)
                with pool.Fori(1, BLOCKS) as b:
                    stage(b)

            @block.tensor
            def _(pe):
                def score(b, g):
                    half = slice(g * HEAD, (g + 1) * HEAD)
                    pe.wait_ge(q_staged, 2 * b + 2)
                    wait(pe, scores_taken, 2 * b + g)
                    for i in range(GROUP):
                        q = q_block[half, i, :]
                        nc.tensor.matmul(s_ps[:, i, 0:META], q, k.kT[half, 0:META], start=True, stop=True)
                        mm = nc.tensor.matmul(s_ps[:, i, META:KEYS], q, k_band[half, :],
                                              start=True, stop=True)
                    mm.then_inc(scores_ready, 1)

                def weigh(b, g):
                    cols = slice(g * HEAD, (g + 1) * HEAD)
                    first = b * (2 * GROUP) + g * GROUP

                    def turn(i):
                        pe.wait_ge(probs_ready, first + (i + 1))
                        wait(pe, pT_ready, first + (i - 1))
                        for j in range(3):
                            nc.tensor.transpose(pt_ps[:, i % 2, j * P:(j + 1) * P],
                                                probs[g][:, i, META + j * P:META + (j + 1) * P], k.ident[:, :])
                        nc.tensor.transpose(pt_ps[0:META, i % 2, BAND:512], probs[g][:, i, 0:META], k.ident[:, :]) \
                          .then_inc(probs_turned, 1)

                    def value(i):
                        pe.wait_ge(pT_ready, first + (i + 1))
                        if i == 0:
                            wait(pe, o_normed, 2 * b + g)
                        o = o_ps[:, i * P + g * HEAD:i * P + (g + 1) * HEAD]
                        for j in range(3):
                            nc.tensor.matmul(o, pT[i % 2][:, j * P:(j + 1) * P], k.v[:, ds(b + j, 1), cols],
                                             start=j == 0, stop=False)
                        nc.tensor.matmul(o, pT[i % 2][0:META, BAND:512], k.v_meta[:, cols],
                                         start=False, stop=True).then_inc(pT_used, 1)

                    turn(0)
                    turn(1)
                    for i in range(GROUP):
                        value(i)
                        if i + 2 < GROUP:
                            turn(i + 2)

                def turn_out(b):
                    pe.wait_ge(o_normed, 2 * b + 2)
                    wait(pe, o_stored, b)
                    for i in range(GROUP):
                        mm = nc.tensor.transpose(ot_ps[:, i * P:(i + 1) * P], o_rows[:, i * P:(i + 1) * P],
                                                 k.ident[:, :])
                    mm.then_inc(o_turned, 1)

                def body(b):
                    for g in range(2):
                        if has(b):
                            score(b, g)
                        if back(b, 1) is not None:
                            weigh(back(b, 1), g)
                        if g == 0 and back(b, 2) is not None:
                            turn_out(back(b, 2))

                pe.wait_ge(bank_cleared, 1)
                run(pe, body)

            @block.scalar
            def _(act):
                act.dma_start(sink[:, :], a["attn_sink"][0:1, :].to_broadcast([P, N_Q])).then_inc(sink_loaded, 16)

                def exps(b, g):
                    act.wait_ge(top_ready, 4 * b + (2 * g + 2))
                    wait(act, probs_turned, b * (2 * GROUP) + (g - 1) * GROUP)
                    for i in range(GROUP):
                        nc.scalar.activation(probs[g][:, i, :], scores[g][:, i, :], ACT.Exp,
                                             bias=neg_top[g][:, i:i + 1],
                                             accum_out=total[g][:, i:i + 1]).then_inc(probs_ready, 1)
                    nc.scalar.activation(sink_exp[g][:, :], sink_gap[g][:, :], ACT.Exp).then_inc(exp_done, 1)

                def copies(b, g):
                    first = b * (2 * GROUP) + g * GROUP
                    for i in range(GROUP):
                        act.wait_ge(probs_turned, first + (i + 1))
                        wait(act, pT_used, first + (i - 1))
                        nc.scalar.activation(pT[i % 2][:, :], pt_ps[:, i % 2, :], ACT.Copy).then_inc(pT_ready, 1)

                def store(b):
                    act.wait_ge(o_turned, b + 1)
                    nc.scalar.activation(k.qT[:, :, ds(b * P, P)], ot_ps[:, :].rearrange("p (i t) -> p i t", t=P),
                                         ACT.Copy).then_inc(o_stored, 1)

                def body(b):
                    if back(b, 1) is not None:
                        exps(back(b, 1), 1)
                        copies(back(b, 1), 0)
                    if has(b):
                        exps(b, 0)
                    if back(b, 2) is not None:
                        store(back(b, 2))
                    if back(b, 1) is not None:
                        copies(back(b, 1), 1)

                run(act, body)

            @block.vector
            def _(dve):
                setup = Chain(dve, bias_chain)
                nc.vector.memset(pt_ps[:, :, :], 0.0).then_inc(bank_cleared, 1)
                dve.wait_ge(dist_made, 2)
                setup.after(nc.vector.tensor_copy(dist[:, :], dist_i[:, :]))
                setup.after(nc.vector.tensor_scalar(far[:, :], dist[:, :], -1.0, None, ALU.mult))
                setup.after(nc.vector.tensor_tensor(dist[:, :], dist[:, :], far[:, :], ALU.max))
                setup.after(nc.vector.tensor_scalar(far[:, :], dist[:, :], float(P), NEG, ALU.is_gt, ALU.mult))
                for h in range(N_Q):
                    slope = 2.0 ** (-8.0 * (h + 1) / N_Q)
                    ins = nc.vector.scalar_tensor_tensor(out=bias[:, h, :], in0=dist[:, :], scalar=-slope,
                                                         in1=far[:, :], op0=ALU.mult, op1=ALU.add)
                setup.after(ins)
                dve.wait_ge(sink_loaded, 16)

                def soft(b, g):
                    heads = slice(g * GROUP, (g + 1) * GROUP)
                    u = 2 * b + g
                    dve.wait_ge(scores_ready, u + 1)
                    wait(dve, exp_done, u - 1)
                    nc.vector.scalar_tensor_tensor(
                        out=scores[g][:, :, :], in0=s_ps[:, :, 0:KEYS], scalar=HEAD ** -0.5,
                        in1=bias[:, heads, :], op0=ALU.mult, op1=ALU.add).then_inc(scores_taken, 1)
                    dve.wait_ge(scores_taken, u + 1)
                    if isinstance(b, int) and b in (0, BLOCKS - 1):
                        cut = META if b == 0 else META + 2 * P
                        setup.after(nc.vector.memset(scores[g][:, :, cut:cut + P], NEG))
                    nc.vector.tensor_reduce(top[g][:, :], scores[g][:, :, :], AX_X, ALU.max).then_inc(top_step, 1)
                    dve.wait_ge(top_step, 2 * u + 1)
                    nc.vector.tensor_tensor(top[g][:, :], top[g][:, :], sink[:, heads], ALU.max).then_inc(top_step, 1)
                    dve.wait_ge(top_step, 2 * u + 2)
                    nc.vector.tensor_scalar(neg_top[g][:, :], top[g][:, :], -1.0, None, ALU.mult) \
                      .then_inc(top_ready, 1)
                    nc.vector.tensor_tensor(sink_gap[g][:, :], sink[:, heads], top[g][:, :],
                                            ALU.subtract).then_inc(top_ready, 1)

                def invert(b, g):
                    u = 2 * b + g
                    dve.wait_ge(exp_done, u + 1)
                    nc.vector.tensor_tensor(total[g][:, :], total[g][:, :], sink_exp[g][:, :], ALU.add) \
                      .then_inc(inverse_ready, 1)
                    dve.wait_ge(inverse_ready, 2 * u + 1)
                    nc.vector.reciprocal(inverse[g][:, :], total[g][:, :]).then_inc(inverse_ready, 1)

                def norm(b, g):
                    u = 2 * b + g
                    dve.wait_ge(pT_used, b * (2 * GROUP) + (g + 1) * GROUP)
                    dve.wait_ge(inverse_ready, 2 * u + 2)
                    if g == 0:
                        wait(dve, o_turned, b)
                    nc.vector.tensor_tensor(
                        o_rows[:, :].rearrange("p (i g d) -> p g i d", g=N_KV, d=HEAD)[:, g, :, :],
                        o_ps[:, :].rearrange("p (i g d) -> p g i d", g=N_KV, d=HEAD)[:, g, :, :],
                        inverse[g][:, :].unsqueeze(2).to_broadcast([P, GROUP, HEAD]), ALU.mult) \
                      .then_inc(o_normed, 1)

                steps = list(conv_steps(k, dve, conv_step, 0, SEQ - PAIR, PAIR)) \
                    + list(conv_steps(k, dve, conv_step, CC * TAPS, SEQ, META))

                def convolve(b):
                    if isinstance(b, int):
                        for step in steps[:CONV_SHARE]:
                            step()
                        del steps[:CONV_SHARE]

                def body(b):
                    for g in range(2):
                        done, weighed = (back(b, 2), 1) if g == 0 else (back(b, 1), 0), (back(b, 1), g)
                        if done[0] is not None:
                            norm(*done)
                        if weighed[0] is not None:
                            invert(*weighed)
                        if has(b):
                            soft(b, g)
                        convolve(b)

                CONV_SHARE = -(-len(steps) // 8)
                run(dve, body, peeled=1)
                assert not steps


def conv_norm(k):
    nc, a = k.nc, k.a
    SPAN = 512
    with ExitStack() as ctx:
        def sb(name, shape, dt=F32):
            return ctx.enter_context(nc.sbuf_tensor("conv_norm_" + name, shape, dt))

        def sem(name):
            return ctx.enter_context(nc.semaphore("conv_norm_" + name))

        ones = sb("ones", [P, P])
        gain = sb("gain", [P, CC])
        shift = sb("shift", [P, CC])
        side = [sb(f"side{s}", [P, CC, SPAN]) for s in range(2)]
        inv = [sb(f"inv{s}", [P, SPAN]) for s in range(2)]
        root = [sb(f"root{s}", [P, SPAN]) for s in range(2)]
        mean_ps = ctx.enter_context(nc.psum_tensor("conv_norm_mean_ps", [P, 2, SPAN], F32))
        var_ps = ctx.enter_context(nc.psum_tensor("conv_norm_var_ps", [P, 2, SPAN], F32))
        ones_ready = sem("ones_ready")
        small_loaded = sem("small_loaded")
        mean_ready = sem("mean_ready")
        centred = sem("centred")
        squared = sem("squared")
        var_ready = sem("var_ready")
        scaled = sem("scaled")
        sigmoid_ready = sem("sigmoid_ready")
        swished = sem("swished")
        root_ready = sem("root_ready")
        vec_chain = sem("vec_chain")

        def z(i, c=None):
            at = ds(META + i * SPAN, SPAN)
            return k.conv[:, :, at] if c is None else k.conv[:, c, at]

        spans = SEQ // SPAN
        with nc.Block() as block:
            @block.gpsimd
            def _(pool):
                pool.memset(ones[:, :], 1.0 / CONV).then_inc(ones_ready, 1)

            @block.tensor
            def _(pe):
                pe.wait_ge(ones_ready, 1)

                def mean(i, par, m):
                    for c in range(CC):
                        mm = nc.tensor.matmul(mean_ps[:, par, :], ones[:, :], z(i, c), start=c == 0, stop=c == CC - 1)
                    mm.then_inc(mean_ready, 1)

                def variance(i, par, m):
                    pe.wait_ge(squared, i + 1)
                    for c in range(CC):
                        mm = nc.tensor.matmul(var_ps[:, par, :], ones[:, :], side[par][:, c, :],
                                              start=c == 0, stop=c == CC - 1)
                    mm.then_inc(var_ready, 1)

                for i in range(spans):
                    if i < 2:
                        mean(i, i % 2, i // 2)
                for i in range(spans):
                    variance(i, i % 2, i // 2)
                    if i + 2 < spans:
                        pe.wait_ge(centred, i + 1)
                        mean(i + 2, i % 2, i // 2)

            @block.scalar
            def _(act):
                act.dma_start(gain[:, :], a["conv_ln_g"]).then_inc(small_loaded, 16)
                act.dma_start(shift[:, :], a["conv_ln_b"]).then_inc(small_loaded, 16)
                act.wait_ge(small_loaded, 32)

                def square(i):
                    act.wait_ge(centred, i + 1)
                    wait(act, swished, i - 1)
                    nc.scalar.activation(side[i % 2][:, :, :], z(i), ACT.Square).then_inc(squared, 1)

                def sigmoid(i):
                    act.wait_ge(scaled, i + 1)
                    for c in range(CC):
                        nc.scalar.activation(side[i % 2][:, c, :], z(i, c), ACT.Sigmoid, scale=gain[:, c:c + 1],
                                             bias=shift[:, c:c + 1]).then_inc(sigmoid_ready, 1)

                def deviation(i):
                    act.wait_ge(var_ready, i + 1)
                    wait(act, scaled, i - 1)
                    nc.scalar.activation(root[i % 2][:, :], var_ps[:, i % 2, :], ACT.Sqrt, bias=k.eps[:, 1:2]) \
                      .then_inc(root_ready, 1)

                square(0)
                for i in range(spans):
                    if i + 1 < spans:
                        square(i + 1)
                    deviation(i)
                    sigmoid(i)

            @block.vector
            def _(dve):
                chain = Chain(dve, vec_chain)
                dve.wait_ge(small_loaded, 32)

                def centre(i):
                    dve.wait_ge(mean_ready, i + 1)
                    nc.vector.tensor_tensor(z(i), z(i), mean_ps[:, i % 2, :].unsqueeze(1).to_broadcast([P, CC, SPAN]),
                                            ALU.subtract).then_inc(centred, 1)

                def scale(i):
                    dve.wait_ge(root_ready, i + 1)
                    chain.after(nc.vector.reciprocal(inv[i % 2][:, :], root[i % 2][:, :]))
                    nc.vector.tensor_tensor(z(i), z(i), inv[i % 2][:, :].unsqueeze(1).to_broadcast([P, CC, SPAN]),
                                            ALU.mult).then_inc(scaled, 1)

                def swish(i):
                    dve.wait_ge(sigmoid_ready, CC * (i + 1))
                    for c in range(CC):
                        ins = nc.vector.tensor_scalar(z(i, c), z(i, c), gain[:, c:c + 1], shift[:, c:c + 1],
                                                      ALU.mult, ALU.add)
                    chain.after(ins)
                    nc.vector.tensor_tensor(z(i), z(i), side[i % 2][:, :, :], ALU.mult).then_inc(swished, 1)

                centre(0)
                for i in range(spans):
                    if i + 1 < spans:
                        centre(i + 1)
                    scale(i)
                    swish(i)


def route(k):
    nc, a = k.nc, k.a
    with ExitStack() as ctx:
        def sb(name, shape, dt=F32):
            return ctx.enter_context(nc.sbuf_tensor("route_" + name, shape, dt))

        def two(name, shape, dt=F32):
            return [sb(f"{name}{s}", shape, dt) for s in range(2)]

        def sem(name):
            return ctx.enter_context(nc.semaphore("route_" + name))

        def sem2(name):
            return [sem(f"{name}{s}") for s in range(2)]

        w_out = sb("w_out", [P, KD, D])
        g2 = sb("g2", [P, D])
        rw = sb("rw", [P, KD, EXPERTS])
        rb = sb("rb", [P, EXPERTS])
        b_down = sb("b_down", [EXPERTS, D])
        before = sb("before", [P, P])
        ones = sb("ones", [P, P])
        col_i = sb("col_i", [P, EXPERTS], I32)
        col = sb("col", [P, EXPERTS])
        token_i = sb("token_i", [P, 1], I32)
        token = sb("token", [P, 1])
        x_t = two("x_t", [P, D])
        mixed = two("mixed", [P, KD, P])
        h2 = two("h2", [P, D])
        hn = two("hn", [P, D])
        h2b = two("h2b", [P, D])
        squares = sb("squares", [P, D])
        ss = two("ss", [P, 1])
        root = two("root", [P, 1])
        rstd = two("rstd", [P, 1])
        hnT = sb("hnT", [P, KD, P])
        logits = sb("logits", [P, EXPERTS])
        best = two("best", [P, 8])
        best_i = sb("best_i", [P, 8], U32)
        pick = two("pick", [P, TOP])
        neg_best = sb("neg_best", [P, 1])
        powers = two("powers", [P, TOP])
        power_sum = two("power_sum", [P, 1])
        inverse = sb("inverse", [P, 1])
        mask = two("mask", [P, TOP, EXPERTS])
        weighted = sb("weighted", [P, TOP, EXPERTS])
        chosen = two("chosen", [P, EXPERTS])
        gate = two("gate", [P, EXPERTS])
        gateT = sb("gateT", [EXPERTS, P])
        rank_all = sb("rank_all", [P, EXPERTS])
        rank_pick = sb("rank_pick", [P, TOP, EXPERTS])
        rank = sb("rank", [P, TOP])
        place = sb("place", [P, TOP])
        place_i = two("place_i", [P, TOP], U32)
        tile_entry = two("tile_entry", [P, TOP, 2], I32)
        choice_i = sb("choice_i", [P, TOP], I32)
        choice = sb("choice", [P, TOP])
        row = sb("row", [P, TOP])
        op_ps = ctx.enter_context(nc.psum_tensor("route_op_ps", [P, D], F32))
        tp_ps = ctx.enter_context(nc.psum_tensor("route_tp_ps", [P, KD, P], F32))
        gb_ps = ctx.enter_context(nc.psum_tensor("route_gb_ps", [P, D], F32))
        lg_ps = ctx.enter_context(nc.psum_tensor("route_lg_ps", [P, 512], F32))
        rk_ps = ctx.enter_context(nc.psum_tensor("route_rk_ps", [P, 512], F32))

        w_loaded = sem("w_loaded")
        small_loaded = sem("small_loaded")
        made = sem("made")
        staged = sem("staged")
        max_begun = sem("max_begun")
        scatter_begun = sem("scatter_begun")
        made_masks = sem("made_masks")
        x_loaded = sem2("x_loaded")
        proj_ready = sem("proj_ready")
        h2_ready = sem("h2_ready")
        ss_ready = sem("ss_ready")
        hn_ready = sem("hn_ready")
        hn_stored = sem2("hn_stored")
        hn_turned = sem("hn_turned")
        hnT_ready = sem("hnT_ready")
        router_ready = sem("router_ready")
        logits_taken = sem("logits_taken")
        best_ready = sem("best_ready")
        powers_ready = sem("powers_ready")
        picked = sem("picked")
        rank_ready = sem("rank_ready")
        rank_taken = sem("rank_taken")
        gateT_ready = sem("gateT_ready")
        bias_ready = sem("bias_ready")
        h2b_ready = sem("h2b_ready")
        h2b_stored = sem2("h2b_stored")
        placed = sem("placed")
        scattered = sem2("scattered")
        vec_setup = sem("vec_setup")
        root_ready = sem("root_ready")
        chain0, chain1, chain2 = sem("vec_chain_norm"), sem("vec_chain_pick"), sem("vec_chain_place")

        x = a["x"][0]
        w_attn = a["w_out"][0, 0:ATTN].rearrange("(g i d) n -> g d i n", g=N_KV, d=HEAD)
        w_conv = a["w_out"][0, ATTN:].rearrange("(c p) n -> p c n", p=P)

        with nc.Block() as block:
            @block.sync
            def _(sp):
                for g in range(N_KV):
                    sp.dma_start(w_out[g * HEAD:(g + 1) * HEAD, 0:GROUP, :], w_attn[g]).then_inc(w_loaded, 16)
                sp.dma_start(w_out[:, GROUP:, :], w_conv).then_inc(w_loaded, 16)

                def load(t, par, m):
                    wait(sp, h2_ready, t - 1)
                    sp.dma_start(x_t[par][:, :], x[ds(t * P, P), :]).then_inc(x_loaded[par], 16)

                def store_hn(t, par, m):
                    sp.wait_ge(hn_ready, t + 1)
                    sp.dma_start(k.hn[ds(t * P, P), :], hn[par][:, :]).then_inc(hn_stored[par], 16)

                def store_h2(t, par, m):
                    sp.wait_ge(h2b_ready, t + 1)
                    sp.dma_start(k.h2[ds(t * P, P), :], h2b[par][:, :]).then_inc(h2b_stored[par], 16)

                def nothing(t, par, m):
                    pass

                pipeline(sp, TILES, [load, store_hn, nothing, store_h2])
                for s in range(2):
                    sp.wait_ge(hn_stored[s], 16 * (TILES // 2))
                    sp.wait_ge(h2b_stored[s], 16 * (TILES // 2))

            @block.gpsimd
            def _(pool):
                pool.memset(ones[:, :], 1.0).then_inc(made, 1)
                pool.iota(col_i[:, :], pattern=[[1, EXPERTS]], base=0, channel_multiplier=0).then_inc(made, 1)
                pool.iota(token_i[:, :], pattern=[[0, 1]], base=0, channel_multiplier=1).then_inc(made, 1)
                pool.iota(choice_i[:, :], pattern=[[1, TOP]], base=0, channel_multiplier=0).then_inc(made, 1)
                pool.wait_ge(made, 4)
                pool.affine_select(out=before[:, :], in_=ones[:, :], compare_op=ALU.is_gt, fill=0.0, base=0,
                                   pattern=[[1, P]], channel_multiplier=-1).then_inc(made_masks, 1)

                def stage(t, par, m):
                    wait(pool, proj_ready, t - 1)
                    pool.tensor_copy(mixed[par][:, 0:GROUP, :], k.qT[:, :, ds(t * P, P)]).then_inc(staged, 1)
                    pool.tensor_copy(mixed[par][:, GROUP:, :], k.conv[:, :, ds(t * P + META, P)]).then_inc(staged, 1)

                def nothing(t, par, m):
                    pass

                def scatter(t, par, m):
                    pool.wait_ge(placed, t + 1)
                    pool.sem_inc(scatter_begun, 1)
                    for j in range(TOP):
                        pool.indirect_dma_start(
                            k.slot_list, bass.IndirectOffsetOnAxis(ap=place_i[par][:, j:j + 1], axis=0),
                            tile_entry[par][:, j, :], None).then_inc(scattered[par], 16)

                pipeline(pool, TILES, [stage, nothing, scatter])
                for s in range(2):
                    pool.wait_ge(scattered[s], 16 * TOP * (TILES // 2))

            @block.scalar
            def _(act):
                act.dma_start(rw[:, :, :], a["router_w"][0].rearrange("(k p) e -> p k e", p=P)).then_inc(small_loaded, 16)
                act.dma_start(rb[:, :], a["router_b"][0:1, :].to_broadcast([P, EXPERTS])).then_inc(small_loaded, 16)
                act.dma_start(g2[:, :], a["norm2_g"][0:1, :].to_broadcast([P, D])).then_inc(small_loaded, 16)
                act.dma_start(b_down[:, :], a["b_down"][0]).then_inc(small_loaded, 16)

                def square(t, par, m):
                    act.wait_ge(h2_ready, t + 1)
                    wait(act, ss_ready, t)
                    nc.scalar.activation(squares[:, :], h2[par][:, :], ACT.Square, accum_out=ss[par][:, :]) \
                      .then_inc(ss_ready, 1)
                    act.wait_ge(ss_ready, t + 1)
                    nc.scalar.activation(root[par][:, :], ss[par][:, :], ACT.Sqrt, scale=1.0 / D,
                                         bias=k.eps[:, 0:1]).then_inc(root_ready, 1)

                def router(t, par, m):
                    act.wait_ge(hn_turned, t + 1)
                    wait(act, router_ready, t)
                    nc.scalar.activation(hnT[:, :, :], tp_ps[:, :, :], ACT.Copy).then_inc(hnT_ready, 1)
                    act.wait_ge(best_ready, t + 1)
                    nc.scalar.activation(powers[par][:, :], best[par][:, 0:TOP], ACT.Exp, bias=neg_best[:, 0:1],
                                         accum_out=power_sum[par][:, :]).then_inc(powers_ready, 1)

                def gate_up(t, par, m):
                    act.wait_ge(rank_ready, t + 1)
                    wait(act, bias_ready, t)
                    nc.scalar.activation(gateT[:, :], lg_ps[0:EXPERTS, P:2 * P], ACT.Copy).then_inc(gateT_ready, 1)

                pipeline(act, TILES, [square, router, gate_up])

            @block.tensor
            def _(pe):
                pe.wait_ge(w_loaded, 48)
                pe.wait_ge(small_loaded, 64)
                pe.wait_ge(made_masks, 1)

                def project_out(t, par, m):
                    pe.wait_ge(staged, 2 * t + 2)
                    wait(pe, h2_ready, t)
                    for half in range(2):
                        for kk in range(KD):
                            mm = nc.tensor.matmul(op_ps[:, half * 512:(half + 1) * 512], mixed[par][:, kk, :],
                                                  w_out[:, kk, half * 512:(half + 1) * 512],
                                                  start=kk == 0, stop=kk == KD - 1)
                    mm.then_inc(proj_ready, 1)

                def router(t, par, m):
                    pe.wait_ge(hn_ready, t + 1)
                    wait(pe, hnT_ready, t)
                    for kk in range(KD):
                        mm = nc.tensor.transpose(tp_ps[:, kk, :], hn[par][:, kk * P:(kk + 1) * P], k.ident[:, :])
                    mm.then_inc(hn_turned, 1)
                    pe.wait_ge(hnT_ready, t + 1)
                    wait(pe, logits_taken, t)
                    for kk in range(KD):
                        mm = nc.tensor.matmul(lg_ps[:, 0:EXPERTS], hnT[:, kk, :], rw[:, kk, :],
                                              start=kk == 0, stop=kk == KD - 1)
                    mm.then_inc(router_ready, 1)

                def ranks(t, par, m):
                    pe.wait_ge(picked, 2 * t + 2)
                    wait(pe, rank_taken, t)
                    wait(pe, gateT_ready, t)
                    nc.tensor.matmul(rk_ps[:, 0:EXPERTS], before[:, :], chosen[par][:, :], start=True, stop=True)
                    nc.tensor.matmul(rk_ps[:, EXPERTS:2 * EXPERTS], ones[:, :], chosen[par][:, :],
                                     start=True, stop=True)
                    nc.tensor.transpose(lg_ps[0:EXPERTS, P:2 * P], gate[par][:, :], k.ident[:, :]) \
                      .then_inc(rank_ready, 1)
                    pe.wait_ge(gateT_ready, t + 1)
                    wait(pe, h2b_ready, t)
                    for half in range(2):
                        mm = nc.tensor.matmul(gb_ps[:, half * 512:(half + 1) * 512], gateT[:, :],
                                              b_down[:, half * 512:(half + 1) * 512], start=True, stop=True)
                    mm.then_inc(bias_ready, 1)

                pipeline(pe, TILES, [project_out, router, ranks])

            @block.vector
            def _(dve):
                setup = Chain(dve, vec_setup)
                norm, choose, put = Chain(dve, chain0), Chain(dve, chain1), Chain(dve, chain2)
                CHOOSE, PUT = 7, 6
                dve.wait_ge(small_loaded, 64)
                dve.wait_ge(made, 4)
                nc.vector.tensor_copy(choice[:, :], choice_i[:, :])
                nc.vector.tensor_copy(col[:, :], col_i[:, :])
                nc.vector.tensor_copy(token[:, :], token_i[:, :])
                setup.after(nc.vector.memset(k.count[:, :], 0.0))

                def residual(t, par, m):
                    dve.wait_ge(proj_ready, t + 1)
                    dve.wait_ge(x_loaded[par], 16 * (m + 1))
                    nc.vector.tensor_tensor(h2[par][:, :], op_ps[:, :], x_t[par][:, :], ALU.add).then_inc(h2_ready, 1)
                    dve.wait_ge(root_ready, t + 1)
                    norm.begin(t)
                    norm.after(nc.vector.reciprocal(rstd[par][:, :], root[par][:, :]))
                    wait(dve, hn_stored[par], 16 * m)
                    nc.vector.scalar_tensor_tensor(out=hn[par][:, :], in0=h2[par][:, :], scalar=rstd[par][:, 0:1],
                                                   in1=g2[:, :], op0=ALU.mult, op1=ALU.mult).then_inc(hn_ready, 1)

                def pick_top(t, par, m):
                    choose.begin(t * CHOOSE)
                    dve.wait_ge(router_ready, t + 1)
                    nc.vector.tensor_tensor(logits[:, :], lg_ps[:, 0:EXPERTS], rb[:, :], ALU.add) \
                      .then_inc(logits_taken, 1)
                    dve.wait_ge(logits_taken, t + 1)
                    dve.sem_inc(max_begun, 1)
                    choose.after(nc.vector.max(best[par][:, :], logits[:, :]))
                    nc.vector.tensor_scalar(neg_best[:, :], best[par][:, 0:1], -1.0, None, ALU.mult) \
                      .then_inc(best_ready, 1)
                    choose.after(nc.vector.max_index(best_i[:, :], best[par][:, :], logits[:, :]))
                    choose.after(nc.vector.tensor_copy(pick[par][:, :], best_i[:, 0:TOP]))
                    choose.after(nc.vector.tensor_tensor(
                        mask[par][:, :, :], col[:, :].unsqueeze(1).to_broadcast([P, TOP, EXPERTS]),
                        pick[par][:, :].unsqueeze(2).to_broadcast([P, TOP, EXPERTS]), ALU.is_equal))
                    nc.vector.tensor_reduce(chosen[par][:, :], mask[par][:, :, :].rearrange("p j e -> p e j"),
                                            AX_X, ALU.add).then_inc(picked, 1)
                    dve.wait_ge(powers_ready, t + 1)
                    choose.after(nc.vector.reciprocal(inverse[:, :], power_sum[par][:, :]))
                    choose.after(nc.vector.tensor_scalar(powers[par][:, :], powers[par][:, :], inverse[:, 0:1], None,
                                                         ALU.mult))
                    nc.vector.tensor_copy(k.gates[:, ds(t, 1), :].rearrange("p one j -> p (one j)"), powers[par][:, :])
                    choose.after(nc.vector.tensor_tensor(
                        weighted[:, :, :], mask[par][:, :, :],
                        powers[par][:, :].unsqueeze(2).to_broadcast([P, TOP, EXPERTS]), ALU.mult))
                    nc.vector.tensor_reduce(gate[par][:, :], weighted[:, :, :].rearrange("p j e -> p e j"),
                                            AX_X, ALU.add).then_inc(picked, 1)
                    assert choose.n == CHOOSE, choose.n

                def put_rows(t, par, m):
                    put.begin(t * PUT)
                    dve.wait_ge(rank_ready, t + 1)
                    put.after(nc.vector.tensor_tensor(rank_all[:, :], rk_ps[:, 0:EXPERTS], k.count[:, :], ALU.add))
                    nc.vector.tensor_tensor(k.count[:, :], rk_ps[:, EXPERTS:2 * EXPERTS], k.count[:, :], ALU.add) \
                      .then_inc(rank_taken, 1)
                    put.after(nc.vector.tensor_tensor(
                        rank_pick[:, :, :], mask[par][:, :, :],
                        rank_all[:, :].unsqueeze(1).to_broadcast([P, TOP, EXPERTS]), ALU.mult))
                    put.after(nc.vector.tensor_reduce(rank[:, :], rank_pick[:, :, :], AX_X, ALU.add))
                    put.after(nc.vector.scalar_tensor_tensor(out=place[:, :], in0=pick[par][:, :],
                                                             scalar=float(REGION), in1=rank[:, :],
                                                             op0=ALU.mult, op1=ALU.add))
                    wait(dve, scattered[par], 16 * TOP * m)
                    nc.vector.tensor_copy(place_i[par][:, :], place[:, :])
                    put.after(nc.vector.scalar_tensor_tensor(
                        out=row[:, :], in0=token[:, 0:1].to_broadcast([P, TOP]), scalar=float(TOP), in1=choice[:, :],
                        op0=ALU.mult, op1=ALU.add))
                    nc.vector.tensor_copy(tile_entry[par][:, :, 0], token[:, 0:1].to_broadcast([P, TOP]))
                    nc.vector.tensor_copy(tile_entry[par][:, :, 1], row[:, :]).then_inc(placed, 1)
                    dve.wait_ge(placed, t + 1)
                    put.after(nc.vector.tensor_scalar(token[:, :], token[:, :], float(P), None, ALU.add))
                    dve.wait_ge(bias_ready, t + 1)
                    wait(dve, h2b_stored[par], 16 * m)
                    nc.vector.tensor_tensor(h2b[par][:, :], gb_ps[:, :], h2[par][:, :], ALU.add) \
                      .then_inc(h2b_ready, 1)
                    assert put.n == PUT

                pipeline(dve, TILES, [residual, pick_top, put_rows])


def plan(k):
    nc = k.nc
    with ExitStack() as ctx:
        def sb(name, shape, dt=F32):
            return ctx.enter_context(nc.sbuf_tensor("plan_" + name, shape, dt))

        def sem(name):
            return ctx.enter_context(nc.semaphore("plan_" + name))

        T = TABLE
        row_i = sb("row_i", [T, 1], I32)
        col_i = sb("col_i", [T, EXPERTS], I32)
        col = sb("col", [T, EXPERTS])
        row = sb("row", [T, 1])
        ones = sb("ones", [T, EXPERTS])
        passes = sb("passes", [T, EXPERTS])
        upto = sb("upto", [T, EXPERTS])
        past = sb("past", [T, EXPERTS])
        past_passes = sb("past_passes", [T, EXPERTS])
        expert = sb("expert", [T, 1])
        used = sb("used", [T, 1])
        chunk = sb("chunk", [T, 1])
        entry = sb("entry", [T, 4])
        entry_i = sb("entry_i", [T, 4], I32)
        rows_made = sem("rows_made")
        vec_chain = sem("vec_chain")
        table_ready = sem("table_ready")
        table_stored = sem("table_stored")
        table_loaded = sem("table_loaded")
        with nc.Block() as block:
            @block.gpsimd
            def _(pool):
                pool.iota(row_i[:, :], pattern=[[0, 1]], base=0, channel_multiplier=1).then_inc(rows_made, 1)
                pool.memset(ones[:, :], 1.0).then_inc(rows_made, 1)
                pool.iota(col_i[:, :], pattern=[[1, EXPERTS]], base=0, channel_multiplier=0).then_inc(rows_made, 1)

            @block.vector
            def _(dve):
                chain = Chain(dve, vec_chain)
                count = k.count[0:T, :]
                dve.wait_ge(rows_made, 3)
                chain.after(nc.vector.tensor_copy(row[:, :], row_i[:, :]))
                chain.after(nc.vector.tensor_copy(col[:, :], col_i[:, :]))
                chain.after(nc.vector.tensor_scalar(passes[:, :], count, 0.0, None, ALU.is_gt))
                for j in range(1, -(-REGION // PASS)):
                    chain.after(nc.vector.scalar_tensor_tensor(out=passes[:, :], in0=count, scalar=float(j * PASS),
                                                               in1=passes[:, :], op0=ALU.is_gt, op1=ALU.add))
                chain.after(nc.vector.tensor_tensor_scan(upto[:, :], ones[:, :], passes[:, :], 0.0,
                                                         ALU.mult, ALU.add))
                chain.after(nc.vector.tensor_scalar(past[:, :], upto[:, :], row[:, 0:1], None, ALU.is_le))
                chain.after(nc.vector.tensor_reduce(expert[:, :], past[:, :], AX_X, ALU.add))
                chain.after(nc.vector.tensor_tensor(past_passes[:, :], past[:, :], passes[:, :], ALU.mult))
                chain.after(nc.vector.tensor_reduce(used[:, :], past_passes[:, :], AX_X, ALU.add))
                chain.after(nc.vector.tensor_scalar(entry[:, 0:1], expert[:, :], float(EXPERTS - 1), None, ALU.min))
                chain.after(nc.vector.tensor_tensor(chunk[:, :], row[:, :], used[:, :], ALU.subtract))
                chain.after(nc.vector.tensor_scalar(chunk[:, :], chunk[:, :], float(PASS), None, ALU.mult))
                chain.after(nc.vector.scalar_tensor_tensor(out=entry[:, 1:2], in0=entry[:, 0:1],
                                                           scalar=float(REGION), in1=chunk[:, :],
                                                           op0=ALU.mult, op1=ALU.add))
                chain.after(nc.vector.tensor_scalar(entry[:, 1:2], entry[:, 1:2], float(SLOTS - PASS), None, ALU.min))
                chain.after(nc.vector.tensor_copy(entry[:, 2:3], upto[:, EXPERTS - 1:EXPERTS]))
                chain.after(nc.vector.tensor_scalar(past[:, :], col[:, :], entry[:, 0:1], None, ALU.is_equal))
                chain.after(nc.vector.tensor_tensor(past[:, :], past[:, :], count, ALU.mult))
                chain.after(nc.vector.tensor_reduce(expert[:, :], past[:, :], AX_X, ALU.add))
                chain.after(nc.vector.tensor_tensor(entry[:, 3:4], expert[:, :], chunk[:, :], ALU.subtract))
                chain.after(nc.vector.tensor_scalar(entry[:, 3:4], entry[:, 3:4], 0.0, None, ALU.max))
                nc.vector.tensor_copy(entry_i[:, :], entry[:, :]).then_inc(table_ready, 1)

            @block.sync
            def _(sp):
                sp.wait_ge(table_ready, 1)
                sp.dma_start(k.table, entry_i[:, :]).then_inc(table_stored, 16)
                sp.wait_ge(table_stored, 16)
                sp.dma_start(k.tab[:, :], k.table.rearrange("r c -> (r c)").rearrange("(one n) -> one n", one=1)) \
                  .then_inc(table_loaded, 16)
                sp.wait_ge(table_loaded, 16)


def pass_count(k, eng):
    return eng.value_load(k.tab[0:1, 2:3], min_val=1, max_val=MAX_PASSES)


def pass_expert(k, eng, p):
    return eng.value_load(k.tab[0:1, ds(p * 4, 1)], min_val=0, max_val=EXPERTS - 1)


def pass_rows(k, eng, p):
    return eng.value_load(k.tab[0:1, ds(p * 4 + 3, 1)], min_val=0, max_val=SEQ)


def pass_slot(k, eng, p):
    return eng.value_load(k.tab[0:1, ds(p * 4 + 1, 1)], min_val=0, max_val=SLOTS - PASS)


def experts(k):
    nc, a = k.nc, k.a
    CHUNKS = 6
    BUFFERS = 3
    LEAD = 2
    HALF = 512
    F = FF // P
    with ExitStack() as ctx:
        def sb(name, shape, dt=F32):
            return ctx.enter_context(nc.sbuf_tensor("experts_" + name, shape, dt))

        def two(name, shape, dt=F32):
            return [sb(f"{name}{s}", shape, dt) for s in range(2)]

        def sem(name):
            return ctx.enter_context(nc.semaphore("experts_" + name))

        def sem2(name):
            return [sem(f"{name}{s}") for s in range(2)]

        raw = [sb(f"raw{s}", [P, KD // 2, HALF]) for s in range(3)]
        wh = [sb(f"wh{s}", [P, KD, HALF], F32R) for s in range(3)]
        wl = [sb(f"wl{s}", [P, KD, HALF], F32R) for s in range(3)]
        xs = sb("xs", [P, PT, D])
        xh = sb("xh", [P, KD, PASS], F32R)
        xl = sb("xl", [P, KD, PASS], F32R)
        ah = sb("ah", [P, F, PASS], F32R)
        al = sb("al", [P, F, PASS], F32R)
        index = sb("index", [P, PT, 2], I32)
        to_row = sb("to_row", [P, PT], I32)
        g_act = two("g_act", [P, PASS])
        u_act = two("u_act", [P, PASS])
        sg = two("sg", [P, PASS])
        gs = two("gs", [P, PASS])
        act_f = two("act_f", [P, PASS])
        y_rows = two("y_rows", [P, HALF])
        bias_rows = sb("bias_rows", [EXPERTS, 2 * FF // 4])
        bias_gu = sb("bias_gu", [P, 2 * F, EXPERTS])
        gu_ps = ctx.enter_context(nc.psum_tensor("experts_gu_ps", [P, 2, 2, 512], F32))
        dn_ps = ctx.enter_context(nc.psum_tensor("experts_dn_ps", [P, 2, 512], F32))
        xt_ps = ctx.enter_context(nc.psum_tensor("experts_xt_ps", [P, 2, 512], F32))

        bias_loaded = sem("bias_loaded")
        bias_turned = sem("bias_turned")
        bias_copied = sem("bias_copied")
        w_loaded = [sem(f"w_loaded{s}") for s in range(3)]
        high_ready = sem("high_ready")
        low_ready = sem("low_ready")
        index_loaded = sem("index_loaded")
        gather_begun = sem("gather_begun")
        gathered = sem("gathered")
        rows_kept = sem("rows_kept")
        x_turned = sem("x_turned")
        xh_ready = sem("xh_ready")
        xl_ready = sem("xl_ready")
        banks_cleared = sem("banks_cleared")
        gu_ready = sem("gu_ready")
        g_ready = sem("g_ready")
        gu_taken = sem("gu_taken")
        sg_ready = sem("sg_ready")
        gs_ready = sem("gs_ready")
        act_ready = sem("act_ready")
        ah_ready = sem("ah_ready")
        al_ready = sem("al_ready")
        dn_ready = sem("dn_ready")
        y_ready = sem("y_ready")
        y_stored = sem2("y_stored")
        y_free = sem("y_free")

        w_gu = a["w_gate_up"][0].rearrange("e (k p) f -> e p k f", p=P)
        w_dn = a["w_down"][0].rearrange("e (k p) f -> e p k f", p=P)

        with nc.Block() as block:
            @block.sync
            def _(sp):
                BQ = 2 * FF // 4
                for q in range(4):
                    wait(sp, bias_turned, q)
                    sp.dma_start(bias_rows[:, :], a["b_gate_up"][0, :, q * BQ:(q + 1) * BQ]) \
                      .then_inc(bias_loaded, 16)

                def load(e, c, part, j):
                    sp.wait_ge(low_ready, j + 1)
                    to = (2 * c + part) % 3
                    ks = slice(part * 4, part * 4 + 4)
                    if c < 4:
                        for side in range(2):
                            first = side * FF + c * 256
                            sp.dma_start(raw[to][:, :, side * 256:(side + 1) * 256],
                                         w_gu[ds(e, 1), :, ks, first:first + 256]
                                         .rearrange("one p k f -> p (one k) f")).then_inc(w_loaded[to], 16)
                    else:
                        for side in range(2):
                            k0 = part * 4 + side * 2
                            sp.dma_start(raw[to][:, side * 2:side * 2 + 2, :],
                                         w_dn[ds(e, 1), :, k0:k0 + 2, (c - 4) * HALF:(c - 3) * HALF]
                                         .rearrange("one p k f -> p (one k) f")).then_inc(w_loaded[to], 16)

                total = pass_count(k, sp)
                first = pass_expert(k, sp, 0)
                for c in range(LEAD):
                    for part in range(2):
                        load(first, c, part, 2 * c + part)
                with sp.Fori(0, total) as p:
                    e = pass_expert(k, sp, p)
                    for c in range(LEAD, CHUNKS):
                        for part in range(2):
                            load(e, c, part, p * (2 * CHUNKS) + (2 * c + part))
                    e_next = pass_expert(k, sp, p + 1)
                    for c in range(LEAD):
                        for part in range(2):
                            load(e_next, c, part, p * (2 * CHUNKS) + (2 * (CHUNKS + c) + part))

            @block.gpsimd
            def _(pool):
                def gather(p, n):
                    slot = pass_slot(k, pool, p)
                    pool.dma_start(index[:, :, :], k.slot_list[ds(slot, PASS), :].rearrange("(t p) two -> p t two", p=P)) \
                        .then_inc(index_loaded, 16)
                    pool.wait_ge(index_loaded, 16 * n)
                    pool.sem_inc(gather_begun, 1)
                    for t in range(PT):
                        pool.indirect_dma_start(xs[:, t, :], None, k.hn,
                                                bass.IndirectOffsetOnAxis(ap=index[:, t, 0:1], axis=0)) \
                            .then_inc(gathered, 16)

                def keep_rows(n):
                    pool.sem_inc(gather_begun, 1)
                    pool.tensor_copy(to_row[:, :], index[:, :, 1]).then_inc(rows_kept, 1)
                    pool.wait_ge(rows_kept, n)
                    pool.sem_inc(gather_begun, 1)

                total = pass_count(k, pool)
                gather(0, 1)
                pool.wait_ge(x_turned, 2 * PT)
                keep_rows(1)
                gather(1, 2)
                with pool.Fori(0, total) as p:
                    for f in range(F):
                        pool.wait_ge(sg_ready, p * F + (f + 1))
                        pool.tensor_tensor(gs[f % 2][:, :], g_act[f % 2][:, :], sg[f % 2][:, :], ALU.mult).then_inc(gs_ready, 1)
                    for q in range(2 * PT):
                        half, t = q // PT, q % PT
                        pool.wait_ge(y_ready, p * (2 * PT) + (q + 3))
                        pool.sem_inc(gather_begun, 1)
                        pool.indirect_dma_start(k.y[half], bass.IndirectOffsetOnAxis(ap=to_row[:, t:t + 1], axis=0),
                                                y_rows[q % 2][:, :], None, bounds_check=ROWS - 1, oob_is_err=False) \
                            .then_inc(y_stored[q % 2], 16)
                        pool.wait_ge(y_stored[q % 2], (p * PT + (q // 2 + 1)) * 16)
                        pool.sem_inc(y_free, 1)
                    pool.wait_ge(x_turned, p * (2 * PT) + 4 * PT)
                    keep_rows(p + 2)
                    gather(p + 2, p + 3)
                pool.wait_ge(gathered, (total + 2) * (16 * PT))

            @block.scalar
            def _(act):
                def high(p, c, part):
                    if c >= BUFFERS:
                        act.wait_ge(gu_ready, p * F + 2 * (c - BUFFERS + 1))
                    elif not isinstance(p, int) and c == 0:
                        act.wait_ge(gu_ready, (p - 1) * F + F)
                    elif not isinstance(p, int) and c == 1:
                        act.wait_ge(dn_ready, (p - 1) * (2 * PT) + PT)
                    of = (2 * c + part) % 3
                    act.wait_ge(w_loaded[of], (p * (2 * CHUNKS // 3) + ((2 * c + part) // 3 + 1)) * 32)
                    nc.scalar.activation(wh[c % 3][:, part * 4:part * 4 + 4, :], raw[of][:, :, :], ACT.Copy) \
                      .then_inc(high_ready, 1)

                def x_high(p, q):
                    act.wait_ge(x_turned, p * (2 * PT) + (q + 1))
                    k0, t = q % 2 * 4, q // 2
                    nc.scalar.activation(xh[:, k0:k0 + 4, t * P:(t + 1) * P],
                                         xt_ps[:, q % 2, :].rearrange("p (k t) -> p k t", t=P), ACT.Copy) \
                      .then_inc(xh_ready, 1)

                act.sem_inc(y_ready, 2)
                act.sem_inc(y_free, 2)
                total = pass_count(k, act)
                for c in range(LEAD):
                    for part in range(2):
                        high(0, c, part)
                for q in range(2 * PT):
                    x_high(0, q)
                with act.Fori(0, total) as p:
                    def act_high(f):
                        act.wait_ge(act_ready, p * F + (f + 1))
                        nc.scalar.activation(ah[:, f, :], act_f[f % 2][:, :], ACT.Copy).then_inc(ah_ready, 1)

                    for f in range(F):
                        act.wait_ge(g_ready, p * F + (f + 1))
                        nc.scalar.activation(sg[f % 2][:, :], g_act[f % 2][:, :], ACT.Sigmoid, scale=ALPHA) \
                          .then_inc(sg_ready, 1)
                        if f >= 1:
                            act_high(f - 1)
                        if f < F - 1:
                            high(p, LEAD + f // 2, f % 2)
                    act_high(F - 1)
                    x_high(p + 1, 0)
                    x_high(p + 1, 1)
                    high(p, CHUNKS - 1, 1)
                    for q in range(2 * PT):
                        act.wait_ge(dn_ready, p * (2 * PT) + (q + 1))
                        act.wait_ge(y_free, p * (2 * PT) + (q + 1))
                        nc.scalar.activation(y_rows[q % 2][:, :], dn_ps[:, q % 2, :], ACT.Copy).then_inc(y_ready, 1)
                        if q + 2 < 2 * PT:
                            x_high(p + 1, q + 2)
                        if q < 2 * LEAD:
                            high(p + 1, q // 2, q % 2)

            @block.tensor
            def _(pe):
                total = pass_count(k, pe)
                for q in range(4):
                    pe.wait_ge(bias_loaded, 16 * (q + 1))
                    wait(pe, bias_copied, q)
                    for i in range(4):
                        mm = nc.tensor.transpose(xt_ps[:, 0, i * EXPERTS:(i + 1) * EXPERTS],
                                                 bias_rows[:, i * P:(i + 1) * P], k.ident[0:EXPERTS, 0:EXPERTS])
                    mm.then_inc(bias_turned, 1)
                pe.wait_ge(bias_copied, 4)

                def turn(p, q):
                    k0, t = q % 2 * 4, q // 2
                    pe.wait_ge(gathered, (p + 1) * (16 * PT))
                    pe.wait_ge(xl_ready, p * (2 * PT) + (q + 1))
                    for i in range(4):
                        mm = nc.tensor.transpose(xt_ps[:, q % 2, i * P:(i + 1) * P],
                                                 xs[:, t, (k0 + i) * P:(k0 + i + 1) * P], k.ident[:, :])
                    mm.then_inc(x_turned, 1)

                for q in range(2 * PT):
                    turn(0, q)
                def gate_up(p, width):
                    for c in range(4):
                        h, lo = wh[c % 3], wl[c % 3]
                        pe.wait_ge(low_ready, p * (2 * CHUNKS) + (2 * c + 2 + 3))
                        for f2 in range(2):
                            f = 2 * c + f2
                            pe.wait_ge(gu_taken, p * F + (f + 1))
                            for part in range(2):
                                at = slice(part * 256 + f2 * P, part * 256 + (f2 + 1) * P)
                                o = gu_ps[:, f2, part, 0:width]
                                for kk in range(KD):
                                    nc.tensor.matmul(o, h[:, kk, at], xh[:, kk, 0:width], start=kk == 0, stop=False)
                                    nc.tensor.matmul(o, h[:, kk, at], xl[:, kk, 0:width], start=False, stop=False)
                                    mm = nc.tensor.matmul(o, lo[:, kk, at], xh[:, kk, 0:width], start=False,
                                                          stop=kk == KD - 1)
                            mm.then_inc(gu_ready, 1)

                def by_width(p, rows, widths):
                    if len(widths) == 1:
                        gate_up(p, widths[0])
                        return
                    mid = len(widths) // 2
                    with pe.If(rows > widths[mid - 1]):
                        by_width(p, rows, widths[mid:])
                    with pe.Else():
                        by_width(p, rows, widths[:mid])

                def down(p, q, wait_rows):
                    half, t = q // PT, q % PT
                    h, lo = wh[(4 + half) % 3], wl[(4 + half) % 3]
                    o = dn_ps[:, q % 2, :]
                    for f in range(F):
                        if wait_rows:
                            pe.wait_ge(al_ready, p * F + (f + 1))
                        at = slice(t * P, (t + 1) * P)
                        nc.tensor.matmul(o, ah[:, f, at], h[:, f, :], start=f == 0, stop=False)
                        nc.tensor.matmul(o, ah[:, f, at], lo[:, f, :], start=False, stop=False)
                        mm = nc.tensor.matmul(o, al[:, f, at], h[:, f, :], start=False, stop=f == F - 1)
                    mm.then_inc(dn_ready, 1)

                pe.wait_ge(banks_cleared, 2)
                with pe.Fori(0, total) as p:
                    rows = pass_rows(k, pe, p)
                    pe.wait_ge(xl_ready, p * (2 * PT) + (2 * PT + 2))
                    by_width(p, rows, WIDTHS)
                    turn(p + 1, 0)
                    for q in range(2 * PT):
                        half, t = q // PT, q % PT
                        if q + 1 < 2 * PT:
                            turn(p + 1, q + 1)
                        if t == 0:
                            pe.wait_ge(low_ready, p * (2 * CHUNKS) + (2 * (4 + half) + 2 + 3))
                        pe.wait_ge(y_ready, p * (2 * PT) + (q + 1))
                        if t == 0:
                            down(p, q, q == 0)
                        else:
                            with pe.If(rows > t * P):
                                down(p, q, False)
                            with pe.Else():
                                pe.wait_ge(dn_ready, p * (2 * PT) + q)
                                pe.sem_inc(dn_ready, 1)

            @block.vector
            def _(dve):
                def low(p, c, part):
                    dve.wait_ge(high_ready, p * (2 * CHUNKS) + (2 * c + part + 1))
                    ks = slice(part * 4, part * 4 + 4)
                    nc.vector.tensor_tensor(wl[c % 3][:, ks, :], raw[(2 * c + part) % 3][:, :, :],
                                            wh[c % 3][:, ks, :].bitcast(F32), ALU.subtract) \
                      .then_inc(low_ready, 1)

                def x_low(p, q):
                    dve.wait_ge(xh_ready, p * (2 * PT) + (q + 1))
                    k0, t = q % 2 * 4, q // 2
                    at = slice(t * P, (t + 1) * P)
                    nc.vector.tensor_tensor(xl[:, k0:k0 + 4, at],
                                            xt_ps[:, q % 2, :].rearrange("p (k t) -> p k t", t=P),
                                            xh[:, k0:k0 + 4, at].bitcast(F32), ALU.subtract).then_inc(xl_ready, 1)

                dve.sem_inc(low_ready, 3)
                dve.sem_inc(xl_ready, 2)
                dve.sem_inc(gu_taken, 2)
                total = pass_count(k, dve)
                for q in range(4):
                    dve.wait_ge(bias_turned, q + 1)
                    nc.vector.tensor_scalar(bias_gu[:, 4 * q:4 * q + 4, :],
                                            xt_ps[:, 0, 0:4 * EXPERTS].rearrange("p (c e) -> p c e", e=EXPERTS),
                                            1.0 if q >= 2 else 0.0, None, ALU.add).then_inc(bias_copied, 1)
                dve.wait_ge(bias_copied, 4)
                nc.vector.memset(gu_ps[:, :, :, :], 0.0).then_inc(banks_cleared, 1)
                nc.vector.memset(dn_ps[:, :, :], 0.0).then_inc(banks_cleared, 1)
                for c in range(LEAD):
                    for part in range(2):
                        low(0, c, part)
                for q in range(2 * PT):
                    x_low(0, q)
                with dve.Fori(0, total) as p:
                    e = pass_expert(k, dve, p)

                    def take(f):
                        dve.wait_ge(gu_ready, p * F + (f + 1))
                        nc.vector.tensor_scalar(g_act[f % 2][:, :], gu_ps[:, f % 2, 0, 0:PASS],
                                                bias_gu[:, f, ds(e, 1)], LIMIT, ALU.add, ALU.min) \
                          .then_inc(g_ready, 1)
                        nc.vector.tensor_scalar(u_act[f % 2][:, :], gu_ps[:, f % 2, 1, 0:PASS],
                                                bias_gu[:, F + f, ds(e, 1)], LIMIT + 1.0, ALU.add, ALU.min) \
                          .then_inc(gu_taken, 1)

                    def act_mul(f):
                        dve.wait_ge(gu_taken, p * F + (f + 3))
                        dve.wait_ge(gs_ready, p * F + (f + 1))
                        nc.vector.scalar_tensor_tensor(out=act_f[f % 2][:, :], in0=u_act[f % 2][:, :],
                                                       scalar=1.0 - LIMIT, in1=gs[f % 2][:, :],
                                                       op0=ALU.max, op1=ALU.mult).then_inc(act_ready, 1)

                    def act_low(f):
                        dve.wait_ge(ah_ready, p * F + (f + 1))
                        nc.vector.tensor_tensor(al[:, f, :], act_f[f % 2][:, :], ah[:, f, :].bitcast(F32),
                                                ALU.subtract).then_inc(al_ready, 1)

                    for f in range(F):
                        take(f)
                        if f >= 1:
                            act_mul(f - 1)
                            if f < F - 1:
                                low(p, LEAD + (f - 1) // 2, (f - 1) % 2)
                            act_low(f - 1)
                    act_mul(F - 1)
                    act_low(F - 1)
                    x_low(p + 1, 0)
                    x_low(p + 1, 1)
                    low(p, CHUNKS - 1, 0)
                    low(p, CHUNKS - 1, 1)
                    for q in range(2 * PT):
                        if q + 2 < 2 * PT:
                            x_low(p + 1, q + 2)
                        if q < 2 * LEAD:
                            low(p + 1, q // 2, q % 2)


def combine(k):
    nc = k.nc
    out = k.out[0]
    with ExitStack() as ctx:
        def two(name, shape, dt=F32):
            return [ctx.enter_context(nc.sbuf_tensor(f"combine_{name}{s}", shape, dt)) for s in range(2)]

        def sem(name):
            return ctx.enter_context(nc.semaphore("combine_" + name))

        def sem2(name):
            return [sem(f"{name}{s}") for s in range(2)]

        HALF = D // 2
        h2 = two("h2", [P, D])
        rows = two("rows", [P, 2, TOP, HALF])
        h2_loaded = sem2("h2_loaded")
        rows_loaded = sem2("rows_loaded")
        summed = sem("summed")
        out_stored = sem2("out_stored")
        vec_chain = sem("vec_chain")

        def nothing(t, par, m):
            pass

        with nc.Block() as block:
            @block.sync
            def _(sp):
                def load(t, par, m):
                    wait(sp, summed, 2 * (t - 1))
                    for half in range(2):
                        sp.dma_start(rows[par][:, half, :, :].rearrange("p j c -> p (j c)"),
                                     k.y[half][ds(t * (P * TOP), P * TOP), :].rearrange("(p j) c -> p (j c)", j=TOP)) \
                          .then_inc(rows_loaded[par], 16)

                pipeline(sp, TILES, [load, nothing])

            @block.scalar
            def _(act):
                def load(t, par, m):
                    wait(act, out_stored[par], 16 * m)
                    act.dma_start(h2[par][:, :], k.h2[ds(t * P, P), :]).then_inc(h2_loaded[par], 16)

                def store(t, par, m):
                    act.wait_ge(summed, 2 * t + 2)
                    act.dma_start(out[ds(t * P, P), :], h2[par][:, :]).then_inc(out_stored[par], 16)

                pipeline(act, TILES, [load, store])
                for s in range(2):
                    act.wait_ge(out_stored[s], 16 * (TILES // 2))

            @block.vector
            def _(dve):
                chain = Chain(dve, vec_chain)

                def add(t, par, m):
                    chain.begin(t * (TOP - 1))
                    dve.wait_ge(h2_loaded[par], 16 * (m + 1))
                    dve.wait_ge(rows_loaded[par], 32 * (m + 1))
                    for j in range(TOP):
                        for half in range(2):
                            cols = slice(half * HALF, (half + 1) * HALF)
                            ins = nc.vector.scalar_tensor_tensor(
                                out=h2[par][:, cols], in0=rows[par][:, half, j, :],
                                scalar=k.gates[:, ds(t, 1), j:j + 1].rearrange("p one j -> p (one j)"),
                                in1=h2[par][:, cols], op0=ALU.mult, op1=ALU.add)
                            if j == TOP - 1:
                                ins.then_inc(summed, 1)
                        if j < TOP - 1:
                            chain.after(ins)

                pipeline(dve, TILES, [add, nothing])


NAMES = ["x", "meta_tokens", "norm1_g", "w_in", "q_norm_g", "k_norm_g", "attn_sink", "dw_w", "dw_b", "conv_ln_g",
         "conv_ln_b", "w_out", "norm2_g", "router_w", "router_b", "w_gate_up", "b_gate_up", "w_down", "b_down"]


def lay_out(inputs):
    import numpy as np

    arrays = {name: np.asarray(inputs[name]) for name in NAMES}
    for name in ("norm1_g", "dw_b", "conv_ln_g", "conv_ln_b"):
        arrays[name] = arrays[name][0].reshape(-1, P).T
    for name in ("q_norm_g", "k_norm_g"):
        arrays[name] = arrays[name][0].reshape(HEAD, 1)
    arrays["dw_w"] = arrays["dw_w"][0, :, 0, :].T
    return {"in_" + name: np.ascontiguousarray(v) for name, v in arrays.items()}


def kernel(**inputs):
    import concourse.bacc as bacc
    from concourse.bass_utils import run_bass_kernel_spmd

    nc = bacc.Bacc("TRN2", target_bir_lowering=False, num_devices=1)
    arrays = lay_out(inputs)
    aps = {name[3:]: nc.dram_tensor(name, a.shape, mybir.dt.from_np(a.dtype), kind="ExternalInput").ap()
           for name, a in arrays.items()}
    out = nc.dram_tensor("out", (1, SEQ, D), F32, kind="ExternalOutput").ap()
    build(nc, aps, out)
    result = run_bass_kernel_spmd(nc, [arrays], core_ids=[0])
    return result.results[0]["out"]
```

```python
from contextlib import ExitStack

import concourse.bass as bass
from concourse import mybir

F32 = mybir.dt.float32
F32R = mybir.dt.float32r
I32 = mybir.dt.int32
U32 = mybir.dt.uint32
ALU = mybir.AluOpType
ACT = mybir.ActivationFunctionType
AX_X = mybir.AxisListType.X
ds = bass.ds

P = 128
D = 1024
KD = D // P
SEQ = 2048
META = 16
L = META + SEQ
TILES = SEQ // P
HEAD = 64
N_Q = 8
N_KV = 2
GROUP = N_Q // N_KV
ATTN = N_Q * HEAD
KV = N_KV * HEAD
QK = ATTN + KV
CONV = D - ATTN
CC = CONV // P
IN_W = ATTN + 2 * KV + 2 * CONV
TAPS = 31
PAD = 16
BAND = 3 * P
KEYS = META + BAND
EXPERTS = 32
TOP = 4
FF = D
PASS = 384
REGION = -(-SEQ // PASS) * PASS
SLOTS = EXPERTS * REGION
ROWS = SEQ * TOP
PT = PASS // P
WIDTHS = list(range(192, PASS + 1, 16))
MAX_PASSES = (SEQ * TOP + EXPERTS * (PASS - 1)) // PASS
TABLE = 64
RMS_EPS = 1e-6
LN_EPS = 1e-5
NEG = -1e30
LIMIT = 7.0
ALPHA = 1.702
assert MAX_PASSES + 2 <= TABLE and IN_W == 1792


def wait(eng, sem, value):
    if isinstance(value, int) and value <= 0:
        return
    eng.wait_ge(sem, value)


class Chain:

    def __init__(self, eng, sem):
        self.eng, self.sem, self.base, self.n = eng, sem, 0, 0

    def begin(self, base):
        self.base, self.n = base, 0

    def after(self, ins):
        self.n += 1
        ins.then_inc(self.sem, 1)
        self.eng.wait_ge(self.sem, self.base + self.n)


def pipeline(eng, n, tasks):
    depth = 1 + max(lag for lag, task in tasks)
    lead = depth + depth % 2

    for i in range(lead):
        for lag, task in tasks:
            if i >= lag:
                task(i - lag, (i - lag) % 2, (i - lag) // 2)
    with eng.Fori(lead // 2, n // 2) as pair:
        for half in range(2):
            for lag, task in tasks:
                off = half - lag
                task(pair * 2 + off, off % 2, pair + off // 2)
    for i in range(n, n + depth - 1):
        for lag, task in tasks:
            if i - lag < n:
                task(i - lag, (i - lag) % 2, (i - lag) // 2)


class Kernel:
    pass


def build(nc, a, out, stop=None):
    k = Kernel()
    k.nc, k.a, k.out = nc, a, out
    k.hn = nc.dram_tensor("hn_rows", [SEQ, D], F32, kind="Internal").ap()
    k.h2 = nc.dram_tensor("h2_rows", [SEQ, D], F32, kind="Internal").ap()
    k.slot_list = nc.dram_tensor("slot_list", [SLOTS, 2], I32, kind="Internal").ap()
    k.y = [nc.dram_tensor(f"expert_rows{s}", [ROWS, D // 2], F32, kind="Internal").ap() for s in range(2)]
    k.table = nc.dram_tensor("pass_table", [TABLE, 4], I32, kind="Internal").ap()

    with ExitStack() as whole:
        k.ident = whole.enter_context(nc.sbuf_tensor("ident", [P, P], F32))
        k.eps = whole.enter_context(nc.sbuf_tensor("eps", [P, 2], F32))
        k.gates = whole.enter_context(nc.sbuf_tensor("gates", [P, TILES, TOP], F32))
        k.count = whole.enter_context(nc.sbuf_tensor("count", [P, EXPERTS], F32))
        k.tab = whole.enter_context(nc.sbuf_tensor("tab", [1, TABLE * 4], I32))
        with ExitStack() as front:
            def keep(name, shape, dt=F32):
                return front.enter_context(nc.sbuf_tensor(name, shape, dt))

            k.qT = keep("qT", [P, GROUP, SEQ])
            k.conv = keep("conv", [P, CC, L])
            k.taps = keep("taps", [P, CC, TAPS])
            k.tap_bias = keep("tap_bias", [P, CC])
            with ExitStack() as mixer:
                def keep2(name, shape, dt=F32):
                    return mixer.enter_context(nc.sbuf_tensor(name, shape, dt))

                k.kT = keep2("kT", [P, META + P + SEQ + P])
                k.v = keep2("v", [P, TILES + 2, KV])
                k.v_meta = keep2("v_meta", [META, KV])
                k.hc = keep2("hc", [P, CC, PAD + L + PAD])
                project(k)
                if stop == "project":
                    return k
                attend(k)
            if stop == "attend":
                return k
            k.w_out = keep("w_out", [P, KD, D])
            conv_norm(k)
            if stop == "conv_norm":
                return k
            route(k)
        if stop == "route":
            return k
        plan(k)
        experts(k)
        combine(k)
    return k


def conv_start(k, c, first, width):
    return k.nc.vector.tensor_scalar(k.conv[:, c, ds(first, width)], k.hc[:, c, ds(first + 1, width)],
                                     k.taps[:, c, 0:1], k.tap_bias[:, c:c + 1], ALU.mult, ALU.add)


def conv_add(k, c, t, first, width):
    return k.nc.vector.scalar_tensor_tensor(
        out=k.conv[:, c, ds(first, width)], in0=k.hc[:, c, ds(first + (1 + t), width)],
        scalar=k.taps[:, c, ds(t, 1)], in1=k.conv[:, c, ds(first, width)], op0=ALU.mult, op1=ALU.add)


def project(k):
    nc, a = k.nc, k.a
    PAIR = 2 * P
    ITERS = 1 + SEQ // PAIR
    with ExitStack() as ctx:
        def sb(name, shape, dt=F32):
            return ctx.enter_context(nc.sbuf_tensor("project_" + name, shape, dt))

        def sem(name):
            return ctx.enter_context(nc.semaphore("project_" + name))

        w_in = sb("w_in", [P, KD, IN_W])
        x_rows = [sb(f"x_rows{s}", [P, D]) for s in range(2)]
        xT = [sb(f"xT{s}", [P, KD, PAIR]) for s in range(2)]
        squares = sb("squares", [P, D])
        qk_rows = sb("qk_rows", [P, QK])
        sig = [sb(f"sig{s}", [P, PAIR]) for s in range(2)]
        ss = [sb(f"ss{s}", [P, 1]) for s in range(2)]
        rstd = [sb(f"rstd{s}", [P, 1]) for s in range(2)]
        root = [sb(f"root{s}", [P, 1]) for s in range(2)]
        ss_head = sb("ss_head", [P, N_Q + N_KV])
        root_head = sb("root_head", [P, N_Q + N_KV])
        rstd_head = sb("rstd_head", [P, N_Q + N_KV])
        g1 = sb("g1", [P, KD])
        qg = sb("qg", [P, 1])
        kg = sb("kg", [P, 1])
        tp = ctx.enter_context(nc.psum_tensor("project_tp", [P, 2, 512], F32))
        q_ps = ctx.enter_context(nc.psum_tensor("project_q_ps", [P, ATTN], F32))
        kv_ps = ctx.enter_context(nc.psum_tensor("project_kv_ps", [P, 512], F32))
        u_ps = ctx.enter_context(nc.psum_tensor("project_u_ps", [P, CC, 2, PAIR], F32))

        w_loaded = [sem(f"w_loaded{kk}") for kk in range(KD)]
        w_scaled = sem("w_scaled")
        small_loaded = sem("small_loaded")
        taps_loaded = sem("taps_loaded")
        x_loaded = [sem(f"x_loaded{s}") for s in range(2)]
        eps_ready = sem("eps_ready")
        ident_zeroed = sem("ident_zeroed")
        ident_ready = sem("ident_ready")
        pads_ready = sem("pads_ready")
        ss_ready = sem("ss_ready")
        xn_ready = sem("xn_ready")
        xn_turned = sem("xn_turned")
        xT_ready = sem("xT_ready")
        qkv_ready = sem("qkv_ready")
        head_squares = sem("head_squares")
        v_copied = sem("v_copied")
        qk_ready = sem("qk_ready")
        qk_turned = sem("qk_turned")
        qk_stored = sem("qk_stored")
        u_ready = sem("u_ready")
        sig_ready = sem("sig_ready")
        glu_done = sem("glu_done")
        conv_step = sem("conv_step")
        root_ready = sem("root_ready")
        head_sums = sem("head_sums")
        head_root_ready = sem("head_root_ready")
        vec_chain = sem("vec_chain")

        x = a["x"][0]
        w_view = a["w_in"][0].rearrange("(k p) n -> p k n", p=P)
        LAST = ITERS - 1

        def run(eng, iteration):
            iteration(0, 0, META)
            with eng.Fori(0, (LAST - 2) // 2) as pair:
                for i in range(2):
                    iteration(pair * 2 + (i + 1), (i + 1) % 2, P)
            for n in (LAST - 1, LAST):
                iteration(n, n % 2, P)

        def has(n, more):
            return not isinstance(n, int) or n + more <= LAST

        with nc.Block() as block:
            @block.sync
            def _(sp):
                def load(n, s):
                    wait(sp, xn_turned, 2 * (n - 1) + (s + 1))
                    if isinstance(n, int) and n == 0:
                        sp.dma_start(x_rows[s][0:META, :], a["meta_tokens"]).then_inc(x_loaded[s], 16)
                    else:
                        sp.dma_start(x_rows[s][:, :], x[ds((n - 1) * PAIR + s * P, P), :]).then_inc(x_loaded[s], 16)

                for s in range(2):
                    load(0, s)
                for kk in range(KD):
                    sp.dma_start(w_in[:, kk, :], w_view[:, kk, :]).then_inc(w_loaded[kk], 16)
                with sp.Fori(1, ITERS) as n:
                    for s in range(2):
                        load(n, s)

            @block.gpsimd
            def _(pool):
                pool.memset(k.eps[:, 0:1], RMS_EPS).then_inc(eps_ready, 1)
                pool.memset(k.eps[:, 1:2], LN_EPS).then_inc(eps_ready, 1)
                pool.memset(k.ident[:, :], 0.0).then_inc(ident_zeroed, 1)
                pool.wait_ge(ident_zeroed, 1)
                pool.affine_select(out=k.ident[:, :], in_=k.ident[:, :], compare_op=ALU.not_equal,
                                   fill=1.0, base=0, pattern=[[-1, P]], channel_multiplier=1) \
                    .then_inc(ident_ready, 1)
                pool.memset(k.hc[:, :, 0:PAD], 0.0).then_inc(pads_ready, 1)
                pool.memset(k.hc[:, :, PAD + L:], 0.0).then_inc(pads_ready, 1)
                pool.memset(k.kT[:, :], 0.0).then_inc(pads_ready, 1)
                pool.memset(k.v[:, :, :], 0.0).then_inc(pads_ready, 1)

            @block.scalar
            def _(act):
                act.dma_start(g1[:, :], a["norm1_g"]).then_inc(small_loaded, 16)
                for g in range(N_KV):
                    half = slice(g * HEAD, (g + 1) * HEAD)
                    act.dma_start(qg[half, :], a["q_norm_g"]) \
                       .then_inc(small_loaded, 16)
                    act.dma_start(kg[half, :], a["k_norm_g"]) \
                       .then_inc(small_loaded, 16)
                act.dma_start(k.taps[:, :, :], a["dw_w"].rearrange("(c p) t -> p c t", p=P)).then_inc(taps_loaded, 16)
                act.dma_start(k.tap_bias[:, :], a["dw_b"]).then_inc(taps_loaded, 16)

                act.wait_ge(eps_ready, 2)

                def row_root(n, s, w=P):
                    act.wait_ge(x_loaded[s], 16 * (n + 1))
                    if s == 0:
                        wait(act, head_sums, 2 * (n - 2) + 1)
                    else:
                        wait(act, head_sums, 2 * (n - 2) + 2)
                    nc.scalar.activation(squares[0:w, :], x_rows[s][0:w, :], ACT.Square,
                                         accum_out=ss[s][0:w, :]).then_inc(ss_ready, 1)
                    act.wait_ge(ss_ready, 2 * n + (s + 1))
                    nc.scalar.activation(root[s][0:w, :], ss[s][0:w, :], ACT.Sqrt, scale=1.0 / D,
                                         bias=k.eps[0:w, 0:1]).then_inc(root_ready, 1)

                def copy_x(n, par, s, w):
                    act.wait_ge(xn_turned, 2 * n + (s + 1))
                    for half in range(2):
                        ins = nc.scalar.activation(xT[par][:, half * 4:half * 4 + 4, s * w:(s + 1) * w],
                                                   tp[:, half, :].rearrange("p (k t) -> p k t", t=P)[:, :, 0:w],
                                                   ACT.Copy)
                    ins.then_inc(xT_ready, 1)

                def iteration(n, par, w):
                    cols = META if w == META else PAIR

                    def head_root(s):
                        act.wait_ge(head_sums, 2 * n + (s + 1))
                        nc.scalar.activation(root_head[0:w, :], ss_head[0:w, :], ACT.Sqrt, scale=1.0 / HEAD,
                                             bias=k.eps[0:w, 0:1]).then_inc(head_root_ready, 1)

                    def heads(s):
                        act.wait_ge(qkv_ready, 2 * n + (s + 1))
                        wait(act, head_sums, 2 * n + s)
                        nc.scalar.activation(squares[0:w, 0:ATTN], q_ps[0:w, :], ACT.Square).then_inc(head_squares, 1)
                        nc.scalar.activation(squares[0:w, ATTN:QK], kv_ps[0:w, 0:KV], ACT.Square) \
                          .then_inc(head_squares, 1)
                        if w == META:
                            wait(act, v_copied, s)
                            v_to = k.v_meta[:, :]
                        else:
                            v_to = k.v[:, ds((n - 1) * 2 + (s + 1), 1), :].rearrange("p one c -> p (one c)")
                        nc.scalar.activation(v_to, kv_ps[0:w, KV:2 * KV], ACT.Copy).then_inc(v_copied, 1)

                    def store_qk(s):
                        act.wait_ge(qk_turned, 2 * n + (s + 1))
                        if w == META:
                            wait(act, qk_stored, s)
                            q_at, k_at = ds(0, w), ds(0, w)
                        else:
                            q_at, k_at = ds((n - 1) * PAIR + s * P, w), ds((n - 1) * PAIR + (s * P + META + P), w)
                        if w != META:
                            nc.scalar.activation(k.qT[:, :, q_at],
                                                 tp[:, 0, :].rearrange("p (i t) -> p i t", t=P)[:, :, 0:w],
                                                 ACT.Copy, scale=qg[:, 0:1])
                        nc.scalar.activation(k.kT[:, k_at], tp[:, 1, 0:w], ACT.Copy, scale=kg[:, 0:1]) \
                          .then_inc(qk_stored, 1)

                    def gate(c):
                        act.wait_ge(u_ready, CC * n + (c + 1))
                        wait(act, glu_done, CC * n + (c - 1))
                        nc.scalar.activation(sig[c % 2][:, 0:cols], u_ps[:, c, 1, 0:cols], ACT.Sigmoid) \
                          .then_inc(sig_ready, 1)

                    if has(n, 1):
                        row_root(n + 1, 1)
                    heads(0)
                    if has(n, 1):
                        copy_x(n + 1, 1 - par, 0, P)
                    head_root(0)
                    if has(n, 2):
                        row_root(n + 2, 0)
                    heads(1)
                    store_qk(0)
                    head_root(1)
                    gate(0)
                    gate(1)
                    if has(n, 1):
                        copy_x(n + 1, 1 - par, 1, P)
                    gate(2)
                    store_qk(1)
                    gate(3)

                row_root(0, 0, META)
                row_root(0, 1, META)
                copy_x(0, 0, 0, META)
                copy_x(0, 0, 1, META)
                row_root(1, 0)
                act.wait_ge(small_loaded, 16 * 5)
                act.wait_ge(pads_ready, 4)
                run(act, iteration)

            @block.tensor
            def _(pe):
                pe.wait_ge(ident_ready, 1)

                def turn_x(n, s, w):
                    pe.wait_ge(xn_ready, 2 * n + (s + 1))
                    wait(pe, qk_stored, 2 * (n - 1) + s)
                    if isinstance(n, int) and n == 0:
                        wait(pe, xT_ready, s)
                    for kk in range(KD):
                        mm = nc.tensor.transpose(tp[:, kk // 4, (kk % 4) * P:(kk % 4) * P + w],
                                                 x_rows[s][0:w, kk * P:(kk + 1) * P], k.ident[0:w, 0:w])
                    mm.then_inc(xn_turned, 1)

                def iteration(n, par, w):
                    cols = META if w == META else PAIR

                    def qkv(s):
                        pe.wait_ge(xT_ready, 2 * n + (s + 1))
                        wait(pe, qk_ready, 2 * n + s)
                        wait(pe, v_copied, 2 * n + s)
                        for kk in range(KD):
                            if w == META and s == 0:
                                pe.wait_ge(w_scaled, kk + 1)
                            nc.tensor.matmul(q_ps[0:w, :], xT[par][:, kk, s * w:(s + 1) * w], w_in[:, kk, 0:ATTN],
                                             start=kk == 0, stop=kk == KD - 1)
                        for kk in range(KD):
                            mm = nc.tensor.matmul(kv_ps[0:w, 0:2 * KV], xT[par][:, kk, s * w:(s + 1) * w],
                                                  w_in[:, kk, ATTN:ATTN + 2 * KV], start=kk == 0, stop=kk == KD - 1)
                        mm.then_inc(qkv_ready, 1)

                    def u(c):
                        pe.wait_ge(xT_ready, 2 * n + 2)
                        wait(pe, glu_done, CC * (n - 1) + (c + 1))
                        for half in range(2):
                            first = ATTN + 2 * KV + half * CONV + c * P
                            for kk in range(KD):
                                mm = nc.tensor.matmul(u_ps[:, c, half, 0:cols], w_in[:, kk, first:first + P],
                                                      xT[par][:, kk, 0:cols], start=kk == 0, stop=kk == KD - 1)
                        mm.then_inc(u_ready, 1)

                    def turn_qk(s):
                        pe.wait_ge(qk_ready, 2 * n + (s + 1))
                        if has(n, 1):
                            pe.wait_ge(xT_ready, 2 * n + (s + 3))
                        else:
                            pe.wait_ge(qk_stored, 2 * n + s)
                        for i in range(GROUP):
                            nc.tensor.transpose(tp[:, 0, i * P:i * P + w], qk_rows[0:w, i * P:(i + 1) * P],
                                                k.ident[0:w, 0:w])
                        nc.tensor.transpose(tp[:, 1, 0:w], qk_rows[0:w, ATTN:QK], k.ident[0:w, 0:w]) \
                          .then_inc(qk_turned, 1)

                    qkv(0)
                    if has(n, 1):
                        turn_x(n + 1, 0, P)
                    u(0)
                    qkv(1)
                    turn_qk(0)
                    u(1)
                    if has(n, 1):
                        turn_x(n + 1, 1, P)
                    u(2)
                    turn_qk(1)
                    u(3)

                turn_x(0, 0, META)
                turn_x(0, 1, META)
                run(pe, iteration)

            @block.vector
            def _(dve):
                chain = Chain(dve, vec_chain)

                def scale_rows(n, s, w=P):
                    dve.wait_ge(root_ready, 2 * n + (s + 1))
                    chain.after(nc.vector.reciprocal(rstd[s][0:w, :], root[s][0:w, :]))
                    nc.vector.tensor_scalar(x_rows[s][0:w, :], x_rows[s][0:w, :], rstd[s][0:w, 0:1], None,
                                            ALU.mult).then_inc(xn_ready, 1)

                def iteration(n, par, w):
                    cols = META if w == META else PAIR
                    steps = [(t, c) for t in range(TAPS) for c in range(CC)]
                    if isinstance(n, int) and n < 2:
                        steps = []

                    def convolve(count):
                        for t, c in steps[:count]:
                            if t == 0:
                                ins = conv_start(k, c, (n - 2) * PAIR, PAIR)
                            else:
                                dve.wait_ge(conv_step, (n - 2) * (CC * TAPS) + (CC * (t - 1) + c + 1))
                                ins = conv_add(k, c, t, (n - 2) * PAIR, PAIR)
                            ins.then_inc(conv_step, 1)
                        del steps[:count]

                    def norm_heads(s):
                        dve.wait_ge(head_squares, 4 * n + 2 * (s + 1))
                        nc.vector.tensor_reduce(
                            ss_head[0:w, :], squares[0:w, 0:QK].rearrange("p (h d) -> p h d", d=HEAD), AX_X,
                            ALU.add).then_inc(head_sums, 1)
                        convolve(4)
                        dve.wait_ge(head_root_ready, 2 * n + (s + 1))
                        chain.after(nc.vector.reciprocal(rstd_head[0:w, :], root_head[0:w, :]))
                        wait(dve, qk_turned, 2 * n + s)
                        nc.vector.tensor_tensor(
                            qk_rows[0:w, 0:ATTN].rearrange("p (i g d) -> p g i d", g=N_KV, d=HEAD),
                            q_ps[0:w, :].rearrange("p (g i d) -> p g i d", g=N_KV, d=HEAD),
                            rstd_head[0:w, 0:N_Q].rearrange("p (g i) -> p g i", g=N_KV).unsqueeze(3)
                            .to_broadcast([w, N_KV, GROUP, HEAD]), ALU.mult)
                        nc.vector.tensor_tensor(
                            qk_rows[0:w, ATTN:QK].rearrange("p (g d) -> p g d", d=HEAD),
                            kv_ps[0:w, 0:KV].rearrange("p (g d) -> p g d", d=HEAD),
                            rstd_head[0:w, N_Q:].unsqueeze(2).to_broadcast([w, N_KV, HEAD]), ALU.mult) \
                          .then_inc(qk_ready, 1)

                    def glu(c):
                        dve.wait_ge(sig_ready, CC * n + (c + 1))
                        at = ds(PAD, cols) if w == META else ds((n - 1) * PAIR + (PAD + META), cols)
                        nc.vector.tensor_tensor(k.hc[:, c, at], u_ps[:, c, 0, 0:cols], sig[c % 2][:, 0:cols],
                                                ALU.mult).then_inc(glu_done, 1)

                    if steps:
                        dve.wait_ge(glu_done, CC * n)
                    convolve(8)
                    if has(n, 1):
                        scale_rows(n + 1, 1)
                    convolve(20)
                    norm_heads(0)
                    convolve(12)
                    if has(n, 2):
                        scale_rows(n + 2, 0)
                    convolve(28)
                    norm_heads(1)
                    convolve(8)
                    glu(0)
                    glu(1)
                    convolve(20)
                    glu(2)
                    convolve(20)
                    glu(3)
                    assert not steps

                scale_rows(0, 0, META)
                scale_rows(0, 1, META)
                dve.wait_ge(small_loaded, 16 * 5)
                for kk in range(KD):
                    if kk == KD // 2:
                        scale_rows(1, 0)
                    dve.wait_ge(w_loaded[kk], 16)
                    nc.vector.tensor_scalar(w_in[:, kk, :], w_in[:, kk, :], g1[:, kk:kk + 1], None, ALU.mult) \
                      .then_inc(w_scaled, 1)
                dve.wait_ge(taps_loaded, 32)
                dve.wait_ge(pads_ready, 4)
                LOOPED = (LAST - 3) // 2
                counts = [chain.n]
                iteration(0, 0, META)
                counts.append(chain.n)
                iteration(1, 1, P)
                per = chain.n - counts[1]
                start = chain.n
                with dve.Fori(0, LOOPED) as pair:
                    for i in range(2):
                        chain.begin((pair * 2 + i) * per + start)
                        iteration(pair * 2 + (i + 2), i, P)
                        assert chain.n == per
                chain.begin(2 * LOOPED * per + start)
                for n in range(2 + 2 * LOOPED, ITERS):
                    iteration(n, n % 2, P)


def attend(k):
    nc, a = k.nc, k.a
    with ExitStack() as ctx:
        def sb(name, shape, dt=F32):
            return ctx.enter_context(nc.sbuf_tensor("attend_" + name, shape, dt))

        def sem(name):
            return ctx.enter_context(nc.semaphore("attend_" + name))

        empty = sb("empty", [P, SLOTS // P, 2], I32)
        dist_i = sb("dist_i", [P, KEYS], I32)
        dist = sb("dist", [P, KEYS])
        far = sb("far", [P, KEYS])
        bias = sb("bias", [P, N_Q, KEYS])
        sink = sb("sink", [P, N_Q])
        scores = [sb(f"scores{s}", [P, GROUP, KEYS]) for s in range(2)]
        probs = [sb(f"probs{s}", [P, GROUP, KEYS]) for s in range(2)]
        top = [sb(f"top{s}", [P, GROUP]) for s in range(2)]
        neg_top = [sb(f"neg_top{s}", [P, GROUP]) for s in range(2)]
        sink_gap = [sb(f"sink_gap{s}", [P, GROUP]) for s in range(2)]
        sink_exp = [sb(f"sink_exp{s}", [P, GROUP]) for s in range(2)]
        total = [sb(f"total{s}", [P, GROUP]) for s in range(2)]
        inverse = [sb(f"inverse{s}", [P, GROUP]) for s in range(2)]
        pT = [sb(f"pT{s}", [P, 4, GROUP * P]) for s in range(2)]
        q_block = sb("q_block", [P, GROUP, P])
        k_band = sb("k_band", [P, KEYS])
        v_band = sb("v_band", [P, 3, KV])
        s_ps = ctx.enter_context(nc.psum_tensor("attend_s_ps", [P, GROUP, 512], F32))
        pt_ps = ctx.enter_context(nc.psum_tensor("attend_pt_ps", [P, 2, 512], F32))
        o_ps = ctx.enter_context(nc.psum_tensor("attend_o_ps", [P, 2, GROUP * P], F32))

        empty_made = sem("empty_made")
        empty_stored = sem("empty_stored")
        dist_made = sem("dist_made")
        sink_loaded = sem("sink_loaded")
        q_staged = sem("q_staged")
        v_staged = sem("v_staged")
        meta_staged = sem("meta_staged")
        scores_ready = sem("scores_ready")
        scores_taken = sem("scores_taken")
        top_ready = sem("top_ready")
        top_step = sem("top_step")
        inverse_ready = sem("inverse_ready")
        exp_done = sem("exp_done")
        probs_ready = sem("probs_ready")
        probs_turned = sem("probs_turned")
        pT_ready = sem("pT_ready")
        o_ready = sem("o_ready")
        o_stored = sem("o_stored")
        bias_chain = sem("bias_chain")
        conv_step = sem("conv_step")
        PAIR = 2 * P

        BLOCKS = TILES

        def run(eng, body, peeled=0):
            body(0)
            body(1)
            with eng.Fori(2, BLOCKS - peeled) as b:
                body(b)
            for b in range(BLOCKS - peeled, BLOCKS + 2):
                body(b)

        def has(b):
            return not isinstance(b, int) or 0 <= b < BLOCKS

        def back(b, n):
            if isinstance(b, int):
                return b - n if 0 <= b - n < BLOCKS else None
            return b - n

        with nc.Block() as block:
            @block.sync
            def _(sp):
                sp.wait_ge(empty_made, 2)
                sp.dma_start(k.slot_list.rearrange("(p n) two -> p (n two)", p=P),
                             empty[:, :, :].rearrange("p n two -> p (n two)")).then_inc(empty_stored, 16)
                sp.wait_ge(empty_stored, 16)

            @block.gpsimd
            def _(pool):
                pool.memset(dist_i[:, 0:META], 0).then_inc(dist_made, 1)
                pool.iota(dist_i[:, META:], pattern=[[1, BAND]], base=-P, channel_multiplier=-1) \
                    .then_inc(dist_made, 1)

                def stage(b):
                    wait(pool, scores_ready, 2 * b)
                    pool.tensor_copy(q_block[:, :, :], k.qT[:, :, ds(b * P, P)]).then_inc(q_staged, 1)
                    pool.tensor_copy(k_band[:, META:], k.kT[:, ds(b * P + META, BAND)]).then_inc(q_staged, 1)

                def stage_v(b):
                    wait(pool, o_ready, 2 * b)
                    pool.tensor_copy(v_band[:, :, :], k.v[:, ds(b, 3), :]).then_inc(v_staged, 1)

                pool.tensor_copy(k_band[:, 0:META], k.kT[:, 0:META]).then_inc(meta_staged, 1)
                stage(0)
                stage_v(0)
                pool.memset(empty[:, :, 0:1], 0).then_inc(empty_made, 1)
                pool.memset(empty[:, :, 1:2], ROWS).then_inc(empty_made, 1)
                stage(1)
                with pool.Fori(2, BLOCKS) as b:
                    stage(b)
                    stage_v(b - 1)
                stage_v(BLOCKS - 1)

            @block.tensor
            def _(pe):
                def score(b, g, heads):
                    half = slice(g * HEAD, (g + 1) * HEAD)
                    if heads[0] == 0:
                        pe.wait_ge(q_staged, 2 * b + 2)
                        wait(pe, scores_taken, 2 * b + g)
                    for i in heads:
                        mm = nc.tensor.matmul(s_ps[:, i, 0:KEYS], q_block[half, i, :], k_band[half, :],
                                              start=True, stop=True)
                    if heads[-1] == GROUP - 1:
                        mm.then_inc(scores_ready, 1)

                def turn(b, g, j):
                    first = b * 8 + g * 4
                    pe.wait_ge(probs_ready, b * 2 + (g + 1))
                    wait(pe, pT_ready, first + (j - 1))
                    rows, at = (P, slice(META + j * P, META + (j + 1) * P)) if j < 3 else (META, slice(0, META))
                    for i in range(GROUP):
                        mm = nc.tensor.transpose(pt_ps[0:rows, j % 2, i * P:(i + 1) * P], probs[g][:, i, at],
                                                 k.ident[:, :])
                    mm.then_inc(probs_turned, 1)

                def value(b, g, j):
                    first = b * 8 + g * 4
                    if j == 0:
                        pe.wait_ge(v_staged, b + 1)
                        wait(pe, o_stored, b * 2 + (g - 1))
                    pe.wait_ge(pT_ready, first + (j + 1))
                    if j < 3:
                        nc.tensor.matmul(o_ps[:, g, :], v_band[:, j, :], pT[g][:, j, :], start=j == 0, stop=False)
                    else:
                        nc.tensor.matmul(o_ps[:, g, :], k.v_meta[:, :], pT[g][0:META, j, :], start=False, stop=True) \
                          .then_inc(o_ready, 1)

                def body(b):
                    for g in range(2):
                        weighed = back(b, 1)
                        if has(b):
                            score(b, g, range(0, GROUP // 2))
                        if weighed is not None:
                            turn(weighed, g, 0)
                            turn(weighed, g, 1)
                        if has(b):
                            score(b, g, range(GROUP // 2, GROUP))
                        if weighed is not None:
                            for j in range(4):
                                value(weighed, g, j)
                                if j < 2:
                                    turn(weighed, g, j + 2)

                pe.wait_ge(meta_staged, 1)
                run(pe, body)

            @block.scalar
            def _(act):
                act.dma_start(sink[:, :], a["attn_sink"][0:1, :].to_broadcast([P, N_Q])).then_inc(sink_loaded, 16)

                def exps(b, g):
                    act.wait_ge(top_ready, 4 * b + (2 * g + 2))
                    wait(act, probs_turned, b * 8 + (g - 1) * 4)
                    for i in range(GROUP):
                        nc.scalar.activation(probs[g][:, i, :], scores[g][:, i, :], ACT.Exp,
                                             bias=neg_top[g][:, i:i + 1],
                                             accum_out=total[g][:, i:i + 1])
                    nc.scalar.activation(sink_exp[g][:, :], sink_gap[g][:, :], ACT.Exp).then_inc(exp_done, 1)

                def copies(b, g):
                    for j in range(4):
                        rows = P if j < 3 else META
                        act.wait_ge(probs_turned, b * 8 + (g * 4 + j + 1))
                        nc.scalar.activation(pT[g][0:rows, j, :], pt_ps[0:rows, j % 2, :], ACT.Copy).then_inc(pT_ready, 1)

                def store(b, g):
                    half = slice(g * HEAD, (g + 1) * HEAD)
                    act.wait_ge(o_ready, b * 2 + (g + 1))
                    nc.scalar.activation(k.qT[half, :, ds(b * P, P)],
                                         o_ps[half, g, :].rearrange("p (i t) -> p i t", t=P), ACT.Copy) \
                      .then_inc(o_stored, 1)

                def body(b):
                    for g in range(2):
                        exp_b = back(b, 1) if g == 0 else (b if has(b) else None)
                        stored = back(b, 2) if g == 0 else back(b, 1)
                        if exp_b is not None:
                            exps(exp_b, 1 - g)
                        if stored is not None:
                            store(stored, 1 - g)
                        if back(b, 1) is not None:
                            copies(back(b, 1), g)

                run(act, body)

            @block.vector
            def _(dve):
                setup = Chain(dve, bias_chain)
                dve.wait_ge(dist_made, 2)
                setup.after(nc.vector.tensor_copy(dist[:, :], dist_i[:, :]))
                setup.after(nc.vector.tensor_scalar(far[:, :], dist[:, :], -1.0, None, ALU.mult))
                setup.after(nc.vector.tensor_tensor(dist[:, :], dist[:, :], far[:, :], ALU.max))
                setup.after(nc.vector.tensor_scalar(far[:, :], dist[:, :], float(P), NEG, ALU.is_gt, ALU.mult))
                for h in range(N_Q):
                    slope = 2.0 ** (-8.0 * (h + 1) / N_Q)
                    ins = nc.vector.scalar_tensor_tensor(out=bias[:, h, :], in0=dist[:, :], scalar=-slope,
                                                         in1=far[:, :], op0=ALU.mult, op1=ALU.add)
                setup.after(ins)
                dve.wait_ge(sink_loaded, 16)

                def soft(b, g):
                    heads = slice(g * GROUP, (g + 1) * GROUP)
                    u = 2 * b + g
                    dve.wait_ge(scores_ready, u + 1)
                    wait(dve, exp_done, u - 1)
                    nc.vector.scalar_tensor_tensor(
                        out=scores[g][:, :, :], in0=s_ps[:, :, 0:KEYS], scalar=HEAD ** -0.5,
                        in1=bias[:, heads, :], op0=ALU.mult, op1=ALU.add).then_inc(scores_taken, 1)
                    dve.wait_ge(scores_taken, u + 1)
                    if isinstance(b, int) and b in (0, BLOCKS - 1):
                        cut = META if b == 0 else META + 2 * P
                        setup.after(nc.vector.memset(scores[g][:, :, cut:cut + P], NEG))
                    nc.vector.tensor_reduce(top[g][:, :], scores[g][:, :, :], AX_X, ALU.max).then_inc(top_step, 1)
                    dve.wait_ge(top_step, 2 * u + 1)
                    nc.vector.tensor_tensor(top[g][:, :], top[g][:, :], sink[:, heads], ALU.max).then_inc(top_step, 1)
                    dve.wait_ge(top_step, 2 * u + 2)
                    nc.vector.tensor_scalar(neg_top[g][:, :], top[g][:, :], -1.0, None, ALU.mult) \
                      .then_inc(top_ready, 1)
                    nc.vector.tensor_tensor(sink_gap[g][:, :], sink[:, heads], top[g][:, :],
                                            ALU.subtract).then_inc(top_ready, 1)

                def invert(b, g):
                    u = 2 * b + g
                    dve.wait_ge(exp_done, u + 1)
                    nc.vector.tensor_tensor(total[g][:, :], total[g][:, :], sink_exp[g][:, :], ALU.add) \
                      .then_inc(inverse_ready, 1)
                    dve.wait_ge(inverse_ready, 2 * u + 1)
                    nc.vector.reciprocal(inverse[g][:, :], total[g][:, :]).then_inc(inverse_ready, 1)

                def norm(b, g):
                    dve.wait_ge(inverse_ready, 4 * b + (2 * g + 2))
                    for i in range(GROUP):
                        ins = nc.vector.tensor_scalar(probs[g][:, i, :], probs[g][:, i, :], inverse[g][:, i:i + 1],
                                                      None, ALU.mult)
                    ins.then_inc(probs_ready, 1)

                def convolve(b, g):
                    first, width = SEQ - PAIR, PAIR + META
                    if isinstance(b, int) and (b, g) == (0, 0):
                        for c in range(CC):
                            conv_start(k, c, first, width).then_inc(conv_step, 1)
                    for c in range(CC):
                        dve.wait_ge(conv_step, (2 * b + g) * CC + (c + 1))
                        conv_add(k, c, 2 * b + (g + 1), first, width).then_inc(conv_step, 1)

                def body(b):
                    for g in range(2):
                        if back(b, 1) is not None:
                            invert(back(b, 1), g)
                            norm(back(b, 1), g)
                        if has(b):
                            soft(b, g)
                        if not isinstance(b, int) or 2 * b + g + 1 < TAPS:
                            convolve(b, g)

                run(dve, body, peeled=1)


def conv_norm(k):
    nc, a = k.nc, k.a
    SPAN = 512
    with ExitStack() as ctx:
        def sb(name, shape, dt=F32):
            return ctx.enter_context(nc.sbuf_tensor("conv_norm_" + name, shape, dt))

        def sem(name):
            return ctx.enter_context(nc.semaphore("conv_norm_" + name))

        ones = sb("ones", [P, P])
        gain = sb("gain", [P, CC])
        shift = sb("shift", [P, CC])
        side = [sb(f"side{s}", [P, CC, SPAN]) for s in range(3)]
        inv = [sb(f"inv{s}", [P, SPAN]) for s in range(2)]
        root = [sb(f"root{s}", [P, SPAN]) for s in range(2)]
        mean_ps = ctx.enter_context(nc.psum_tensor("conv_norm_mean_ps", [P, 2, SPAN], F32))
        var_ps = ctx.enter_context(nc.psum_tensor("conv_norm_var_ps", [P, 2, SPAN], F32))
        ones_ready = sem("ones_ready")
        small_loaded = sem("small_loaded")
        w_loaded = sem("w_loaded")
        shifted = sem("shifted")
        mean_ready = sem("mean_ready")
        centred = sem("centred")
        squared = sem("squared")
        var_ready = sem("var_ready")
        scaled = sem("scaled")
        sigmoid_ready = sem("sigmoid_ready")
        swished = sem("swished")
        root_ready = sem("root_ready")
        vec_chain = sem("vec_chain")

        def z(i, c=None):
            at = ds(META + i * SPAN, SPAN)
            return k.conv[:, :, at] if c is None else k.conv[:, c, at]

        w_attn = a["w_out"][0, 0:ATTN].rearrange("(g i d) n -> g d i n", g=N_KV, d=HEAD)
        w_conv = a["w_out"][0, ATTN:].rearrange("(c p) n -> p c n", p=P)
        spans = SEQ // SPAN
        with nc.Block() as block:
            @block.sync
            def _(sp):
                for g in range(N_KV):
                    sp.dma_start(k.w_out[g * HEAD:(g + 1) * HEAD, 0:GROUP, :], w_attn[g]).then_inc(w_loaded, 16)
                sp.dma_start(k.w_out[:, GROUP:, :], w_conv).then_inc(w_loaded, 16)
                sp.wait_ge(w_loaded, 48)

            @block.gpsimd
            def _(pool):
                pool.memset(ones[:, :], 1.0 / CONV).then_inc(ones_ready, 1)
                pool.wait_ge(small_loaded, 32)
                for i in range(spans):
                    pool.wait_ge(sigmoid_ready, CC * (i + 1))
                    for c in range(CC):
                        ins = pool.tensor_scalar(z(i, c), z(i, c), gain[:, c:c + 1], shift[:, c:c + 1],
                                                 ALU.mult, ALU.add)
                    ins.then_inc(shifted, 1)

            @block.tensor
            def _(pe):
                pe.wait_ge(ones_ready, 1)

                def mean(i, par, m):
                    for c in range(CC):
                        mm = nc.tensor.matmul(mean_ps[:, par, :], ones[:, :], z(i, c), start=c == 0, stop=c == CC - 1)
                    mm.then_inc(mean_ready, 1)

                def variance(i, par, m):
                    pe.wait_ge(squared, i + 1)
                    for c in range(CC):
                        mm = nc.tensor.matmul(var_ps[:, par, :], ones[:, :], side[i % 3][:, c, :],
                                              start=c == 0, stop=c == CC - 1)
                    mm.then_inc(var_ready, 1)

                for i in range(spans):
                    if i < 2:
                        mean(i, i % 2, i // 2)
                for i in range(spans):
                    variance(i, i % 2, i // 2)
                    if i + 2 < spans:
                        pe.wait_ge(centred, i + 1)
                        mean(i + 2, i % 2, i // 2)

            @block.scalar
            def _(act):
                act.dma_start(gain[:, :], a["conv_ln_g"]).then_inc(small_loaded, 16)
                act.dma_start(shift[:, :], a["conv_ln_b"]).then_inc(small_loaded, 16)
                act.wait_ge(small_loaded, 32)

                def square(i):
                    act.wait_ge(centred, i + 1)
                    wait(act, swished, i - 2)
                    nc.scalar.activation(side[i % 3][:, :, :], z(i), ACT.Square).then_inc(squared, 1)

                def sigmoid(i):
                    act.wait_ge(scaled, i + 1)
                    for c in range(CC):
                        nc.scalar.activation(side[i % 3][:, c, :], z(i, c), ACT.Sigmoid, scale=gain[:, c:c + 1],
                                             bias=shift[:, c:c + 1]).then_inc(sigmoid_ready, 1)

                def deviation(i):
                    act.wait_ge(var_ready, i + 1)
                    wait(act, scaled, i - 1)
                    nc.scalar.activation(root[i % 2][:, :], var_ps[:, i % 2, :], ACT.Sqrt, bias=k.eps[:, 1:2]) \
                      .then_inc(root_ready, 1)

                square(0)
                for i in range(spans):
                    if i + 1 < spans:
                        square(i + 1)
                    deviation(i)
                    sigmoid(i)

            @block.vector
            def _(dve):
                chain = Chain(dve, vec_chain)
                dve.wait_ge(small_loaded, 32)

                def centre(i):
                    dve.wait_ge(mean_ready, i + 1)
                    nc.vector.tensor_tensor(z(i), z(i), mean_ps[:, i % 2, :].unsqueeze(1).to_broadcast([P, CC, SPAN]),
                                            ALU.subtract).then_inc(centred, 1)

                def scale(i):
                    dve.wait_ge(root_ready, i + 1)
                    chain.after(nc.vector.reciprocal(inv[i % 2][:, :], root[i % 2][:, :]))
                    nc.vector.tensor_tensor(z(i), z(i), inv[i % 2][:, :].unsqueeze(1).to_broadcast([P, CC, SPAN]),
                                            ALU.mult).then_inc(scaled, 1)

                def swish(i):
                    dve.wait_ge(shifted, i + 1)
                    nc.vector.tensor_tensor(z(i), z(i), side[i % 3][:, :, :], ALU.mult).then_inc(swished, 1)

                centre(0)
                for i in range(spans):
                    if i + 1 < spans:
                        centre(i + 1)
                    scale(i)
                    if i >= 1:
                        swish(i - 1)
                swish(spans - 1)


def route(k):
    nc, a = k.nc, k.a
    with ExitStack() as ctx:
        def sb(name, shape, dt=F32):
            return ctx.enter_context(nc.sbuf_tensor("route_" + name, shape, dt))

        def two(name, shape, dt=F32):
            return [sb(f"{name}{s}", shape, dt) for s in range(2)]

        def sem(name):
            return ctx.enter_context(nc.semaphore("route_" + name))

        def sem2(name):
            return [sem(f"{name}{s}") for s in range(2)]

        w_out = k.w_out
        g2 = sb("g2", [P, D])
        rw = sb("rw", [P, KD, EXPERTS])
        rb = sb("rb", [P, EXPERTS])
        b_down = sb("b_down", [EXPERTS, D])
        before = sb("before", [P, P])
        ones = sb("ones", [P, P])
        col_i = sb("col_i", [P, EXPERTS], I32)
        col = sb("col", [P, EXPERTS])
        token_i = sb("token_i", [P, 1], I32)
        token = sb("token", [P, 1])
        x_t = two("x_t", [P, D])
        mixed = two("mixed", [P, KD, P])
        h2 = two("h2", [P, D])
        hn = two("hn", [P, D])
        h2b = two("h2b", [P, D])
        squares = sb("squares", [P, D])
        ss = two("ss", [P, 1])
        root = two("root", [P, 1])
        rstd = two("rstd", [P, 1])
        hnT = sb("hnT", [P, KD, P])
        logits = sb("logits", [P, EXPERTS])
        best = two("best", [P, 8])
        best_i = sb("best_i", [P, 8], U32)
        pick = two("pick", [P, TOP])
        neg_best = sb("neg_best", [P, 1])
        powers = two("powers", [P, TOP])
        power_sum = two("power_sum", [P, 1])
        inverse = sb("inverse", [P, 1])
        mask = two("mask", [P, TOP, EXPERTS])
        weighted = sb("weighted", [P, TOP, EXPERTS])
        chosen = two("chosen", [P, EXPERTS])
        gate = two("gate", [P, EXPERTS])
        gateT = sb("gateT", [EXPERTS, P])
        rank_all = sb("rank_all", [P, EXPERTS])
        rank_pick = sb("rank_pick", [P, TOP, EXPERTS])
        rank = sb("rank", [P, TOP])
        place = sb("place", [P, TOP])
        place_i = two("place_i", [P, TOP], U32)
        tile_entry = two("tile_entry", [P, TOP, 2], I32)
        choice_i = sb("choice_i", [P, TOP], I32)
        choice = sb("choice", [P, TOP])
        row = sb("row", [P, TOP])
        op_ps = ctx.enter_context(nc.psum_tensor("route_op_ps", [P, D], F32))
        tp_ps = ctx.enter_context(nc.psum_tensor("route_tp_ps", [P, KD, P], F32))
        gb_ps = ctx.enter_context(nc.psum_tensor("route_gb_ps", [P, D], F32))
        lg_ps = ctx.enter_context(nc.psum_tensor("route_lg_ps", [P, 512], F32))
        rk_ps = ctx.enter_context(nc.psum_tensor("route_rk_ps", [P, 512], F32))

        small_loaded = sem("small_loaded")
        made = sem("made")
        staged = sem("staged")
        max_begun = sem("max_begun")
        scatter_begun = sem("scatter_begun")
        made_masks = sem("made_masks")
        x_loaded = sem2("x_loaded")
        proj_ready = sem("proj_ready")
        h2_ready = sem("h2_ready")
        ss_ready = sem("ss_ready")
        hn_ready = sem("hn_ready")
        hn_stored = sem2("hn_stored")
        hn_turned = sem("hn_turned")
        hnT_ready = sem("hnT_ready")
        router_ready = sem("router_ready")
        logits_taken = sem("logits_taken")
        best_ready = sem("best_ready")
        powers_ready = sem("powers_ready")
        picked = sem("picked")
        rank_ready = sem("rank_ready")
        rank_taken = sem("rank_taken")
        gateT_ready = sem("gateT_ready")
        bias_ready = sem("bias_ready")
        h2b_ready = sem("h2b_ready")
        h2b_stored = sem2("h2b_stored")
        placed = sem("placed")
        scattered = sem2("scattered")
        vec_setup = sem("vec_setup")
        root_ready = sem("root_ready")
        chain0, chain1, chain2 = sem("vec_chain_norm"), sem("vec_chain_pick"), sem("vec_chain_place")

        x = a["x"][0]
        with nc.Block() as block:
            @block.sync
            def _(sp):
                def load(t, par, m):
                    wait(sp, h2_ready, t - 1)
                    sp.dma_start(x_t[par][:, :], x[ds(t * P, P), :]).then_inc(x_loaded[par], 16)

                def store_hn(t, par, m):
                    sp.wait_ge(hn_ready, t + 1)
                    sp.dma_start(k.hn[ds(t * P, P), :], hn[par][:, :]).then_inc(hn_stored[par], 16)

                def store_h2(t, par, m):
                    sp.wait_ge(h2b_ready, t + 1)
                    sp.dma_start(k.h2[ds(t * P, P), :], h2b[par][:, :]).then_inc(h2b_stored[par], 16)

                pipeline(sp, TILES, [(3, store_h2), (1, store_hn), (0, load)])
                for s in range(2):
                    sp.wait_ge(hn_stored[s], 16 * (TILES // 2))
                    sp.wait_ge(h2b_stored[s], 16 * (TILES // 2))

            @block.gpsimd
            def _(pool):
                pool.memset(ones[:, :], 1.0).then_inc(made, 1)
                pool.iota(col_i[:, :], pattern=[[1, EXPERTS]], base=0, channel_multiplier=0).then_inc(made, 1)
                pool.iota(token_i[:, :], pattern=[[0, 1]], base=0, channel_multiplier=1).then_inc(made, 1)
                pool.iota(choice_i[:, :], pattern=[[1, TOP]], base=0, channel_multiplier=0).then_inc(made, 1)
                pool.wait_ge(made, 4)
                pool.affine_select(out=before[:, :], in_=ones[:, :], compare_op=ALU.is_gt, fill=0.0, base=0,
                                   pattern=[[1, P]], channel_multiplier=-1).then_inc(made_masks, 1)

                def stage(t, par, m):
                    wait(pool, proj_ready, t - 1)
                    pool.tensor_copy(mixed[par][:, 0:GROUP, :], k.qT[:, :, ds(t * P, P)]).then_inc(staged, 1)
                    pool.tensor_copy(mixed[par][:, GROUP:, :], k.conv[:, :, ds(t * P + META, P)]).then_inc(staged, 1)

                def scatter(t, par, m):
                    pool.wait_ge(placed, t + 1)
                    pool.sem_inc(scatter_begun, 1)
                    for j in range(TOP):
                        pool.indirect_dma_start(
                            k.slot_list, bass.IndirectOffsetOnAxis(ap=place_i[par][:, j:j + 1], axis=0),
                            tile_entry[par][:, j, :], None).then_inc(scattered[par], 16)

                pipeline(pool, TILES, [(3, scatter), (0, stage)])
                for s in range(2):
                    pool.wait_ge(scattered[s], 16 * TOP * (TILES // 2))

            @block.scalar
            def _(act):
                act.dma_start(rw[:, :, :], a["router_w"][0].rearrange("(k p) e -> p k e", p=P)).then_inc(small_loaded, 16)
                act.dma_start(rb[:, :], a["router_b"][0:1, :].to_broadcast([P, EXPERTS])).then_inc(small_loaded, 16)
                act.dma_start(g2[:, :], a["norm2_g"][0:1, :].to_broadcast([P, D])).then_inc(small_loaded, 16)
                act.dma_start(b_down[:, :], a["b_down"][0]).then_inc(small_loaded, 16)

                def square(t, par, m):
                    act.wait_ge(h2_ready, t + 1)
                    wait(act, ss_ready, t)
                    nc.scalar.activation(squares[:, :], h2[par][:, :], ACT.Square, accum_out=ss[par][:, :]) \
                      .then_inc(ss_ready, 1)
                    act.wait_ge(ss_ready, t + 1)
                    nc.scalar.activation(root[par][:, :], ss[par][:, :], ACT.Sqrt, scale=1.0 / D,
                                         bias=k.eps[:, 0:1]).then_inc(root_ready, 1)

                def copy_turned(t, par, m):
                    act.wait_ge(hn_turned, t + 1)
                    wait(act, router_ready, t)
                    nc.scalar.activation(hnT[:, :, :], tp_ps[:, :, :], ACT.Copy).then_inc(hnT_ready, 1)

                def exponentials(t, par, m):
                    act.wait_ge(best_ready, t + 1)
                    nc.scalar.activation(powers[par][:, :], best[par][:, 0:TOP], ACT.Exp, bias=neg_best[:, 0:1],
                                         accum_out=power_sum[par][:, :]).then_inc(powers_ready, 1)

                def copy_gates(t, par, m):
                    act.wait_ge(rank_ready, t + 1)
                    wait(act, bias_ready, t)
                    nc.scalar.activation(gateT[:, :], lg_ps[0:EXPERTS, P:2 * P], ACT.Copy).then_inc(gateT_ready, 1)

                pipeline(act, TILES, [(2, copy_gates), (1, copy_turned), (0, square), (1, exponentials)])

            @block.tensor
            def _(pe):
                pe.wait_ge(small_loaded, 64)
                pe.wait_ge(made_masks, 1)

                def project_out(t, par, half):
                    for kk in range(KD):
                        mm = nc.tensor.matmul(op_ps[:, half * 512:(half + 1) * 512], mixed[par][:, kk, :],
                                              w_out[:, kk, half * 512:(half + 1) * 512],
                                              start=kk == 0, stop=kk == KD - 1)
                    return mm

                def project_left(t, par, m):
                    pe.wait_ge(staged, 2 * t + 2)
                    wait(pe, h2_ready, t)
                    project_out(t, par, 0)

                def project_right(t, par, m):
                    project_out(t, par, 1).then_inc(proj_ready, 1)

                def turn(t, par, m):
                    pe.wait_ge(hn_ready, t + 1)
                    wait(pe, hnT_ready, t)
                    for kk in range(KD):
                        mm = nc.tensor.transpose(tp_ps[:, kk, :], hn[par][:, kk * P:(kk + 1) * P], k.ident[:, :])
                    mm.then_inc(hn_turned, 1)

                def router(t, par, m):
                    pe.wait_ge(hnT_ready, t + 1)
                    wait(pe, logits_taken, t)
                    wait(pe, gateT_ready, t)
                    for kk in range(KD):
                        mm = nc.tensor.matmul(lg_ps[:, 0:EXPERTS], hnT[:, kk, :], rw[:, kk, :],
                                              start=kk == 0, stop=kk == KD - 1)
                    mm.then_inc(router_ready, 1)

                def ranks(t, par, m):
                    pe.wait_ge(picked, 2 * t + 2)
                    wait(pe, rank_taken, t)
                    nc.tensor.matmul(rk_ps[:, 0:EXPERTS], before[:, :], chosen[par][:, :], start=True, stop=True)
                    nc.tensor.matmul(rk_ps[:, EXPERTS:2 * EXPERTS], ones[:, :], chosen[par][:, :],
                                     start=True, stop=True)
                    nc.tensor.transpose(lg_ps[0:EXPERTS, P:2 * P], gate[par][:, :], k.ident[:, :]) \
                      .then_inc(rank_ready, 1)

                def biases(t, par, m):
                    pe.wait_ge(gateT_ready, t + 1)
                    wait(pe, h2b_ready, t)
                    for half in range(2):
                        mm = nc.tensor.matmul(gb_ps[:, half * 512:(half + 1) * 512], gateT[:, :],
                                              b_down[:, half * 512:(half + 1) * 512], start=True, stop=True)
                    mm.then_inc(bias_ready, 1)

                pipeline(pe, TILES, [(0, project_left), (2, ranks), (1, turn), (2, biases), (0, project_right),
                                     (1, router)])

            @block.vector
            def _(dve):
                setup = Chain(dve, vec_setup)
                norm, choose, put = Chain(dve, chain0), Chain(dve, chain1), Chain(dve, chain2)
                CHOOSE, PUT = 7, 6
                dve.wait_ge(small_loaded, 64)
                dve.wait_ge(made, 4)
                nc.vector.tensor_copy(choice[:, :], choice_i[:, :])
                nc.vector.tensor_copy(col[:, :], col_i[:, :])
                nc.vector.tensor_copy(token[:, :], token_i[:, :])
                setup.after(nc.vector.memset(k.count[:, :], 0.0))

                def residual(t, par, m):
                    dve.wait_ge(proj_ready, t + 1)
                    dve.wait_ge(x_loaded[par], 16 * (m + 1))
                    wait(dve, h2b_ready, t - 1)
                    nc.vector.tensor_tensor(h2[par][:, :], op_ps[:, :], x_t[par][:, :], ALU.add).then_inc(h2_ready, 1)

                def norm_rows(t, par, m):
                    dve.wait_ge(root_ready, t + 1)
                    norm.begin(t)
                    norm.after(nc.vector.reciprocal(rstd[par][:, :], root[par][:, :]))
                    wait(dve, hn_stored[par], 16 * m)
                    nc.vector.scalar_tensor_tensor(out=hn[par][:, :], in0=h2[par][:, :], scalar=rstd[par][:, 0:1],
                                                   in1=g2[:, :], op0=ALU.mult, op1=ALU.mult).then_inc(hn_ready, 1)

                def pick_top(t, par, m):
                    choose.begin(t * CHOOSE)
                    dve.wait_ge(router_ready, t + 1)
                    nc.vector.tensor_tensor(logits[:, :], lg_ps[:, 0:EXPERTS], rb[:, :], ALU.add) \
                      .then_inc(logits_taken, 1)
                    dve.wait_ge(logits_taken, t + 1)
                    dve.sem_inc(max_begun, 1)
                    choose.after(nc.vector.max(best[par][:, :], logits[:, :]))
                    nc.vector.tensor_scalar(neg_best[:, :], best[par][:, 0:1], -1.0, None, ALU.mult) \
                      .then_inc(best_ready, 1)
                    choose.after(nc.vector.max_index(best_i[:, :], best[par][:, :], logits[:, :]))
                    choose.after(nc.vector.tensor_copy(pick[par][:, :], best_i[:, 0:TOP]))
                    choose.after(nc.vector.tensor_tensor(
                        mask[par][:, :, :], col[:, :].unsqueeze(1).to_broadcast([P, TOP, EXPERTS]),
                        pick[par][:, :].unsqueeze(2).to_broadcast([P, TOP, EXPERTS]), ALU.is_equal))
                    nc.vector.tensor_reduce(chosen[par][:, :], mask[par][:, :, :].rearrange("p j e -> p e j"),
                                            AX_X, ALU.add).then_inc(picked, 1)
                    assert choose.n == 4

                def weigh_top(t, par, m):
                    choose.begin(t * CHOOSE)
                    choose.n = 4
                    dve.wait_ge(powers_ready, t + 1)
                    choose.after(nc.vector.reciprocal(inverse[:, :], power_sum[par][:, :]))
                    choose.after(nc.vector.tensor_scalar(powers[par][:, :], powers[par][:, :], inverse[:, 0:1], None,
                                                         ALU.mult))
                    nc.vector.tensor_copy(k.gates[:, ds(t, 1), :].rearrange("p one j -> p (one j)"), powers[par][:, :])
                    choose.after(nc.vector.tensor_tensor(
                        weighted[:, :, :], mask[par][:, :, :],
                        powers[par][:, :].unsqueeze(2).to_broadcast([P, TOP, EXPERTS]), ALU.mult))
                    nc.vector.tensor_reduce(gate[par][:, :], weighted[:, :, :].rearrange("p j e -> p e j"),
                                            AX_X, ALU.add).then_inc(picked, 1)
                    assert choose.n == CHOOSE, choose.n

                def put_rows(t, par, m):
                    put.begin(t * PUT)
                    dve.wait_ge(rank_ready, t + 1)
                    put.after(nc.vector.tensor_tensor(rank_all[:, :], rk_ps[:, 0:EXPERTS], k.count[:, :], ALU.add))
                    nc.vector.tensor_tensor(k.count[:, :], rk_ps[:, EXPERTS:2 * EXPERTS], k.count[:, :], ALU.add) \
                      .then_inc(rank_taken, 1)
                    put.after(nc.vector.tensor_tensor(
                        rank_pick[:, :, :], mask[par][:, :, :],
                        rank_all[:, :].unsqueeze(1).to_broadcast([P, TOP, EXPERTS]), ALU.mult))
                    put.after(nc.vector.tensor_reduce(rank[:, :], rank_pick[:, :, :], AX_X, ALU.add))
                    put.after(nc.vector.scalar_tensor_tensor(out=place[:, :], in0=pick[par][:, :],
                                                             scalar=float(REGION), in1=rank[:, :],
                                                             op0=ALU.mult, op1=ALU.add))
                    wait(dve, scattered[par], 16 * TOP * m)
                    nc.vector.tensor_copy(place_i[par][:, :], place[:, :])
                    put.after(nc.vector.scalar_tensor_tensor(
                        out=row[:, :], in0=token[:, 0:1].to_broadcast([P, TOP]), scalar=float(TOP), in1=choice[:, :],
                        op0=ALU.mult, op1=ALU.add))
                    nc.vector.tensor_copy(tile_entry[par][:, :, 0], token[:, 0:1].to_broadcast([P, TOP]))
                    nc.vector.tensor_copy(tile_entry[par][:, :, 1], row[:, :]).then_inc(placed, 1)
                    dve.wait_ge(placed, t + 1)
                    put.after(nc.vector.tensor_scalar(token[:, :], token[:, :], float(P), None, ALU.add))
                    assert put.n == PUT

                def add_biases(t, par, m):
                    dve.wait_ge(bias_ready, t + 1)
                    wait(dve, h2b_stored[par], 16 * m)
                    nc.vector.tensor_tensor(h2b[par][:, :], gb_ps[:, :], h2[par][:, :], ALU.add) \
                      .then_inc(h2b_ready, 1)

                pipeline(dve, TILES, [(2, put_rows), (2, add_biases), (0, residual), (1, pick_top), (0, norm_rows),
                                      (1, weigh_top)])


def plan(k):
    nc = k.nc
    with ExitStack() as ctx:
        def sb(name, shape, dt=F32):
            return ctx.enter_context(nc.sbuf_tensor("plan_" + name, shape, dt))

        def sem(name):
            return ctx.enter_context(nc.semaphore("plan_" + name))

        T = TABLE
        row_i = sb("row_i", [T, 1], I32)
        col_i = sb("col_i", [T, EXPERTS], I32)
        col = sb("col", [T, EXPERTS])
        row = sb("row", [T, 1])
        ones = sb("ones", [T, EXPERTS])
        passes = sb("passes", [T, EXPERTS])
        upto = sb("upto", [T, EXPERTS])
        past = sb("past", [T, EXPERTS])
        past_passes = sb("past_passes", [T, EXPERTS])
        expert = sb("expert", [T, 1])
        used = sb("used", [T, 1])
        chunk = sb("chunk", [T, 1])
        entry = sb("entry", [T, 4])
        entry_i = sb("entry_i", [T, 4], I32)
        rows_made = sem("rows_made")
        vec_chain = sem("vec_chain")
        table_ready = sem("table_ready")
        table_stored = sem("table_stored")
        table_loaded = sem("table_loaded")
        with nc.Block() as block:
            @block.gpsimd
            def _(pool):
                pool.iota(row_i[:, :], pattern=[[0, 1]], base=0, channel_multiplier=1).then_inc(rows_made, 1)
                pool.memset(ones[:, :], 1.0).then_inc(rows_made, 1)
                pool.iota(col_i[:, :], pattern=[[1, EXPERTS]], base=0, channel_multiplier=0).then_inc(rows_made, 1)

            @block.vector
            def _(dve):
                chain = Chain(dve, vec_chain)
                count = k.count[0:T, :]
                dve.wait_ge(rows_made, 3)
                chain.after(nc.vector.tensor_copy(row[:, :], row_i[:, :]))
                chain.after(nc.vector.tensor_copy(col[:, :], col_i[:, :]))
                chain.after(nc.vector.tensor_scalar(passes[:, :], count, 0.0, None, ALU.is_gt))
                for j in range(1, -(-REGION // PASS)):
                    chain.after(nc.vector.scalar_tensor_tensor(out=passes[:, :], in0=count, scalar=float(j * PASS),
                                                               in1=passes[:, :], op0=ALU.is_gt, op1=ALU.add))
                chain.after(nc.vector.tensor_tensor_scan(upto[:, :], ones[:, :], passes[:, :], 0.0,
                                                         ALU.mult, ALU.add))
                chain.after(nc.vector.tensor_scalar(past[:, :], upto[:, :], row[:, 0:1], None, ALU.is_le))
                chain.after(nc.vector.tensor_reduce(expert[:, :], past[:, :], AX_X, ALU.add))
                chain.after(nc.vector.tensor_tensor(past_passes[:, :], past[:, :], passes[:, :], ALU.mult))
                chain.after(nc.vector.tensor_reduce(used[:, :], past_passes[:, :], AX_X, ALU.add))
                chain.after(nc.vector.tensor_scalar(entry[:, 0:1], expert[:, :], float(EXPERTS - 1), None, ALU.min))
                chain.after(nc.vector.tensor_tensor(chunk[:, :], row[:, :], used[:, :], ALU.subtract))
                chain.after(nc.vector.tensor_scalar(chunk[:, :], chunk[:, :], float(PASS), None, ALU.mult))
                chain.after(nc.vector.scalar_tensor_tensor(out=entry[:, 1:2], in0=entry[:, 0:1],
                                                           scalar=float(REGION), in1=chunk[:, :],
                                                           op0=ALU.mult, op1=ALU.add))
                chain.after(nc.vector.tensor_scalar(entry[:, 1:2], entry[:, 1:2], float(SLOTS - PASS), None, ALU.min))
                chain.after(nc.vector.tensor_copy(entry[:, 2:3], upto[:, EXPERTS - 1:EXPERTS]))
                chain.after(nc.vector.tensor_scalar(past[:, :], col[:, :], entry[:, 0:1], None, ALU.is_equal))
                chain.after(nc.vector.tensor_tensor(past[:, :], past[:, :], count, ALU.mult))
                chain.after(nc.vector.tensor_reduce(expert[:, :], past[:, :], AX_X, ALU.add))
                chain.after(nc.vector.tensor_tensor(entry[:, 3:4], expert[:, :], chunk[:, :], ALU.subtract))
                chain.after(nc.vector.tensor_scalar(entry[:, 3:4], entry[:, 3:4], 0.0, None, ALU.max))
                nc.vector.tensor_copy(entry_i[:, :], entry[:, :]).then_inc(table_ready, 1)

            @block.sync
            def _(sp):
                sp.wait_ge(table_ready, 1)
                sp.dma_start(k.table, entry_i[:, :]).then_inc(table_stored, 16)
                sp.wait_ge(table_stored, 16)
                sp.dma_start(k.tab[:, :], k.table.rearrange("r c -> (r c)").rearrange("(one n) -> one n", one=1)) \
                  .then_inc(table_loaded, 16)
                sp.wait_ge(table_loaded, 16)


def pass_count(k, eng):
    return eng.value_load(k.tab[0:1, 2:3], min_val=1, max_val=MAX_PASSES)


def pass_expert(k, eng, p):
    return eng.value_load(k.tab[0:1, ds(p * 4, 1)], min_val=0, max_val=EXPERTS - 1)


def pass_rows(k, eng, p):
    return eng.value_load(k.tab[0:1, ds(p * 4 + 3, 1)], min_val=0, max_val=SEQ)


def pass_slot(k, eng, p):
    return eng.value_load(k.tab[0:1, ds(p * 4 + 1, 1)], min_val=0, max_val=SLOTS - PASS)


def experts(k):
    nc, a = k.nc, k.a
    CHUNKS = 6
    BUFFERS = 3
    LEAD = 2
    HALF = 512
    F = FF // P
    with ExitStack() as ctx:
        def sb(name, shape, dt=F32):
            return ctx.enter_context(nc.sbuf_tensor("experts_" + name, shape, dt))

        def two(name, shape, dt=F32):
            return [sb(f"{name}{s}", shape, dt) for s in range(2)]

        def sem(name):
            return ctx.enter_context(nc.semaphore("experts_" + name))

        def sem2(name):
            return [sem(f"{name}{s}") for s in range(2)]

        raw = [sb(f"raw{s}", [P, KD // 2, HALF]) for s in range(3)]
        wh = [sb(f"wh{s}", [P, KD, HALF], F32R) for s in range(3)]
        wl = [sb(f"wl{s}", [P, KD, HALF], F32R) for s in range(3)]
        xs = sb("xs", [P, PT, D])
        xh = sb("xh", [P, KD, PASS], F32R)
        xl = sb("xl", [P, KD, PASS], F32R)
        ah = sb("ah", [P, F, PASS], F32R)
        al = sb("al", [P, F, PASS], F32R)
        index = sb("index", [P, PT, 2], I32)
        to_row = sb("to_row", [P, PT], I32)
        g_act = two("g_act", [P, PASS])
        u_act = two("u_act", [P, PASS])
        sg = two("sg", [P, PASS])
        gs = two("gs", [P, PASS])
        act_f = two("act_f", [P, PASS])
        y_rows = two("y_rows", [P, HALF])
        bias_rows = sb("bias_rows", [EXPERTS, 2 * FF // 4])
        bias_gu = sb("bias_gu", [P, 2 * F, EXPERTS])
        gu_ps = ctx.enter_context(nc.psum_tensor("experts_gu_ps", [P, 2, 2, 512], F32))
        dn_ps = ctx.enter_context(nc.psum_tensor("experts_dn_ps", [P, 2, 512], F32))
        xt_ps = ctx.enter_context(nc.psum_tensor("experts_xt_ps", [P, 2, 512], F32))

        bias_loaded = sem("bias_loaded")
        bias_turned = sem("bias_turned")
        bias_copied = sem("bias_copied")
        w_loaded = [sem(f"w_loaded{s}") for s in range(3)]
        high_ready = sem("high_ready")
        low_ready = sem("low_ready")
        index_loaded = sem("index_loaded")
        gather_begun = sem("gather_begun")
        gathered = sem("gathered")
        rows_kept = sem("rows_kept")
        x_turned = sem("x_turned")
        xh_ready = sem("xh_ready")
        xl_ready = sem("xl_ready")
        banks_cleared = sem("banks_cleared")
        gu_ready = sem("gu_ready")
        g_ready = sem("g_ready")
        gu_taken = sem("gu_taken")
        sg_ready = sem("sg_ready")
        gs_ready = sem("gs_ready")
        act_ready = sem("act_ready")
        ah_ready = sem("ah_ready")
        al_ready = sem("al_ready")
        dn_ready = sem("dn_ready")
        y_ready = sem("y_ready")
        y_stored = sem2("y_stored")
        y_free = sem("y_free")

        w_gu = a["w_gate_up"][0].rearrange("e (k p) f -> e p k f", p=P)
        w_dn = a["w_down"][0].rearrange("e (k p) f -> e p k f", p=P)

        with nc.Block() as block:
            @block.sync
            def _(sp):
                def load(e, c, part, j):
                    sp.wait_ge(low_ready, j + 1)
                    to = (2 * c + part) % 3
                    ks = slice(part * 4, part * 4 + 4)
                    if c < 4:
                        for side in range(2):
                            first = side * FF + c * 256
                            sp.dma_start(raw[to][:, :, side * 256:(side + 1) * 256],
                                         w_gu[ds(e, 1), :, ks, first:first + 256]
                                         .rearrange("one p k f -> p (one k) f")).then_inc(w_loaded[to], 16)
                    else:
                        for side in range(2):
                            k0 = part * 4 + side * 2
                            sp.dma_start(raw[to][:, side * 2:side * 2 + 2, :],
                                         w_dn[ds(e, 1), :, k0:k0 + 2, (c - 4) * HALF:(c - 3) * HALF]
                                         .rearrange("one p k f -> p (one k) f")).then_inc(w_loaded[to], 16)

                total = pass_count(k, sp)
                first = pass_expert(k, sp, 0)
                for c in range(LEAD):
                    for part in range(2):
                        load(first, c, part, 2 * c + part)
                with sp.Fori(0, total) as p:
                    e = pass_expert(k, sp, p)
                    for c in range(LEAD, CHUNKS):
                        for part in range(2):
                            load(e, c, part, p * (2 * CHUNKS) + (2 * c + part))
                    e_next = pass_expert(k, sp, p + 1)
                    for c in range(LEAD):
                        for part in range(2):
                            load(e_next, c, part, p * (2 * CHUNKS) + (2 * (CHUNKS + c) + part))

            @block.gpsimd
            def _(pool):
                def load_index(p):
                    slot = pass_slot(k, pool, p)
                    pool.dma_start(index[:, :, :], k.slot_list[ds(slot, PASS), :].rearrange("(t p) two -> p t two", p=P)) \
                        .then_inc(index_loaded, 16)

                def gather(t):
                    pool.sem_inc(gather_begun, 1)
                    pool.indirect_dma_start(xs[:, t, :], None, k.hn,
                                            bass.IndirectOffsetOnAxis(ap=index[:, t, 0:1], axis=0)) \
                        .then_inc(gathered, 16)

                total = pass_count(k, pool)
                load_index(0)
                pool.wait_ge(index_loaded, 16)
                for t in range(PT):
                    gather(t)
                with pool.Fori(0, total) as p:
                    for f in range(F):
                        pool.wait_ge(sg_ready, p * F + (f + 1))
                        pool.tensor_tensor(gs[f % 2][:, :], g_act[f % 2][:, :], sg[f % 2][:, :], ALU.mult) \
                            .then_inc(gs_ready, 1)
                        if f == 1:
                            pool.wait_ge(x_turned, p * (2 * PT) + 2 * PT)
                            pool.sem_inc(gather_begun, 1)
                            pool.tensor_copy(to_row[:, :], index[:, :, 1]).then_inc(rows_kept, 1)
                            pool.wait_ge(rows_kept, p + 1)
                            pool.sem_inc(gather_begun, 1)
                            load_index(p + 1)
                        elif 2 <= f < 2 + PT:
                            if f == 2:
                                pool.wait_ge(index_loaded, p * 16 + 32)
                            gather(f - 2)
                    for q in range(2 * PT):
                        half, t = q // PT, q % PT
                        pool.wait_ge(y_ready, p * (2 * PT) + (q + 3))
                        pool.sem_inc(gather_begun, 1)
                        pool.indirect_dma_start(k.y[half], bass.IndirectOffsetOnAxis(ap=to_row[:, t:t + 1], axis=0),
                                                y_rows[q % 2][:, :], None, bounds_check=ROWS - 1, oob_is_err=False) \
                            .then_inc(y_stored[q % 2], 16)
                        pool.wait_ge(y_stored[q % 2], (p * PT + (q // 2 + 1)) * 16)
                        pool.sem_inc(y_free, 1)
                pool.wait_ge(gathered, (total + 1) * (16 * PT))

            @block.scalar
            def _(act):
                def high(p, c, part):
                    if c >= BUFFERS:
                        act.wait_ge(gu_ready, p * F + 2 * (c - BUFFERS + 1))
                    elif not isinstance(p, int) and c == 0:
                        act.wait_ge(gu_ready, (p - 1) * F + F)
                    elif not isinstance(p, int) and c == 1:
                        act.wait_ge(dn_ready, (p - 1) * (2 * PT) + PT)
                    of = (2 * c + part) % 3
                    act.wait_ge(w_loaded[of], (p * (2 * CHUNKS // 3) + ((2 * c + part) // 3 + 1)) * 32)
                    nc.scalar.activation(wh[c % 3][:, part * 4:part * 4 + 4, :], raw[of][:, :, :], ACT.Copy) \
                      .then_inc(high_ready, 1)

                def x_high(p, q):
                    act.wait_ge(x_turned, p * (2 * PT) + (q + 1))
                    k0, t = q % 2 * 4, q // 2
                    nc.scalar.activation(xh[:, k0:k0 + 4, t * P:(t + 1) * P],
                                         xt_ps[:, q % 2, :].rearrange("p (k t) -> p k t", t=P), ACT.Copy) \
                      .then_inc(xh_ready, 1)

                BQ = 2 * FF // 4
                for q in range(4):
                    wait(act, bias_turned, q)
                    act.dma_start(bias_rows[:, :], a["b_gate_up"][0, :, q * BQ:(q + 1) * BQ]) \
                       .then_inc(bias_loaded, 16)
                act.sem_inc(y_ready, 2)
                act.sem_inc(y_free, 2)
                total = pass_count(k, act)
                for c in range(LEAD):
                    for part in range(2):
                        high(0, c, part)
                for q in range(2 * PT):
                    x_high(0, q)
                with act.Fori(0, total) as p:
                    def act_high(f):
                        act.wait_ge(act_ready, p * F + (f + 1))
                        nc.scalar.activation(ah[:, f, :], act_f[f % 2][:, :], ACT.Copy).then_inc(ah_ready, 1)

                    for f in range(F):
                        act.wait_ge(g_ready, p * F + (f + 1))
                        nc.scalar.activation(sg[f % 2][:, :], g_act[f % 2][:, :], ACT.Sigmoid, scale=ALPHA) \
                          .then_inc(sg_ready, 1)
                        if f >= 1:
                            act_high(f - 1)
                        if f < F - 1:
                            high(p, LEAD + f // 2, f % 2)
                    act_high(F - 1)
                    x_high(p + 1, 0)
                    x_high(p + 1, 1)
                    high(p, CHUNKS - 1, 1)
                    for q in range(2 * PT):
                        act.wait_ge(dn_ready, p * (2 * PT) + (q + 1))
                        act.wait_ge(y_free, p * (2 * PT) + (q + 1))
                        nc.scalar.activation(y_rows[q % 2][:, :], dn_ps[:, q % 2, :], ACT.Copy).then_inc(y_ready, 1)
                        if q + 2 < 2 * PT:
                            x_high(p + 1, q + 2)
                        if q < 2 * LEAD:
                            high(p + 1, q // 2, q % 2)

            @block.tensor
            def _(pe):
                total = pass_count(k, pe)
                for q in range(4):
                    pe.wait_ge(bias_loaded, 16 * (q + 1))
                    wait(pe, bias_copied, q)
                    for i in range(4):
                        mm = nc.tensor.transpose(xt_ps[:, 0, i * EXPERTS:(i + 1) * EXPERTS],
                                                 bias_rows[:, i * P:(i + 1) * P], k.ident[0:EXPERTS, 0:EXPERTS])
                    mm.then_inc(bias_turned, 1)
                pe.wait_ge(bias_copied, 4)

                def turn(p, q):
                    k0, t = q % 2 * 4, q // 2
                    pe.wait_ge(gathered, (p + 1) * (16 * PT))
                    pe.wait_ge(xl_ready, p * (2 * PT) + (q + 1))
                    for i in range(4):
                        mm = nc.tensor.transpose(xt_ps[:, q % 2, i * P:(i + 1) * P],
                                                 xs[:, t, (k0 + i) * P:(k0 + i + 1) * P], k.ident[:, :])
                    mm.then_inc(x_turned, 1)

                for q in range(2 * PT):
                    turn(0, q)
                def gate_up(p, width):
                    for c in range(4):
                        h, lo = wh[c % 3], wl[c % 3]
                        pe.wait_ge(low_ready, p * (2 * CHUNKS) + (2 * c + 2 + 3))
                        for f2 in range(2):
                            f = 2 * c + f2
                            pe.wait_ge(gu_taken, p * F + (f + 1))
                            for part in range(2):
                                at = slice(part * 256 + f2 * P, part * 256 + (f2 + 1) * P)
                                o = gu_ps[:, f2, part, 0:width]
                                for kk in range(KD):
                                    nc.tensor.matmul(o, h[:, kk, at], xh[:, kk, 0:width], start=kk == 0, stop=False)
                                    nc.tensor.matmul(o, h[:, kk, at], xl[:, kk, 0:width], start=False, stop=False)
                                    mm = nc.tensor.matmul(o, lo[:, kk, at], xh[:, kk, 0:width], start=False,
                                                          stop=kk == KD - 1)
                            mm.then_inc(gu_ready, 1)

                def by_width(p, rows, widths):
                    if len(widths) == 1:
                        gate_up(p, widths[0])
                        return
                    mid = len(widths) // 2
                    with pe.If(rows > widths[mid - 1]):
                        by_width(p, rows, widths[mid:])
                    with pe.Else():
                        by_width(p, rows, widths[:mid])

                def down(p, q, wait_rows):
                    half, t = q // PT, q % PT
                    h, lo = wh[(4 + half) % 3], wl[(4 + half) % 3]
                    o = dn_ps[:, q % 2, :]
                    for f in range(F):
                        if wait_rows:
                            pe.wait_ge(al_ready, p * F + (f + 1))
                        at = slice(t * P, (t + 1) * P)
                        nc.tensor.matmul(o, ah[:, f, at], h[:, f, :], start=f == 0, stop=False)
                        nc.tensor.matmul(o, ah[:, f, at], lo[:, f, :], start=False, stop=False)
                        mm = nc.tensor.matmul(o, al[:, f, at], h[:, f, :], start=False, stop=f == F - 1)
                    mm.then_inc(dn_ready, 1)

                pe.wait_ge(banks_cleared, 2)
                with pe.Fori(0, total) as p:
                    rows = pass_rows(k, pe, p)
                    pe.wait_ge(xl_ready, p * (2 * PT) + (2 * PT + 2))
                    by_width(p, rows, WIDTHS)
                    turn(p + 1, 0)
                    for q in range(2 * PT):
                        half, t = q // PT, q % PT
                        if q + 1 < 2 * PT:
                            turn(p + 1, q + 1)
                        if t == 0:
                            pe.wait_ge(low_ready, p * (2 * CHUNKS) + (2 * (4 + half) + 2 + 3))
                        pe.wait_ge(y_ready, p * (2 * PT) + (q + 1))
                        if t == 0:
                            down(p, q, q == 0)
                        else:
                            with pe.If(rows > t * P):
                                down(p, q, False)
                            with pe.Else():
                                nc.tensor.matmul(dn_ps[:, q % 2, 0:P], ah[:, 0, t * P:(t + 1) * P],
                                                 wh[(4 + half) % 3][:, 0, 0:P], start=True, stop=True) \
                                  .then_inc(dn_ready, 1)

            @block.vector
            def _(dve):
                def low(p, c, part):
                    dve.wait_ge(high_ready, p * (2 * CHUNKS) + (2 * c + part + 1))
                    ks = slice(part * 4, part * 4 + 4)
                    nc.vector.tensor_tensor(wl[c % 3][:, ks, :], raw[(2 * c + part) % 3][:, :, :],
                                            wh[c % 3][:, ks, :].bitcast(F32), ALU.subtract) \
                      .then_inc(low_ready, 1)

                def x_low(p, q):
                    dve.wait_ge(xh_ready, p * (2 * PT) + (q + 1))
                    k0, t = q % 2 * 4, q // 2
                    at = slice(t * P, (t + 1) * P)
                    nc.vector.tensor_tensor(xl[:, k0:k0 + 4, at],
                                            xt_ps[:, q % 2, :].rearrange("p (k t) -> p k t", t=P),
                                            xh[:, k0:k0 + 4, at].bitcast(F32), ALU.subtract).then_inc(xl_ready, 1)

                dve.sem_inc(low_ready, 3)
                dve.sem_inc(xl_ready, 2)
                dve.sem_inc(gu_taken, 2)
                total = pass_count(k, dve)
                for q in range(4):
                    dve.wait_ge(bias_turned, q + 1)
                    nc.vector.tensor_scalar(bias_gu[:, 4 * q:4 * q + 4, :],
                                            xt_ps[:, 0, 0:4 * EXPERTS].rearrange("p (c e) -> p c e", e=EXPERTS),
                                            1.0 if q >= 2 else 0.0, None, ALU.add).then_inc(bias_copied, 1)
                dve.wait_ge(bias_copied, 4)
                nc.vector.memset(gu_ps[:, :, :, :], 0.0).then_inc(banks_cleared, 1)
                nc.vector.memset(dn_ps[:, :, :], 0.0).then_inc(banks_cleared, 1)
                for c in range(LEAD):
                    for part in range(2):
                        low(0, c, part)
                for q in range(2 * PT):
                    x_low(0, q)
                with dve.Fori(0, total) as p:
                    e = pass_expert(k, dve, p)

                    def take(f):
                        dve.wait_ge(gu_ready, p * F + (f + 1))
                        nc.vector.tensor_scalar(g_act[f % 2][:, :], gu_ps[:, f % 2, 0, 0:PASS],
                                                bias_gu[:, f, ds(e, 1)], LIMIT, ALU.add, ALU.min) \
                          .then_inc(g_ready, 1)
                        nc.vector.tensor_scalar(u_act[f % 2][:, :], gu_ps[:, f % 2, 1, 0:PASS],
                                                bias_gu[:, F + f, ds(e, 1)], LIMIT + 1.0, ALU.add, ALU.min) \
                          .then_inc(gu_taken, 1)

                    def act_mul(f):
                        dve.wait_ge(gu_taken, p * F + (f + 3))
                        dve.wait_ge(gs_ready, p * F + (f + 1))
                        nc.vector.scalar_tensor_tensor(out=act_f[f % 2][:, :], in0=u_act[f % 2][:, :],
                                                       scalar=1.0 - LIMIT, in1=gs[f % 2][:, :],
                                                       op0=ALU.max, op1=ALU.mult).then_inc(act_ready, 1)

                    def act_low(f):
                        dve.wait_ge(ah_ready, p * F + (f + 1))
                        nc.vector.tensor_tensor(al[:, f, :], act_f[f % 2][:, :], ah[:, f, :].bitcast(F32),
                                                ALU.subtract).then_inc(al_ready, 1)

                    for f in range(F):
                        take(f)
                        if f >= 1:
                            act_mul(f - 1)
                            if f < F - 1:
                                low(p, LEAD + (f - 1) // 2, (f - 1) % 2)
                            act_low(f - 1)
                    act_mul(F - 1)
                    act_low(F - 1)
                    x_low(p + 1, 0)
                    x_low(p + 1, 1)
                    low(p, CHUNKS - 1, 0)
                    low(p, CHUNKS - 1, 1)
                    for q in range(2 * PT):
                        if q + 2 < 2 * PT:
                            x_low(p + 1, q + 2)
                        if q < 2 * LEAD:
                            low(p + 1, q // 2, q % 2)


def combine(k):
    nc = k.nc
    out = k.out[0]
    with ExitStack() as ctx:
        def two(name, shape, dt=F32):
            return [ctx.enter_context(nc.sbuf_tensor(f"combine_{name}{s}", shape, dt)) for s in range(2)]

        def sem(name):
            return ctx.enter_context(nc.semaphore("combine_" + name))

        def sem2(name):
            return [sem(f"{name}{s}") for s in range(2)]

        HALF = D // 2
        h2 = two("h2", [P, D])
        rows = two("rows", [P, 2, TOP, HALF])
        h2_loaded = sem2("h2_loaded")
        rows_loaded = sem2("rows_loaded")
        summed = sem("summed")
        out_stored = sem2("out_stored")
        vec_chain = sem("vec_chain")

        with nc.Block() as block:
            @block.sync
            def _(sp):
                def load(t, par, m):
                    wait(sp, summed, 2 * (t - 1))
                    for half in range(2):
                        sp.dma_start(rows[par][:, half, :, :].rearrange("p j c -> p (j c)"),
                                     k.y[half][ds(t * (P * TOP), P * TOP), :].rearrange("(p j) c -> p (j c)", j=TOP)) \
                          .then_inc(rows_loaded[par], 16)

                pipeline(sp, TILES, [(0, load)])

            @block.scalar
            def _(act):
                def load(t, par, m):
                    wait(act, out_stored[par], 16 * m)
                    act.dma_start(h2[par][:, :], k.h2[ds(t * P, P), :]).then_inc(h2_loaded[par], 16)

                def store(t, par, m):
                    act.wait_ge(summed, 2 * t + 2)
                    act.dma_start(out[ds(t * P, P), :], h2[par][:, :]).then_inc(out_stored[par], 16)

                pipeline(act, TILES, [(0, load), (1, store)])
                for s in range(2):
                    act.wait_ge(out_stored[s], 16 * (TILES // 2))

            @block.vector
            def _(dve):
                chain = Chain(dve, vec_chain)

                def add(t, par, m):
                    chain.begin(t * (TOP - 1))
                    dve.wait_ge(h2_loaded[par], 16 * (m + 1))
                    dve.wait_ge(rows_loaded[par], 32 * (m + 1))
                    for j in range(TOP):
                        for half in range(2):
                            cols = slice(half * HALF, (half + 1) * HALF)
                            ins = nc.vector.scalar_tensor_tensor(
                                out=h2[par][:, cols], in0=rows[par][:, half, j, :],
                                scalar=k.gates[:, ds(t, 1), j:j + 1].rearrange("p one j -> p (one j)"),
                                in1=h2[par][:, cols], op0=ALU.mult, op1=ALU.add)
                            if j == TOP - 1:
                                ins.then_inc(summed, 1)
                        if j < TOP - 1:
                            chain.after(ins)

                pipeline(dve, TILES, [(0, add)])


NAMES = ["x", "meta_tokens", "norm1_g", "w_in", "q_norm_g", "k_norm_g", "attn_sink", "dw_w", "dw_b", "conv_ln_g",
         "conv_ln_b", "w_out", "norm2_g", "router_w", "router_b", "w_gate_up", "b_gate_up", "w_down", "b_down"]


def lay_out(inputs):
    import numpy as np

    arrays = {name: np.asarray(inputs[name]) for name in NAMES}
    for name in ("norm1_g", "dw_b", "conv_ln_g", "conv_ln_b"):
        arrays[name] = arrays[name][0].reshape(-1, P).T
    for name in ("q_norm_g", "k_norm_g"):
        arrays[name] = arrays[name][0].reshape(HEAD, 1)
    arrays["dw_w"] = arrays["dw_w"][0, :, 0, :].T
    return {"in_" + name: np.ascontiguousarray(v) for name, v in arrays.items()}


def kernel(**inputs):
    import concourse.bacc as bacc
    from concourse.bass_utils import run_bass_kernel_spmd

    nc = bacc.Bacc("TRN2", target_bir_lowering=False, num_devices=1)
    arrays = lay_out(inputs)
    aps = {name[3:]: nc.dram_tensor(name, a.shape, mybir.dt.from_np(a.dtype), kind="ExternalInput").ap()
           for name, a in arrays.items()}
    out = nc.dram_tensor("out", (1, SEQ, D), F32, kind="ExternalOutput").ap()
    build(nc, aps, out)
    result = run_bass_kernel_spmd(nc, [arrays], core_ids=[0])
    return result.results[0]["out"]
```
